# Optimizing a Trainium2 kernel written in Bass

```python
import math
import jax, jax.numpy as jnp
from jax import lax
import numpy as np

D_MODEL = 1024
BATCH = 1
SEQ = 512
DEPTH = 1

DA_HEADS = 4
DA_HEAD_DIM = 128
DA_V_DIM = 2 * DA_HEAD_DIM
DA_COLS = DA_HEADS * DA_V_DIM
MLA_HEADS = 8
MLA_NOPE_DIM = 128
MLA_ROPE_DIM = 64
MLA_QK_DIM = MLA_NOPE_DIM + MLA_ROPE_DIM
MLA_V_DIM = 128
MLA_Q_RANK = 384
MLA_KV_RANK = 256
MLA_COLS = MLA_HEADS * MLA_V_DIM
ROPE_THETA = 10000.0
REL_BUCKETS = 32
REL_MAX_DISTANCE = 128
PEER_HEADS = 8
PEER_N_KEYS = 128
PEER_N_EXPERTS = PEER_N_KEYS * PEER_N_KEYS
PEER_KEY_DIM = 256
PEER_HALF = PEER_KEY_DIM // 2
PEER_TOPK = 16
N_BRANCHES = 2
Q_BLOCK = 128
TOKEN_BLOCK = 128
EPS = 1e-6

DA_Q_COLS = DA_HEADS * 2 * DA_HEAD_DIM
DA_K_COLS = DA_HEADS * 2 * DA_HEAD_DIM
DA_V_COLS = DA_HEADS * DA_V_DIM
GATE_COLS = N_BRANCHES * D_MODEL
IN_SPLITS = (DA_Q_COLS, DA_K_COLS, DA_V_COLS, MLA_Q_RANK, MLA_KV_RANK, MLA_ROPE_DIM, GATE_COLS)
IN_COLS = DA_Q_COLS + DA_K_COLS + DA_V_COLS + MLA_Q_RANK + MLA_KV_RANK + MLA_ROPE_DIM + GATE_COLS

kernel_name = 'hybrid_diffattn_mla_peer_block'

def rms_norm(x, g):
    xf = x.astype(jnp.float32)
    y = xf * lax.rsqrt(jnp.mean(xf * xf, axis=-1, keepdims=True) + EPS)
    return (y * g.astype(jnp.float32)).astype(x.dtype)

def split_cols(t, sizes):
    out, off = [], 0
    for n in sizes:
        out.append(t[..., off:off + n])
        off += n
    return out

def apply_rope(x, cos, sin):
    half = x.shape[-1] // 2
    x1, x2 = x[..., :half], x[..., half:]
    return jnp.concatenate([x1 * cos - x2 * sin, x1 * sin + x2 * cos], axis=-1).astype(x.dtype)

def lambda_init_fn(layer_idx):
    return 0.8 - 0.6 * math.exp(-0.3 * layer_idx)

def t5_bucket(dist):
    n = jnp.maximum(dist, 0)
    max_exact = REL_BUCKETS // 2
    nf = jnp.maximum(n, max_exact).astype(jnp.float32)
    large = max_exact + (jnp.log(nf / max_exact) / math.log(REL_MAX_DISTANCE / max_exact)
                         * (REL_BUCKETS - max_exact)).astype(jnp.int32)
    large = jnp.minimum(large, REL_BUCKETS - 1)
    return jnp.where(n < max_exact, n, large)

def diff_attention(q, k, v, rel_bias, lam):
    seq = q.shape[3]
    scale = DA_HEAD_DIM ** -0.5
    kpos = jnp.arange(seq)

    def block(i):
        start = i * Q_BLOCK
        qb = lax.dynamic_slice_in_dim(q, start, Q_BLOCK, axis=3)
        qpos = start + jnp.arange(Q_BLOCK)
        dist = qpos[:, None] - kpos[None, :]
        bias = jnp.take(rel_bias, t5_bucket(dist), axis=0)
        logits = jnp.einsum('bhmqd,bhmkd->bhmqk', qb, k).astype(jnp.float32) * scale
        logits = logits + jnp.transpose(bias, (2, 0, 1)).astype(jnp.float32)[None, :, None]
        logits = jnp.where(dist >= 0, logits, -jnp.inf)
        p = jax.nn.softmax(logits, axis=-1)
        w = p[:, :, 0] - lam * p[:, :, 1]
        return jnp.einsum('bhqk,bhkd->bhqd', w.astype(v.dtype), v)

    out = lax.map(block, jnp.arange(seq // Q_BLOCK))
    nblk, b, h, qn, dv = out.shape
    return jnp.transpose(out, (1, 0, 3, 2, 4)).reshape(b, seq, h, dv)

def causal_attention(q, k, v):
    seq = q.shape[2]
    scale = q.shape[-1] ** -0.5
    kpos = jnp.arange(seq)

    def block(i):
        start = i * Q_BLOCK
        qb = lax.dynamic_slice_in_dim(q, start, Q_BLOCK, axis=2)
        qpos = start + jnp.arange(Q_BLOCK)
        logits = jnp.einsum('bhqd,bhkd->bhqk', qb, k).astype(jnp.float32) * scale
        logits = jnp.where(kpos[None, :] <= qpos[:, None], logits, -jnp.inf)
        p = jax.nn.softmax(logits, axis=-1)
        return jnp.einsum('bhqk,bhkd->bhqd', p.astype(v.dtype), v)

    out = lax.map(block, jnp.arange(seq // Q_BLOCK))
    nblk, b, h, qn, dv = out.shape
    return jnp.transpose(out, (1, 0, 3, 2, 4)).reshape(b, seq, h * dv)

def peer(h, w_query, sub_keys, u_table, v_table):
    b, s, d = h.shape
    q = jnp.einsum('bsd,dp->bsp', h, w_query).reshape(b, s, PEER_HEADS, 2, PEER_HALF)
    scores = jnp.einsum('bshcp,hcnp->bshcn', q, sub_keys).astype(jnp.float32)
    s1, i1 = lax.top_k(scores[..., 0, :], PEER_TOPK)
    s2, i2 = lax.top_k(scores[..., 1, :], PEER_TOPK)
    cand = (s1[..., :, None] + s2[..., None, :]).reshape(b, s, PEER_HEADS, PEER_TOPK * PEER_TOPK)
    cidx = (i1[..., :, None] * PEER_N_KEYS + i2[..., None, :]).reshape(b, s, PEER_HEADS, PEER_TOPK * PEER_TOPK)
    top, pos = lax.top_k(cand, PEER_TOPK)
    eidx = jnp.take_along_axis(cidx, pos, axis=-1)
    gate = jax.nn.softmax(top, axis=-1).astype(h.dtype)
    nblk = s // TOKEN_BLOCK

    def to_blocks(t):
        return jnp.moveaxis(t.reshape((b, nblk, TOKEN_BLOCK) + t.shape[2:]), 1, 0)

    def block(args):
        hb, ib, gb = args
        u = jnp.take(u_table, ib, axis=0)
        a = jax.nn.gelu(jnp.einsum('btd,bthkd->bthk', hb, u), approximate=False)
        vsel = jnp.take(v_table, ib, axis=0)
        return jnp.einsum('bthk,bthkd->btd', gb * a, vsel)

    out = lax.map(block, (to_blocks(h), to_blocks(eidx), to_blocks(gate)))
    return jnp.moveaxis(out, 0, 1).reshape(b, s, d)

def setup_inputs(seed: int = 0) -> dict:
    key = jax.random.key(seed)
    ks = jax.random.split(key, 26)

    def nrm(k, shape, scale):
        return jax.random.normal(k, shape, jnp.float32) * scale

    def gain(k, shape):
        return 1.0 + 0.02 * jax.random.normal(k, shape, jnp.float32)

    return {
        'x': nrm(ks[0], (BATCH, SEQ, D_MODEL), 1.0),
        'w_in': nrm(ks[1], (DEPTH, D_MODEL, IN_COLS), D_MODEL ** -0.5),
        'attn_norm': gain(ks[2], (DEPTH, D_MODEL)),
        'da_q_norm': gain(ks[3], (DEPTH, DA_HEAD_DIM)),
        'da_k_norm': gain(ks[4], (DEPTH, DA_HEAD_DIM)),
        'da_lambda_q1': nrm(ks[5], (DEPTH, DA_HEAD_DIM), 0.1),
        'da_lambda_k1': nrm(ks[6], (DEPTH, DA_HEAD_DIM), 0.1),
        'da_lambda_q2': nrm(ks[7], (DEPTH, DA_HEAD_DIM), 0.1),
        'da_lambda_k2': nrm(ks[8], (DEPTH, DA_HEAD_DIM), 0.1),
        'da_out_norm': gain(ks[9], (DEPTH, DA_V_DIM)),
        'da_proj': nrm(ks[10], (DEPTH, DA_COLS, D_MODEL), DA_COLS ** -0.5),
        'mla_q_latent_norm': gain(ks[11], (DEPTH, MLA_Q_RANK)),
        'mla_w_uq': nrm(ks[12], (DEPTH, MLA_Q_RANK, MLA_HEADS * MLA_QK_DIM), MLA_Q_RANK ** -0.5),
        'mla_kv_latent_norm': gain(ks[13], (DEPTH, MLA_KV_RANK)),
        'mla_w_ukv': nrm(ks[14], (DEPTH, MLA_KV_RANK, MLA_HEADS * (MLA_NOPE_DIM + MLA_V_DIM)), MLA_KV_RANK ** -0.5),
        'mla_q_norm': gain(ks[15], (DEPTH, MLA_QK_DIM)),
        'mla_k_norm': gain(ks[16], (DEPTH, MLA_QK_DIM)),
        'mla_proj': nrm(ks[17], (DEPTH, MLA_COLS, D_MODEL), MLA_COLS ** -0.5),
        'w_out': nrm(ks[18], (DEPTH, D_MODEL, D_MODEL), D_MODEL ** -0.5),
        'rel_bias': nrm(ks[19], (REL_BUCKETS, DA_HEADS), 0.5),
        'ffn_norm': gain(ks[20], (DEPTH, D_MODEL)),
        'peer_w_query': nrm(ks[21], (DEPTH, D_MODEL, PEER_HEADS * PEER_KEY_DIM), D_MODEL ** -0.5),
        'peer_sub_keys': nrm(ks[22], (DEPTH, PEER_HEADS, 2, PEER_N_KEYS, PEER_HALF), PEER_HALF ** -0.5),
        'peer_u': nrm(ks[23], (DEPTH, PEER_N_EXPERTS, D_MODEL), D_MODEL ** -0.5),
        'peer_v': nrm(ks[24], (DEPTH, PEER_N_EXPERTS, D_MODEL), 0.5),
    }

def reference(x, w_in, attn_norm, da_q_norm, da_k_norm, da_lambda_q1, da_lambda_k1, da_lambda_q2,
              da_lambda_k2, da_out_norm, da_proj, mla_q_latent_norm, mla_w_uq, mla_kv_latent_norm,
              mla_w_ukv, mla_q_norm, mla_k_norm, mla_proj, w_out, rel_bias, ffn_norm, peer_w_query,
              peer_sub_keys, peer_u, peer_v):
    b, s, _ = x.shape
    pos = jnp.arange(s, dtype=jnp.float32)
    inv_freq = ROPE_THETA ** (-jnp.arange(0, MLA_ROPE_DIM, 2, dtype=jnp.float32) / MLA_ROPE_DIM)
    ang = pos[:, None] * inv_freq[None, :]
    cos, sin = jnp.cos(ang), jnp.sin(ang)

    for l in range(DEPTH):
        h = rms_norm(x, attn_norm[l])
        proj = jnp.einsum('bsd,dc->bsc', h, w_in[l])
        qa, ka, va, cq, ckv, kr, gates = split_cols(proj, IN_SPLITS)

        qa = rms_norm(qa.reshape(b, s, DA_HEADS, 2, DA_HEAD_DIM), da_q_norm[l])
        ka = rms_norm(ka.reshape(b, s, DA_HEADS, 2, DA_HEAD_DIM), da_k_norm[l])
        qa = jnp.transpose(qa, (0, 2, 3, 1, 4))
        ka = jnp.transpose(ka, (0, 2, 3, 1, 4))
        va = jnp.transpose(va.reshape(b, s, DA_HEADS, DA_V_DIM), (0, 2, 1, 3))
        lam_init = lambda_init_fn(l)
        lam = (jnp.exp(jnp.sum(da_lambda_q1[l].astype(jnp.float32) * da_lambda_k1[l].astype(jnp.float32)))
               - jnp.exp(jnp.sum(da_lambda_q2[l].astype(jnp.float32) * da_lambda_k2[l].astype(jnp.float32)))
               + lam_init)
        ya = diff_attention(qa, ka, va, rel_bias, lam)
        ya = rms_norm(ya, da_out_norm[l]) * (1.0 - lam_init)
        ya = jnp.einsum('bsc,cd->bsd', ya.reshape(b, s, DA_COLS), da_proj[l])

        cq = rms_norm(cq, mla_q_latent_norm[l])
        qb = jnp.einsum('bsr,rc->bsc', cq, mla_w_uq[l]).reshape(b, s, MLA_HEADS, MLA_QK_DIM)
        q_nope, q_rope = qb[..., :MLA_NOPE_DIM], qb[..., MLA_NOPE_DIM:]
        q_rope = apply_rope(q_rope, cos[:, None, :], sin[:, None, :])
        ckv = rms_norm(ckv, mla_kv_latent_norm[l])
        kv = jnp.einsum('bsr,rc->bsc', ckv, mla_w_ukv[l]).reshape(b, s, MLA_HEADS, MLA_NOPE_DIM + MLA_V_DIM)
        k_nope, vb = kv[..., :MLA_NOPE_DIM], kv[..., MLA_NOPE_DIM:]
        k_rope = apply_rope(kr, cos, sin)
        k_rope = jnp.broadcast_to(k_rope[:, :, None, :], (b, s, MLA_HEADS, MLA_ROPE_DIM))
        qb = rms_norm(jnp.concatenate([q_nope, q_rope], axis=-1), mla_q_norm[l])
        kb = rms_norm(jnp.concatenate([k_nope, k_rope], axis=-1), mla_k_norm[l])
        yb = causal_attention(jnp.transpose(qb, (0, 2, 1, 3)), jnp.transpose(kb, (0, 2, 1, 3)),
                              jnp.transpose(vb, (0, 2, 1, 3)))
        yb = jnp.einsum('bsc,cd->bsd', yb, mla_proj[l])

        g = jax.nn.sigmoid(gates.reshape(b, s, N_BRANCHES, D_MODEL))
        merged = g[:, :, 0] * ya + g[:, :, 1] * yb
        x = x + jnp.einsum('bsd,de->bse', merged, w_out[l])

        h2 = rms_norm(x, ffn_norm[l])
        x = x + peer(h2, peer_w_query[l], peer_sub_keys[l], peer_u[l], peer_v[l])
    return x


_drawn_inputs = setup_inputs


def setup_inputs(seed=0):
    import zlib

    import numpy as np

    out = dict(_drawn_inputs(seed))
    spreads = {}
    factors = {'mla_q_latent_norm': 6.667,
     'mla_kv_latent_norm': 5.386,
     'mla_q_norm': 6.171,
     'mla_k_norm': 5.992,
     'da_q_norm': 8.0,
     'da_k_norm': 8.0,
     'da_lambda_q1': 3.56,
     'da_lambda_k2': 7.659,
     'da_out_norm': 8.0,
     'ffn_norm': 4.653}
    for name, (base, spread) in spreads.items():
        noise = np.random.default_rng([zlib.crc32(name.encode()), seed]).standard_normal(out[name].shape)
        drawn = base * np.exp(spread * noise) if base else spread * noise
        out[name] = __import__('jax').numpy.asarray(drawn.astype(out[name].dtype))
    for name, factor in factors.items():
        out[name] = (out[name] * factor).astype(out[name].dtype)
    return out
```

```python
from contextlib import ExitStack

import concourse.bass as bass
from concourse import mybir

F32 = mybir.dt.float32
F32R = mybir.dt.float32r
U32 = mybir.dt.uint32
ALU = mybir.AluOpType
ACT = mybir.ActivationFunctionType
AX_X = mybir.AxisListType.X

P = 128
D = 1024
DC = D // P
T = 512
TB = T // P
EPS = 1e-6
NEG = -1e30

DA_HEADS, DA_DIM, DA_V = 4, 128, 256
MLA_HEADS, NOPE, ROPE, MLA_V = 8, 128, 64, 128
Q_RANK, KV_RANK = 384, 256
LAM_INIT = 0.8 - 0.6
KEYS, TOPK, PEER_HEADS = 128, 16, 8
HK = PEER_HEADS * TOPK

QA, KA, VA, CQ, CKV, KR, GATES, IN_TILES = 0, 8, 16, 24, 27, 29, 30, 46
G_ATTN, G_FFN, G_DAQ, G_DAK, G_DAOUT, G_QLAT, G_KVLAT, G_MQN, G_MQR, G_MKN, G_MKR, G_LAM, G_COLS = (
    0, 8, 16, 17, 18, 20, 23, 25, 26, 27, 28, 29, 33)
BIAS_LEN = 640
PASSES = ((0, 0), (0, 1), (1, 0))


class Scope:

    def __init__(self, nc, name):
        self.nc, self.name, self.stack = nc, name, ExitStack()

    def __enter__(self):
        return self

    def __exit__(self, *e):
        return self.stack.__exit__(*e)

    def sb(self, name, shape, dt=F32):
        return self.stack.enter_context(self.nc.sbuf_tensor(f"{self.name}_{name}", shape, dt))

    def ps(self, name, shape):
        return self.stack.enter_context(self.nc.psum_tensor(f"{self.name}_{name}", shape, F32))

    def sem(self, name):
        return self.stack.enter_context(self.nc.semaphore(f"{self.name}_{name}"))


class Chain:

    def __init__(self, eng, sem):
        self.eng, self.sem, self.n = eng, sem, 0

    def __call__(self, ins):
        self.n += 1
        ins.then_inc(self.sem, 1)
        self.eng.wait_ge(self.sem, self.n)


def project(nc, name, weights, chunks, tiles, act, c0, dest, d0):
    with Scope(nc, name) as s:
        raw = s.sb("raw", [P, 2, chunks * P])
        half = [[s.sb(f"half{b}{h}", [P, chunks * P], F32R) for h in range(2)] for b in range(2)]
        acc = [s.ps(f"acc{b}", [P, T]) for b in range(2)]
        raw_in = [s.sem(f"raw_in{b}") for b in range(2)]
        hi_done, lo_done, mm_done, out_done, opened = (
            s.sem("hi_done"), s.sem("lo_done"), s.sem("mm_done"), s.sem("out_done"), s.sem("opened"))

        with nc.Block() as block:
            @block.sync
            def _(sp):
                with sp.Fori(0, tiles // 2) as i:
                    for b in range(2):
                        n = sp.snap(2 * i + b)
                        sp.wait_ge(lo_done, n + 1)
                        sp.wait_ge(opened, 1)
                        sp.dma_start(raw[:, b, :], weights[bass.ds(n, 1)].rearrange("o p f -> p (o f)")
                                     ).then_inc(raw_in[b], 16)

            @block.vector
            def _(dve):
                dve.sem_inc(mm_done, 2)
                with dve.Fori(0, tiles // 2) as i:
                    for b in range(2):
                        dve.wait_ge(raw_in[b], 16 * i + 16)
                        dve.wait_ge(mm_done, 2 * i + b + 1)
                        nc.vector.tensor_copy(half[b][0][:], raw[:, b, :]).then_inc(hi_done, 1)

            @block.gpsimd
            def _(pool):
                pool.sem_inc(lo_done, 2)
                pool.sem_inc(opened, 1)
                with pool.Fori(0, tiles // 2) as i:
                    for b in range(2):
                        pool.wait_ge(hi_done, 2 * i + b + 1)
                        nc.gpsimd.tensor_tensor(half[b][1][:], raw[:, b, :], half[b][0][:].bitcast(F32),
                                                ALU.subtract).then_inc(lo_done, 1)

            @block.tensor
            def _(pe):
                with pe.Fori(0, tiles // 2) as i:
                    for b in range(2):
                        pe.wait_ge(lo_done, 2 * i + b + 3)
                        pe.wait_ge(out_done, 2 * i + b + 1)
                        for c in range(chunks):
                            for k, (w, a) in enumerate(PASSES):
                                last = nc.tensor.matmul(
                                    acc[b][:], half[b][w][:, c * P:(c + 1) * P], act[a][:, c0 + c, :],
                                    start=(c == 0 and k == 0), stop=(c == chunks - 1 and k == 2))
                        last.then_inc(mm_done, 1)

            @block.scalar
            def _(act_eng):
                act_eng.sem_inc(out_done, 2)
                with act_eng.Fori(0, tiles // 2) as i:
                    for b in range(2):
                        act_eng.wait_ge(mm_done, 2 * i + b + 3)
                        nc.scalar.activation(dest[:, bass.ds(2 * i + (d0 + b), 1), :].rearrange("p o t -> p (o t)"),
                                             acc[b][:], ACT.Copy).then_inc(out_done, 1)


def rms_norms(nc, name, groups, consts, split=None):
    ones, eps = consts["ones"], consts["eps"]
    terms = [(g, t, m) for g, (_, ts, _) in enumerate(groups) for t, m in ts]
    last_term = {g: k for k, (g, _, _) in enumerate(terms)}
    first_term = {}
    for k, (g, _, _) in enumerate(terms):
        first_term.setdefault(g, k)
    with Scope(nc, name) as s:
        R = 4
        sq = s.sb("sq", [P, R, T])
        root = s.sb("root", [P, 2, T])
        tmp = s.sb("tmp", [P, 2, T]) if split else None
        total = [s.ps(f"total{b}", [P, T]) for b in range(2)]
        squared, summed, rooted, normed, inner = (
            s.sem("squared"), s.sem("summed"), s.sem("rooted"), s.sem("normed"), s.sem("inner"))
        with nc.Block() as block:
            @block.scalar
            def _(act):
                def squares(g):
                    for k in range(first_term[g], last_term[g] + 1):
                        tile, _ = terms[k][1:]
                        if k >= R:
                            act.wait_ge(summed, k - R + 1)
                        p0 = tile.start_partition() if callable(tile.start_partition) else tile.start_partition
                        nc.scalar.activation(sq[p0:p0 + tile.shape[0], k % R, :], tile, ACT.Square
                                             ).then_inc(squared, 1)

                squares(0)
                for g, (width, _, _) in enumerate(groups):
                    if g + 1 < len(groups):
                        squares(g + 1)
                    act.wait_ge(summed, last_term[g] + 1)
                    if g >= 2:
                        act.wait_ge(normed, g - 1)
                    nc.scalar.activation(root[:, g % 2, :], total[g % 2][:], ACT.Sqrt, bias=eps[:, 0:1],
                                         scale=1.0 / width).then_inc(rooted, 1)

            @block.tensor
            def _(pe):
                for k, (g, tile, mask) in enumerate(terms):
                    if k == first_term[g] and g >= 2:
                        pe.wait_ge(rooted, g - 1)
                    pe.wait_ge(squared, k + 1)
                    p0 = tile.start_partition() if callable(tile.start_partition) else tile.start_partition
                    n = tile.shape[0]
                    nc.tensor.matmul(total[g % 2][:], ones[p0:p0 + n, :], sq[p0:p0 + n, k % R, :],
                                     start=(k == first_term[g]), stop=(k == last_term[g])).then_inc(summed, 1)

            @block.vector
            def _(dve):
                chain = Chain(dve, inner)
                for g, (_, _, outs) in enumerate(groups):
                    dve.wait_ge(rooted, g + 1)
                    chain(nc.vector.reciprocal(root[:, g % 2, :], root[:, g % 2, :]))
                    for n, (tile, gain, dest) in enumerate(outs):
                        p0 = tile.start_partition() if callable(tile.start_partition) else tile.start_partition
                        m = tile.shape[0]
                        r = root[p0:p0 + m, g % 2, :]
                        if split is None:
                            ins = nc.vector.scalar_tensor_tensor(dest, tile, gain, r, ALU.mult, ALU.mult)
                        else:
                            chain(nc.vector.scalar_tensor_tensor(tmp[:, n % 2, :], tile, gain, r,
                                                                 ALU.mult, ALU.mult))
                            chain(nc.vector.tensor_copy(split[0][:, dest, :], tmp[:, n % 2, :]))
                            ins = nc.vector.tensor_tensor(split[1][:, dest, :], tmp[:, n % 2, :],
                                                          split[0][:, dest, :].bitcast(F32), ALU.subtract)
                        if n < len(outs) - 1:
                            chain(ins)
                    ins.then_inc(normed, 1)


def attention(nc, name, blocks, consts, scale, maps, vtiles, neglam=None):
    ident = consts["ident"]
    N = len(blocks)
    with Scope(nc, name) as s:
        logits = s.sb("logits", [P, 2, maps, T])
        low = s.sb("low", [P, 2, 2])
        sums = s.sb("sums", [P, 2, 2])
        inv = s.sb("inv", [P, 2, 2])
        prob = s.sb("prob", [P, 2, T])
        probT = s.sb("probT", [P, 2, T])
        ps_s = [[s.ps(f"s{b}{m}", [P, T]) for m in range(maps)] for b in range(2)]
        ps_t = [s.ps(f"t{b}", [P, T]) for b in range(2)]
        ps_o = [s.ps(f"o{b}", [P, T]) for b in range(2)]
        scored, maxed, exped, weighted, turned, turned_out, valued, stored, inner = (
            s.sem(x) for x in ("scored", "maxed", "exped", "weighted", "turned", "turned_out", "valued",
                               "stored", "inner"))
        with nc.Block() as block:
            @block.tensor
            def _(pe):
                for st in range(N + 2):
                    if st < N:
                        n = st
                        qb, pairs, _, _, _ = blocks[n]
                        if n >= 2:
                            pe.wait_ge(maxed, n - 1)
                        for m in range(maps):
                            for k, (q, kk) in enumerate(pairs[m]):
                                last = nc.tensor.matmul(ps_s[n % 2][m][:, 0:(qb + 1) * P], q[:, qb * P:(qb + 1) * P],
                                                        kk[:, 0:(qb + 1) * P], start=(k == 0),
                                                        stop=(k == len(pairs[m]) - 1))
                        last.then_inc(scored, 1)
                    if 1 <= st <= N:
                        n = st - 1
                        pe.wait_ge(weighted, n + 1)
                        if n >= 2:
                            pe.wait_ge(turned_out, n - 1)
                        for kb in range(blocks[n][0] + 1):
                            last = nc.tensor.transpose(ps_t[n % 2][:, kb * P:(kb + 1) * P],
                                                       prob[:, n % 2, kb * P:(kb + 1) * P], ident[:])
                        last.then_inc(turned, 1)
                    if st >= 2:
                        n = st - 2
                        qb, _, _, values, _ = blocks[n]
                        pe.wait_ge(turned_out, n + 1)
                        if n >= 2:
                            pe.wait_ge(stored, n - 1)
                        for v in range(vtiles):
                            for kb in range(qb + 1):
                                last = nc.tensor.matmul(ps_o[n % 2][:, v * P:(v + 1) * P],
                                                        values[v][:, kb * P:(kb + 1) * P],
                                                        probT[:, n % 2, kb * P:(kb + 1) * P],
                                                        start=(kb == 0), stop=(kb == qb))
                        last.then_inc(valued, 1)

            @block.vector
            def _(dve):
                chain = Chain(dve, inner)
                for st in range(N + 1):
                    if st < N:
                        n = st
                        qb, _, bias, _, _ = blocks[n]
                        w = (qb + 1) * P
                        dve.wait_ge(scored, n + 1)
                        if n >= 2:
                            dve.wait_ge(weighted, n - 1)
                        for m in range(maps):
                            ins = nc.vector.scalar_tensor_tensor(logits[:, n % 2, m, 0:w], ps_s[n % 2][m][:, 0:w],
                                                                 scale, bias[:, T - w:T], ALU.mult, ALU.add)
                            chain(ins)
                        for m in range(maps):
                            ins = nc.vector.tensor_reduce(low[:, n % 2, m:m + 1], logits[:, n % 2, m, 0:w], AX_X,
                                                          ALU.max, negate=True)
                            if m < maps - 1:
                                chain(ins)
                        ins.then_inc(maxed, 1)
                    if st >= 1:
                        n = st - 1
                        w = (blocks[n][0] + 1) * P
                        dve.wait_ge(exped, n + 1)
                        if n >= 2:
                            dve.wait_ge(turned, n - 1)
                        chain(nc.vector.reciprocal(inv[:, n % 2, 0:maps], sums[:, n % 2, 0:maps]))
                        if maps == 1:
                            nc.vector.tensor_scalar(prob[:, n % 2, 0:w], logits[:, n % 2, 0, 0:w],
                                                    inv[:, n % 2, 0:1], None, ALU.mult).then_inc(weighted, 1)
                        else:
                            chain(nc.vector.tensor_scalar(prob[:, n % 2, 0:w], logits[:, n % 2, 0, 0:w],
                                                          inv[:, n % 2, 0:1], None, ALU.mult))
                            chain(nc.vector.tensor_scalar(inv[:, n % 2, 1:2], inv[:, n % 2, 1:2], neglam, None,
                                                          ALU.mult))
                            nc.vector.scalar_tensor_tensor(prob[:, n % 2, 0:w], logits[:, n % 2, 1, 0:w],
                                                           inv[:, n % 2, 1:2], prob[:, n % 2, 0:w], ALU.mult,
                                                           ALU.add).then_inc(weighted, 1)

            @block.scalar
            def _(act):
                for st in range(N + 2):
                    if st < N:
                        n = st
                        w = (blocks[n][0] + 1) * P
                        act.wait_ge(maxed, n + 1)
                        for m in range(maps):
                            ins = nc.scalar.activation(logits[:, n % 2, m, 0:w], logits[:, n % 2, m, 0:w], ACT.Exp,
                                                       bias=low[:, n % 2, m:m + 1],
                                                       accum_out=sums[:, n % 2, m:m + 1])
                        ins.then_inc(exped, 1)
                    if 1 <= st <= N:
                        n = st - 1
                        w = (blocks[n][0] + 1) * P
                        act.wait_ge(turned, n + 1)
                        if n >= 2:
                            act.wait_ge(valued, n - 1)
                        nc.scalar.activation(probT[:, n % 2, 0:w], ps_t[n % 2][:, 0:w], ACT.Copy
                                             ).then_inc(turned_out, 1)
                    if st >= 2:
                        n = st - 2
                        act.wait_ge(valued, n + 1)
                        nc.scalar.activation(blocks[n][4], ps_o[n % 2][:, 0:vtiles * P].rearrange(
                            "p (v q) -> p v q", v=vtiles), ACT.Copy).then_inc(stored, 1)


def turn_values(nc, name, tiles, consts):
    with Scope(nc, name) as s:
        ps = [s.ps(f"t{b}", [P, T]) for b in range(2)]
        turned, stored = s.sem("turned"), s.sem("stored")
        with nc.Block() as block:
            @block.tensor
            def _(pe):
                for n, tile in enumerate(tiles):
                    if n >= 2:
                        pe.wait_ge(stored, n - 1)
                    for tb in range(TB):
                        last = nc.tensor.transpose(ps[n % 2][:, tb * P:(tb + 1) * P], tile[:, tb * P:(tb + 1) * P],
                                                   consts["ident"][:])
                    last.then_inc(turned, 1)

            @block.scalar
            def _(act):
                for n, tile in enumerate(tiles):
                    act.wait_ge(turned, n + 1)
                    nc.scalar.activation(tile, ps[n % 2][:], ACT.Copy).then_inc(stored, 1)


def split_chunks(nc, name, source, act, count):
    with Scope(nc, name) as s:
        hi = s.sem("hi")
        with nc.Block() as block:
            @block.scalar
            def _(a):
                for c in range(count):
                    nc.scalar.activation(act[0][:, c, :], source[:, c, :], ACT.Copy).then_inc(hi, 1)

            @block.vector
            def _(dve):
                for c in range(count):
                    dve.wait_ge(hi, c + 1)
                    nc.vector.tensor_tensor(act[1][:, c, :], source[:, c, :], act[0][:, c, :].bitcast(F32),
                                            ALU.subtract)


def setup(nc, dram, consts, bias, neglam, xT):
    with Scope(nc, "setup") as s:
        relb = s.sb("relb", [33, DA_HEADS])
        relw = s.sb("relw", [33, DA_HEADS, P])
        onehot = s.sb("onehot", [33, BIAS_LEN])
        row = s.sb("row", [P, DA_HEADS, BIAS_LEN])
        prod = s.sb("prod", [P, 2])
        lam = s.sb("lam", [P, 2])
        ps = [s.ps(f"b{h}", [P, T]) for h in range(DA_HEADS)]
        ps_end = s.ps("end", [P, DA_HEADS, P])
        ps_l = s.ps("lam_ps", [P, 2])
        loaded, filled, rel_in, wide, rowed, row_out, skewed, inner, lam_mm, lam_exp, prodd, bias_mm = (
            s.sem(x) for x in ("loaded", "filled", "rel_in", "wide", "rowed", "row_out", "skewed", "inner", "lam_mm",
                               "lam_exp", "prodd", "bias_mm"))
        with nc.Block() as block:
            @block.sync
            def _(sp):
                sp.dma_start(relb[0:32, :], dram["rel_bias"][:, :]).then_inc(rel_in, 16)
                sp.dma_start(onehot[:], dram["onehot"][:, :]).then_inc(rel_in, 16)
                sp.dma_start(consts["gains"][:], dram["gains"][:, :]).then_inc(loaded, 16)
                for c in range(DC):
                    sp.dma_start(xT[:, c, :], dram["xT"][c]).then_inc(loaded, 16)
                for name in ("ident", "perm", "cos", "sin", "mask", "iota"):
                    sp.dma_start(consts[name][:], dram[name][:, :]).then_inc(loaded, 16)
                sp.wait_ge(rowed, DA_HEADS + 1)
                sp.dma_start(dram["skew"].rearrange("h (q n) -> q h n", n=BIAS_LEN), row[:]).then_inc(row_out, 16)
                sp.wait_ge(row_out, 16)
                for h in range(DA_HEADS):
                    src = dram["skew"][h, P - 1:P - 1 + P * (BIAS_LEN - 1)]
                    sp.dma_start(bias[:, h, :], src.rearrange("(q n) -> q n", n=BIAS_LEN - 1)[:, 0:T]
                                 ).then_inc(skewed, 16)
                sp.wait_ge(skewed, 16 * DA_HEADS)
                sp.wait_ge(loaded, 16 * (1 + DC + 6))

            @block.gpsimd
            def _(pool):
                nc.gpsimd.memset(consts["ones"][:], 1.0).then_inc(filled, 1)
                nc.gpsimd.memset(consts["eps"][:], EPS).then_inc(filled, 1)
                pool.wait_ge(filled, 2)
                nc.gpsimd.memset(relb[32:33, :], NEG).then_inc(filled, 1)

            @block.vector
            def _(dve):
                chain = Chain(dve, inner)
                dve.wait_ge(filled, 3)
                dve.wait_ge(rel_in, 32)
                for h in range(DA_HEADS):
                    nc.vector.tensor_copy(relw[:, h, :], relb[:, h:h + 1].to_broadcast([33, P])).then_inc(wide, 1)
                dve.wait_ge(loaded, 16 * (1 + DC + 6))
                g = consts["gains"]
                for k in range(2):
                    nc.vector.tensor_tensor(prod[:, k:k + 1], g[:, G_LAM + 2 * k:G_LAM + 2 * k + 1],
                                            g[:, G_LAM + 2 * k + 1:G_LAM + 2 * k + 2], ALU.mult).then_inc(prodd, 1)
                chain(nc.vector.tensor_scalar(g[:, G_DAOUT:G_DAOUT + 2], g[:, G_DAOUT:G_DAOUT + 2], 1.0 - LAM_INIT,
                                              None, ALU.mult))
                dve.wait_ge(lam_exp, 1)
                chain(nc.vector.tensor_tensor(neglam[:], lam[:, 1:2], lam[:, 0:1], ALU.subtract))
                chain(nc.vector.tensor_scalar(neglam[:], neglam[:], -LAM_INIT, None, ALU.add))

            @block.tensor
            def _(pe):
                pe.wait_ge(wide, DA_HEADS)
                for h in range(DA_HEADS):
                    nc.tensor.matmul(ps[h][:], relw[:, h, :], onehot[:, 0:T], start=True, stop=True
                                     ).then_inc(bias_mm, 1)
                for h in range(DA_HEADS):
                    last = nc.tensor.matmul(ps_end[:, h, :], relw[:, h, :], onehot[:, T:BIAS_LEN], start=True,
                                            stop=True)
                last.then_inc(bias_mm, 1)
                pe.wait_ge(prodd, 2)
                nc.tensor.matmul(ps_l[:], consts["ones"][:], prod[:], start=True, stop=True).then_inc(lam_mm, 1)

            @block.scalar
            def _(act):
                for h in range(DA_HEADS):
                    act.wait_ge(bias_mm, h + 1)
                    nc.scalar.activation(row[:, h, 0:T], ps[h][:], ACT.Copy).then_inc(rowed, 1)
                act.wait_ge(bias_mm, DA_HEADS + 1)
                nc.scalar.activation(row[:, :, T:BIAS_LEN], ps_end[:], ACT.Copy).then_inc(rowed, 1)
                act.wait_ge(lam_mm, 1)
                nc.scalar.activation(lam[:], ps_l[:], ACT.Exp).then_inc(lam_exp, 1)


def rotate(nc, name, tiles, consts):
    with Scope(nc, name) as s:
        turned = s.sb("turned", [P, 2, T])
        ps = [s.ps(f"p{b}", [P, T]) for b in range(2)]
        swapped, used, inner = s.sem("swapped"), s.sem("used"), s.sem("inner")
        with nc.Block() as block:
            @block.tensor
            def _(pe):
                for n, tile in enumerate(tiles):
                    if n >= 2:
                        pe.wait_ge(used, n - 1)
                    nc.tensor.matmul(ps[n % 2][:], consts["perm"][:], tile, start=True, stop=True
                                     ).then_inc(swapped, 1)

            @block.vector
            def _(dve):
                chain = Chain(dve, inner)
                for n, tile in enumerate(tiles):
                    dve.wait_ge(swapped, n + 1)
                    nc.vector.tensor_tensor(turned[:, n % 2, :], ps[n % 2][:], consts["sin"][:], ALU.mult
                                            ).then_inc(used, 1)
                    chain(nc.vector.tensor_tensor(tile, tile, consts["cos"][:], ALU.mult))
                    dve.wait_ge(used, n + 1)
                    chain(nc.vector.tensor_tensor(tile, tile, turned[:, n % 2, :], ALU.add))


def gate_sigmoids(nc, proj):
    with Scope(nc, "sig") as s:
        with nc.Block() as block:
            @block.scalar
            def _(act):
                for n in range(GATES, IN_TILES, 4):
                    nc.scalar.activation(proj[:, n:n + 4, :], proj[:, n:n + 4, :], ACT.Sigmoid)


def merge(nc, name, ya, gate, out, add):
    with Scope(nc, name) as s:
        done = s.sem("done")
        with nc.Block() as block:
            @block.vector
            def _(dve):
                for c in range(DC):
                    nc.vector.tensor_tensor(ya[:, c, :] if add else out[:, c, :], ya[:, c, :], gate[:, c, :], ALU.mult
                                            ).then_inc(done, 1)
                if add:
                    for c in range(DC):
                        dve.wait_ge(done, c + 1)
                        nc.vector.tensor_tensor(out[:, c, :], out[:, c, :], ya[:, c, :], ALU.add)


def add_chunks(nc, name, out, more):
    with nc.Block() as block:
        @block.vector
        def _(dve):
            for c in range(DC):
                nc.vector.tensor_tensor(out[:, c, :], out[:, c, :], more[:, c, :], ALU.add)


def route(nc, query, dram, consts, pickT):
    with Scope(nc, "route") as s:
        H, K = PEER_HEADS, TOPK
        keys = s.sb("keys", [P, 2 * H, KEYS])
        score = s.sb("score", [P, 2, 2 * H, KEYS])
        top = s.sb("top", [P, 2 * H, K])
        top_i = s.sb("top_i", [P, 2 * H, K], U32)
        top_f = s.sb("top_f", [P, 2 * H, K])
        cand = s.sb("cand", [P, H, K, K])
        best = s.sb("best", [P, H, K])
        pos = s.sb("pos", [P, H, K], U32)
        half_i = s.sb("half_i", [P, 2, H, K], U32)
        half_f = s.sb("half_f", [P, 2, H, K])
        hit = s.sb("hit", [P, H, K, K])
        pick = s.sb("pick", [P, 3, H, K])
        gsum = s.sb("gsum", [P, H])
        ps = [[s.ps(f"q{b}{q}", [P, 4, KEYS]) for q in range(4)] for b in range(2)]
        keys_in, scored, score_out, inner, shifted, exped, picked, turned, pick_out = (
            s.sem(x) for x in ("keys_in", "scored", "score_out", "inner", "shifted", "exped", "picked", "turned",
                               "pick_out"))
        iota = consts["iota"]
        with nc.Block() as block:
            @block.sync
            def _(sp):
                sp.dma_start(keys[:], dram["keys"].rearrange("p (g n) -> p g n", n=KEYS)).then_inc(keys_in, 16)

            @block.tensor
            def _(pe):
                pe.wait_ge(keys_in, 16)

                def scores(tb):
                    if tb >= 2:
                        pe.wait_ge(pick_out, tb - 1)
                    for g in range(2 * H):
                        last = nc.tensor.matmul(ps[tb % 2][g // 4][:, g % 4, :], query[:, g, tb * P:(tb + 1) * P],
                                                keys[:, g, :], start=True, stop=True)
                    last.then_inc(scored, 1)

                scores(0)
                for tb in range(TB):
                    if tb + 1 < TB:
                        scores(tb + 1)
                    pe.wait_ge(picked, tb + 1)
                    for k in range(3):
                        last = nc.tensor.transpose(ps[tb % 2][0][:, k, :],
                                                   pick[:, k, :, :].rearrange("p h k -> p (h k)"), consts["ident"][:])
                    last.then_inc(turned, 1)

            @block.scalar
            def _(act):
                def evacuate(tb):
                    act.wait_ge(scored, tb + 1)
                    if tb >= 2:
                        act.wait_ge(picked, tb - 1)
                    for q in range(4):
                        last = nc.scalar.activation(score[:, tb % 2, 4 * q:4 * q + 4, :], ps[tb % 2][q][:], ACT.Copy)
                    last.then_inc(score_out, 1)

                evacuate(0)
                for tb in range(TB):
                    act.wait_ge(shifted, tb + 1)
                    nc.scalar.activation(pick[:, 2, :, :], pick[:, 2, :, :], ACT.Exp).then_inc(exped, 1)
                    act.wait_ge(turned, tb + 1)
                    for k in range(3):
                        last = nc.scalar.activation(pickT[:, k, tb * P:(tb + 1) * P], ps[tb % 2][0][:, k, :],
                                                    ACT.Copy)
                    last.then_inc(pick_out, 1)
                    if tb + 1 < TB:
                        evacuate(tb + 1)

            @block.vector
            def _(dve):
                count = [0]

                def done(ins):
                    count[0] += 1
                    ins.then_inc(inner, 1)

                def sync():
                    dve.wait_ge(inner, count[0])

                def top16(rows, values, indices):
                    for st in range(5):
                        for r, row in enumerate(rows):
                            lo, hi = values[r][:, 0:8], values[r][:, 8:16]
                            if st == 0:
                                done(nc.vector.max(lo, row))
                            elif st == 1:
                                done(nc.vector.max_index(indices[r][:, 0:8], lo, row))
                            elif st == 2:
                                done(nc.vector.match_replace(row, lo, row, -3e38))
                            elif st == 3:
                                done(nc.vector.max(hi, row))
                            else:
                                done(nc.vector.max_index(indices[r][:, 8:16], hi, row))
                        sync()

                for tb in range(TB):
                    dve.wait_ge(score_out, tb + 1)
                    top16([score[:, tb % 2, g, :] for g in range(2 * H)], [top[:, g, :] for g in range(2 * H)],
                          [top_i[:, g, :] for g in range(2 * H)])
                    done(nc.vector.tensor_copy(top_f[:], top_i[:]))
                    pair = top[:].rearrange("p (h c) k -> p h c k", c=2)
                    done(nc.vector.tensor_tensor(cand[:], pair[:, :, 0, :].unsqueeze(3).to_broadcast([P, H, K, K]),
                                                 pair[:, :, 1, :].unsqueeze(2).to_broadcast([P, H, K, K]), ALU.add))
                    sync()
                    top16([cand[:, h, :, :].rearrange("p a b -> p (a b)") for h in range(H)],
                          [best[:, h, :] for h in range(H)], [pos[:, h, :] for h in range(H)])
                    done(nc.vector.tensor_scalar(half_i[:, 0], pos[:], 4, None, ALU.logical_shift_right))
                    done(nc.vector.tensor_scalar(half_i[:, 1], pos[:], 15, None, ALU.bitwise_and))
                    if tb >= 1:
                        dve.wait_ge(turned, tb)
                    ins = nc.vector.tensor_tensor(pick[:, 2], best[:], best[:, :, 0:1].to_broadcast([P, H, K]),
                                                  ALU.subtract)
                    ins.then_inc(shifted, 1)
                    sync()
                    done(nc.vector.tensor_copy(half_f[:], half_i[:]))
                    sync()
                    pair_i = top_f[:].rearrange("p (h c) k -> p h c k", c=2)
                    for c in range(2):
                        done(nc.vector.tensor_tensor(
                            hit[:], half_f[:, c].unsqueeze(3).to_broadcast([P, H, K, K]),
                            iota[:, 0:K].unsqueeze(1).unsqueeze(1).to_broadcast([P, H, K, K]), ALU.is_equal))
                        sync()
                        done(nc.vector.tensor_tensor(hit[:], hit[:],
                                                     pair_i[:, :, c, :].unsqueeze(2).to_broadcast([P, H, K, K]),
                                                     ALU.mult))
                        sync()
                        done(nc.vector.tensor_reduce(pick[:, c], hit[:], AX_X, ALU.add))
                        sync()
                    dve.wait_ge(exped, tb + 1)
                    done(nc.vector.tensor_reduce(gsum[:], pick[:, 2], AX_X, ALU.add))
                    sync()
                    done(nc.vector.reciprocal(gsum[:], gsum[:]))
                    sync()
                    nc.vector.tensor_tensor(pick[:, 2], pick[:, 2], gsum[:].unsqueeze(2).to_broadcast([P, H, K]),
                                            ALU.mult).then_inc(picked, 1)


def gate_matrices(nc, gates, consts, pickT):
    with Scope(nc, "gm") as s:
        HALF = 4
        grid = s.sb("grid", [P, 2, KEYS, P])
        row_i = s.sb("row_i", [P, 2, HALF, KEYS])
        row_j = s.sb("row_j", [P, 2, HALF, KEYS])
        ps = [s.ps(f"g{b}", [P, HALF, KEYS]) for b in range(2)]
        rows_i, rows_j, mm_done, out_done, grid_out = (
            s.sem("rows_i"), s.sem("rows_j"), s.sem("mm_done"), s.sem("out_done"), s.sem("grid_out"))
        grid_out = [s.sem(f"grid_out{b}") for b in range(2)]
        STEPS = P // (2 * HALF)
        QUADS = 2 * STEPS
        iota = consts["iota"]
        with nc.Block() as block:
            @block.vector
            def _(dve):
                for tb in range(TB):
                    with dve.Fori(0, STEPS) as i:
                        for b in range(2):
                            dve.wait_ge(mm_done, i * 2 + (tb * QUADS + b + 1))
                            for t in range(HALF):
                                tok = i * (2 * HALF) + (tb * P + b * HALF + t)
                                a = nc.vector.tensor_scalar(row_i[:, b, t, :], iota[:], pickT[:, 0, bass.ds(tok, 1)],
                                                            None, ALU.is_equal)
                                c = nc.vector.tensor_scalar(row_j[:, b, t, :], iota[:], pickT[:, 1, bass.ds(tok, 1)],
                                                            pickT[:, 2, bass.ds(tok, 1)], ALU.is_equal, ALU.mult)
                            a.then_inc(rows_i, 1)
                            c.then_inc(rows_j, 1)

            @block.tensor
            def _(pe):
                pe.sem_inc(mm_done, 2)
                for tb in range(TB):
                    with pe.Fori(0, STEPS) as i:
                        for b in range(2):
                            pe.wait_ge(rows_i, i * 2 + (tb * QUADS + b + 1))
                            pe.wait_ge(rows_j, i * 2 + (tb * QUADS + b + 1))
                            pe.wait_ge(out_done, i * 2 + (tb * QUADS + b + 1))
                            for t in range(HALF):
                                last = nc.tensor.matmul(ps[b][:, t, :], row_i[:, b, t, :], row_j[:, b, t, :],
                                                        start=True, stop=True)
                            last.then_inc(mm_done, 1)

            @block.scalar
            def _(act):
                act.sem_inc(out_done, 2)
                for tb in range(TB):
                    if tb >= 2:
                        act.wait_ge(grid_out[tb % 2], 16)
                    with act.Fori(0, STEPS) as i:
                        for b in range(2):
                            act.wait_ge(mm_done, i * 2 + (tb * QUADS + b + 3))
                            nc.scalar.activation(
                                grid[:, tb % 2, :, bass.ds(i * (2 * HALF) + b * HALF, HALF)].rearrange("p j t -> p t j"),
                                ps[b][:], ACT.Copy).then_inc(out_done, 1)

            @block.sync
            def _(sp):
                for tb in range(TB):
                    sp.wait_ge(out_done, (tb + 1) * QUADS + 2)
                    sp.dma_start(gates.rearrange("j i t -> i j t")[:, :, tb * P:(tb + 1) * P], grid[:, tb % 2]
                                 ).then_inc(grid_out[tb % 2], 16)
                for b in range(2):
                    sp.wait_ge(grid_out[b], 16 * TB // 2)


def experts(nc, dram, gates, act, total):
    J = 4
    GROUPS = KEYS // J
    with Scope(nc, "ex") as s:
        u_raw = s.sb("u_raw", [P, 2, D])
        u = [[s.sb(f"u{b}{h}", [P, D], F32R) for h in range(2)] for b in range(2)]
        v_raw = s.sb("v_raw", [P, 2, D])
        v = [[s.sb(f"v{q}{h}", [P, D], F32R) for h in range(2)] for q in range(J)]
        g_in = s.sb("g_in", [P, 2, T])
        gel = s.sb("gel", [P, 2, T])
        w = [[[s.sb(f"w{b}{q}{h}", [P, T], F32R) for h in range(2)] for q in range(J)] for b in range(2)]
        ps_a = [s.ps(f"a{b}", [P, T]) for b in range(2)]
        ps_b = [s.ps(f"b{b}", [P, T]) for b in range(2)]
        u_in = [s.sem(f"u_in{b}") for b in range(2)]
        v_in = [s.sem(f"v_in{b}") for b in range(2)]
        gate_in = [s.sem(f"gate_in{b}") for b in range(2)]
        (u_hi, u_lo, v_hi, v_lo, a_done, gelued, gated, w_hi, w_lo, b_used, b_done, added, opened, written) = (
            s.sem(x) for x in ("u_hi", "u_lo", "v_hi", "v_lo", "a_done", "gelued", "gated", "w_hi", "w_lo", "b_used",
                               "b_done", "added", "opened", "written"))
        v_dram = dram["v"].rearrange("(i j) d -> j i d", j=KEYS)
        with nc.Block() as block:
            @block.sync
            def _(sp):
                def load(buffer, source, j, free, count, landed):
                    sp.wait_ge(free, count)
                    sp.wait_ge(opened, 1)
                    sp.dma_start(buffer, source[bass.ds(j, 1)].rearrange("o p f -> p (o f)")).then_inc(landed, 16)

                for n in range(J):
                    load(u_raw[:, n % 2, :], dram["u"], n, u_lo, n + 1, u_in[n % 2])
                    load(g_in[:, n % 2, :], gates, n, gated, n + 1, gate_in[n % 2])
                with sp.Fori(J // 2, KEYS // 2) as i:
                    for b in range(2):
                        n = sp.snap(2 * i + b)
                        load(u_raw[:, b, :], dram["u"], n, u_lo, n + 1, u_in[b])
                        load(g_in[:, b, :], gates, n, gated, n + 1, gate_in[b])
                        m = sp.snap(2 * i + (b - J))
                        load(v_raw[:, b, :], v_dram, m, v_lo, m + 1, v_in[b])
                for m in range(KEYS - J, KEYS):
                    load(v_raw[:, m % 2, :], v_dram, m, v_lo, m + 1, v_in[m % 2])

            @block.gpsimd
            def _(pool):
                for count in (u_lo, v_lo, a_done, gelued, added):
                    pool.sem_inc(count, 2)
                pool.sem_inc(b_used, 1)
                pool.sem_inc(opened, 1)

                def split_u(n, q):
                    pool.wait_ge(u_hi, n + 1)
                    nc.gpsimd.tensor_tensor(u[q % 2][1][:], u_raw[:, q % 2, :], u[q % 2][0][:].bitcast(F32),
                                            ALU.subtract).then_inc(u_lo, 1)

                def split_v(n, q):
                    pool.wait_ge(v_hi, n + 1)
                    nc.gpsimd.tensor_tensor(v[q][1][:], v_raw[:, q % 2, :], v[q][0][:].bitcast(F32), ALU.subtract
                                            ).then_inc(v_lo, 1)

                def split_w(n, par, q):
                    pool.wait_ge(w_hi, n + 1)
                    nc.gpsimd.tensor_tensor(w[par][q][1][:], gel[:, q % 2, :], w[par][q][0][:].bitcast(F32),
                                            ALU.subtract).then_inc(w_lo, 1)

                def weigh(g, par, q):
                    split_w(g * J + q, par, q)

                def step(g, par, more=True):
                    for q in range(J):
                        split_v(g * J + q, q)
                        if q < J // 2:
                            split_u((g + 1) * J + (q + 2), q)
                        weigh(g + 1, par, q)
                    if more:
                        for q in range(2):
                            split_u((g + 2) * J + q, q)

                for q in range(J):
                    split_u(q, q)
                    weigh(0, 0, q)
                for q in range(2):
                    split_u(J + q, q)
                with pool.Fori(0, (GROUPS - 2) // 2) as i:
                    for k in range(2):
                        step(2 * i + k, (k + 1) % 2)
                step(GROUPS - 2, 1, False)
                for q in range(J):
                    split_v((GROUPS - 1) * J + q, q)

            @block.vector
            def _(dve):
                dve.sem_inc(gated, 2)

                def split_u(n, seen, q):
                    dve.wait_ge(u_in[q % 2], seen)
                    dve.wait_ge(a_done, n + 1)
                    nc.vector.tensor_copy(u[q % 2][0][:], u_raw[:, q % 2, :]).then_inc(u_hi, 1)

                def split_v(g, seen, q):
                    dve.wait_ge(v_in[q % 2], seen)
                    dve.wait_ge(b_used, g + 1)
                    nc.vector.tensor_copy(v[q][0][:], v_raw[:, q % 2, :]).then_inc(v_hi, 1)

                def gate(n, seen, par, q):
                    dve.wait_ge(gelued, n + 3)
                    dve.wait_ge(gate_in[q % 2], seen)
                    nc.vector.tensor_tensor(gel[:, q % 2, :], gel[:, q % 2, :], g_in[:, q % 2, :], ALU.mult
                                            ).then_inc(gated, 1)
                    dve.wait_ge(gated, n + 3)
                    nc.vector.tensor_copy(w[par][q][0][:], gel[:, q % 2, :]).then_inc(w_hi, 1)

                def seen(g, q):
                    return g * (16 * J // 2) + (16 * (q // 2) + 16)

                def add(g):
                    for c in range(DC):
                        dve.wait_ge(b_done, g * DC + (c + 1))
                        nc.vector.tensor_tensor(total[:, c, :], total[:, c, :], ps_b[c % 2][:], ALU.add
                                                ).then_inc(added, 1)

                def step(g, par, more=True):
                    for q in range(J):
                        split_v(g, seen(g, q), q)
                        if q < J // 2:
                            split_u((g + 1) * J + (q + 2), seen(g + 1, q + 2), q)
                        gate((g + 1) * J + q, seen(g + 1, q), par, q)
                    if more:
                        for q in range(2):
                            split_u((g + 2) * J + q, seen(g + 2, q), q)
                    add(g)

                for q in range(J):
                    split_u(q, seen(0, q), q)
                    gate(q, seen(0, q), 0, q)
                for q in range(2):
                    split_u(J + q, seen(1, q), q)
                with dve.Fori(0, (GROUPS - 2) // 2) as i:
                    for k in range(2):
                        step(2 * i + k, (k + 1) % 2)
                step(GROUPS - 2, 1, False)
                for q in range(J):
                    split_v(GROUPS - 1, seen(GROUPS - 1, q), q)
                add(GROUPS - 1)

            @block.scalar
            def _(a):
                with a.Fori(0, KEYS // 2) as i:
                    for b in range(2):
                        a.wait_ge(a_done, 2 * i + (b + 3))
                        a.wait_ge(w_lo, 2 * i + (b + 1))
                        nc.scalar.activation(gel[:, b, :], ps_a[b][:], ACT.Gelu).then_inc(gelued, 1)

            @block.tensor
            def _(pe):
                pe.sem_inc(w_lo, 2)

                def phase_a(g):
                    for q in range(J):
                        b = q % 2
                        n = g * J + q
                        pe.wait_ge(u_lo, n + 3)
                        pe.wait_ge(gelued, n + 1)
                        for c in range(DC):
                            for k, (x, y) in enumerate(PASSES):
                                last = nc.tensor.matmul(ps_a[b][:], u[b][x][:, c * P:(c + 1) * P], act[y][:, c, :],
                                                        start=(c == 0 and k == 0), stop=(c == DC - 1 and k == 2))
                        last.then_inc(a_done, 1)

                def phase_b(g, par):
                    pe.wait_ge(w_lo, g * J + (J + 2))
                    pe.wait_ge(v_lo, g * J + (J + 2))
                    for c in range(DC):
                        pe.wait_ge(added, g * DC + (c + 1))
                        for q in range(J):
                            for k, (x, y) in enumerate(PASSES):
                                last = nc.tensor.matmul(ps_b[c % 2][:], v[q][x][:, c * P:(c + 1) * P],
                                                        w[par][q][y][:], start=(q == 0 and k == 0),
                                                        stop=(q == J - 1 and k == 2))
                        last.then_inc(b_done, 1)
                    pe.wait_ge(b_done, g * DC + DC)
                    pe.sem_inc(b_used, 1)

                phase_a(0)
                with pe.Fori(0, (GROUPS - 2) // 2) as i:
                    for k in range(2):
                        g = 2 * i + k
                        phase_a(g + 1)
                        phase_b(g, k)
                phase_a(GROUPS - 1)
                phase_b(GROUPS - 2, 0)
                phase_b(GROUPS - 1, 1)


def store(nc, out, total):
    with Scope(nc, "store") as s:
        stored = s.sem("stored")
        with nc.Block() as block:
            @block.sync
            def _(sp):
                for c in range(DC):
                    sp.dma_start(out[c], total[:, c, :]).then_inc(stored, 16)
                sp.wait_ge(stored, 16 * DC)


def program(nc, dram, out):
    dram["skew"] = nc.dram_tensor("skew", [DA_HEADS, P * BIAS_LEN], F32).ap()
    gates_dram = nc.dram_tensor("gate_grid", [KEYS, P, T], F32).ap()
    with Scope(nc, "all") as s:
        consts = {"ones": s.sb("ones", [P, P]), "eps": s.sb("eps", [P, 1]), "ident": s.sb("ident", [P, P]),
                  "iota": s.sb("iota", [P, KEYS]), "gains": s.sb("gains", [P, G_COLS])}
        neglam = s.sb("neglam", [P, 1])
        xT = s.sb("xT", [P, DC, T])
        act = [s.sb(f"act{h}", [P, DC, T], F32R) for h in range(2)]
        gain = lambda k: consts["gains"][:, k:k + 1]
        with Scope(nc, "mix") as m:
            proj = m.sb("proj", [P, IN_TILES, T])
            consts.update(perm=m.sb("perm", [P, P]), cos=m.sb("cos", [P, T]), sin=m.sb("sin", [P, T]),
                          mask=m.sb("mask", [P, T]))
            bias = m.sb("bias", [P, DA_HEADS, T])
            setup(nc, dram, consts, bias, neglam, xT)
            rms_norms(nc, "n_x", [(D, [(xT[:, c, :], None) for c in range(DC)],
                                   [(xT[:, c, :], gain(G_ATTN + c), c) for c in range(DC)])], consts, act)
            project(nc, "p_in", dram["w_in"], DC, IN_TILES, act, 0, proj, 0)
            gate_sigmoids(nc, proj)
            tile = lambda n: proj[:, n, :]
            rms_norms(nc, "n_qk", [(DA_DIM, [(tile(n), None)], [(tile(n), gain(G_DAQ if n < KA else G_DAK), tile(n))])
                                   for n in range(QA, VA)], consts)
            turn_values(nc, "tv_a", [tile(n) for n in range(VA, CQ)], consts)
            extra = m.sb("extra", [P, 12, T])
            blocks = []
            for h in range(DA_HEADS):
                for qb in range(TB):
                    blocks.append((qb, [[(tile(QA + 2 * h + k), tile(KA + 2 * h + k))] for k in range(2)],
                                   bias[:, h, :], [tile(VA + 2 * h + k) for k in range(2)],
                                   extra[:, 2 * h:2 * h + 2, qb * P:(qb + 1) * P]))
            attention(nc, "da", blocks, consts, DA_DIM ** -0.5, 2, 2, neglam[:, 0:1])
            rms_norms(nc, "n_ya", [(DA_V, [(extra[:, 2 * h + k, :], None) for k in range(2)],
                                    [(extra[:, 2 * h + k, :], gain(G_DAOUT + k), 2 * h + k) for k in range(2)])
                                   for h in range(DA_HEADS)], consts, act)
            project(nc, "p_da", dram["w_da"], DC, DC, act, 0, extra, 0)
            merged = proj[:, 0:DC, :]
            merge(nc, "m_a", extra, proj[:, GATES:GATES + DC, :], merged, False)
            rms_norms(nc, "n_lat",
                      [(Q_RANK, [(tile(CQ + c), None) for c in range(3)],
                        [(tile(CQ + c), gain(G_QLAT + c), c) for c in range(3)]),
                       (KV_RANK, [(tile(CKV + c), None) for c in range(2)],
                        [(tile(CKV + c), gain(G_KVLAT + c), 3 + c) for c in range(2)])], consts, act)
            project(nc, "p_uq", dram["w_uq"], Q_RANK // P, 12, act, 0, extra, 0)
            project(nc, "p_ukv", dram["w_ukv"], KV_RANK // P, 16, act, 3, proj, 8)
            qn = lambda h: extra[:, h, :]
            qr = lambda h: extra[ROPE * (h % 2):ROPE * (h % 2) + ROPE, 8 + h // 2, :]
            kn = lambda h: proj[:, 8 + h, :]
            kr = lambda h: proj[ROPE * (h % 2):ROPE * (h % 2) + ROPE, KR, :]
            kr_out = lambda h: proj[ROPE * (h % 2):ROPE * (h % 2) + ROPE, CQ + h // 2, :]
            g_of = lambda k, h: consts["gains"][ROPE * (h % 2):ROPE * (h % 2) + ROPE, k:k + 1]
            rotate(nc, "rot", [extra[:, 8 + n, :] for n in range(4)] + [tile(KR)], consts)
            rms_norms(nc, "n_mq",
                      [(NOPE + ROPE, [(qn(h), None), (qr(h), None)],
                        [(qn(h), gain(G_MQN), qn(h)), (qr(h), g_of(G_MQR, h), qr(h))]) for h in range(MLA_HEADS)] +
                      [(NOPE + ROPE, [(kn(h), None), (kr(h), None)],
                        [(kn(h), gain(G_MKN), kn(h)), (kr(h), g_of(G_MKR, h), kr_out(h))]) for h in range(MLA_HEADS)],
                      consts)
            turn_values(nc, "tv_b", [proj[:, 16 + h, :] for h in range(MLA_HEADS)], consts)
            blocks = []
            for h in range(MLA_HEADS):
                for qb in range(TB):
                    blocks.append((qb, [[(qn(h), kn(h)), (qr(h), kr_out(h))]], consts["mask"][:],
                                   [proj[:, 16 + h, :]], extra[:, h:h + 1, qb * P:(qb + 1) * P]))
            attention(nc, "mla", blocks, consts, (NOPE + ROPE) ** -0.5, 1, 1)
            split_chunks(nc, "s_yb", extra, act, DC)
            project(nc, "p_mla", dram["w_mla"], DC, DC, act, 0, extra, 0)
            merge(nc, "m_b", extra, proj[:, GATES + DC:GATES + 2 * DC, :], merged, True)
            split_chunks(nc, "s_m", merged, act, DC)
            project(nc, "p_out", dram["w_out"], DC, DC, act, 0, extra, 0)
            add_chunks(nc, "x2", xT, extra)
        with Scope(nc, "peer") as m:
            pickT = m.sb("pickT", [P, 3, T])
            with Scope(nc, "rt") as r:
                query = r.sb("query", [P, 2 * PEER_HEADS, T])
                rms_norms(nc, "n_x2", [(D, [(xT[:, c, :], None) for c in range(DC)],
                                        [(xT[:, c, :], gain(G_FFN + c), c) for c in range(DC)])], consts, act)
                project(nc, "p_q", dram["w_query"], DC, 2 * PEER_HEADS, act, 0, query, 0)
                route(nc, query, dram, consts, pickT)
            gate_matrices(nc, gates_dram, consts, pickT)
        experts(nc, dram, gates_dram, act, xT)
        store(nc, out, xT)


def shape_constants():
    import numpy as np
    c = {"ident": np.eye(P, dtype=np.float32)}
    c["iota"] = np.tile(np.arange(KEYS, dtype=np.float32), (P, 1))
    f = np.arange(P) % (ROPE // 2)
    inv = np.float32(10000.0) ** (-(2 * f).astype(np.float32) / np.float32(ROPE))
    ang = inv[:, None] * np.arange(T, dtype=np.float32)[None, :]
    first = (np.arange(P) % ROPE) < ROPE // 2
    c["cos"] = np.cos(ang).astype(np.float32)
    c["sin"] = (np.sin(ang) * np.where(first, -1.0, 1.0)[:, None]).astype(np.float32)
    perm = np.zeros((P, P), np.float32)
    for m in range(P):
        perm[m + ROPE // 2 if first[m] else m - ROPE // 2, m] = 1.0
    c["perm"] = perm
    q, n = np.arange(P)[:, None], np.arange(T)[None, :]
    c["mask"] = np.where(T - P + q - n >= 0, 0.0, NEG).astype(np.float32)
    dist = T - 1 - np.arange(BIAS_LEN)
    nf = np.maximum(dist, 16).astype(np.float32)
    large = 16 + (np.log(nf / 16) / np.log(8.0) * 16).astype(np.int32)
    bucket = np.where(dist < 16, np.maximum(dist, 0), np.minimum(large, 31))
    onehot = np.zeros((33, BIAS_LEN), np.float32)
    onehot[np.where(dist >= 0, bucket, 32), np.arange(BIAS_LEN)] = 1.0
    c["onehot"] = onehot
    return c


def kernel(**inputs):
    import numpy as np
    import concourse.bacc as bacc
    from concourse.bass_utils import run_bass_kernel_spmd

    a = {k: np.asarray(v) for k, v in inputs.items()}

    def tiles(w):
        k, n = w.shape
        return np.ascontiguousarray(w.reshape(k // P, P, n // P, P).transpose(2, 1, 0, 3)).reshape(n // P, P, k)

    def cols(v):
        return v.reshape(-1, P).T

    w_in = a["w_in"][0]
    kr0 = (CKV + 2) * P
    uq = a["mla_w_uq"][0].reshape(Q_RANK, MLA_HEADS, NOPE + ROPE)
    ukv = a["mla_w_ukv"][0].reshape(KV_RANK, MLA_HEADS, NOPE + MLA_V)
    qn, kn = a["mla_q_norm"][0], a["mla_k_norm"][0]
    data = {
        "xT": np.ascontiguousarray(a["x"][0].T).reshape(DC, P, T),
        "w_in": tiles(np.concatenate([w_in[:, :kr0 + ROPE], w_in[:, kr0:kr0 + ROPE], w_in[:, kr0 + ROPE:]], axis=1)),
        "w_da": tiles(a["da_proj"][0]),
        "w_uq": tiles(np.concatenate([uq[:, :, :NOPE].reshape(Q_RANK, -1), uq[:, :, NOPE:].reshape(Q_RANK, -1)], axis=1)),
        "w_ukv": tiles(np.concatenate([ukv[:, :, :NOPE].reshape(KV_RANK, -1), ukv[:, :, NOPE:].reshape(KV_RANK, -1)],
                                      axis=1)),
        "w_mla": tiles(a["mla_proj"][0]),
        "w_out": tiles(a["w_out"][0]),
        "w_query": tiles(a["peer_w_query"][0]),
        "rel_bias": a["rel_bias"],
        "keys": np.ascontiguousarray(a["peer_sub_keys"][0].reshape(2 * PEER_HEADS, KEYS, P).transpose(2, 0, 1)
                                     ).reshape(P, 2 * PEER_HEADS * KEYS),
        "u": np.ascontiguousarray(a["peer_u"][0].reshape(KEYS, KEYS, DC, P).transpose(1, 3, 2, 0)).reshape(KEYS, P, D),
        "v": a["peer_v"][0],
        "gains": np.ascontiguousarray(np.concatenate(
            [cols(a["attn_norm"][0]), cols(a["ffn_norm"][0]), cols(a["da_q_norm"][0]), cols(a["da_k_norm"][0]),
             cols(a["da_out_norm"][0]), cols(a["mla_q_latent_norm"][0]), cols(a["mla_kv_latent_norm"][0]),
             cols(qn[:NOPE]), cols(np.concatenate([qn[NOPE:], qn[NOPE:]])),
             cols(kn[:NOPE]), cols(np.concatenate([kn[NOPE:], kn[NOPE:]])),
             cols(a["da_lambda_q1"][0]), cols(a["da_lambda_k1"][0]), cols(a["da_lambda_q2"][0]),
             cols(a["da_lambda_k2"][0])], axis=1)),
    }
    data.update(shape_constants())
    nc = bacc.Bacc("TRN2", target_bir_lowering=False, num_devices=1)
    arrays, dram = {}, {}
    for name, x in data.items():
        arrays[f"in_{name}"] = x
        dram[name] = nc.dram_tensor(f"in_{name}", x.shape, F32, kind="ExternalInput").ap()
    out = nc.dram_tensor("out_T", (DC, P, T), F32, kind="ExternalOutput").ap()
    program(nc, dram, out)
    r = run_bass_kernel_spmd(nc, [arrays], core_ids=[0])
    return np.ascontiguousarray(r.results[0]["out_T"].reshape(D, T).T)[None]
```

```python
from contextlib import ExitStack

import concourse.bass as bass
from concourse import mybir

F32 = mybir.dt.float32
F32R = mybir.dt.float32r
U32 = mybir.dt.uint32
ALU = mybir.AluOpType
ACT = mybir.ActivationFunctionType
AX_X = mybir.AxisListType.X

P = 128
D = 1024
DC = D // P
T = 512
TB = T // P
EPS = 1e-6
NEG = -1e30

DA_HEADS, DA_DIM, DA_V = 4, 128, 256
MLA_HEADS, NOPE, ROPE, MLA_V = 8, 128, 64, 128
Q_RANK, KV_RANK = 384, 256
LAM_INIT = 0.8 - 0.6
KEYS, TOPK, PEER_HEADS = 128, 16, 8
HK = PEER_HEADS * TOPK

QA, KA, VA, CQ, CKV, KR, GATES, IN_TILES = 0, 8, 16, 24, 27, 29, 30, 46
G_ATTN, G_FFN, G_DAQ, G_DAK, G_DAOUT, G_QLAT, G_KVLAT, G_MQN, G_MQR, G_MKN, G_MKR, G_LAM, G_COLS = (
    0, 8, 16, 17, 18, 20, 23, 25, 26, 27, 28, 29, 33)
BIAS_LEN = 640
PASSES = ((0, 0), (0, 1), (1, 0))


USED_SEMAPHORES = []


def recycle_semaphores(nc):
    nc.all_engine_barrier()
    nc.clear_and_free_semaphores(USED_SEMAPHORES)
    nc.all_engine_barrier()
    USED_SEMAPHORES.clear()


class Scope:

    def __init__(self, nc, name):
        self.nc, self.name, self.stack, self.sems = nc, name, ExitStack(), []

    def __enter__(self):
        return self

    def __exit__(self, *e):
        USED_SEMAPHORES.extend(self.sems)
        return self.stack.__exit__(*e)

    def sb(self, name, shape, dt=F32):
        return self.stack.enter_context(self.nc.sbuf_tensor(f"{self.name}_{name}", shape, dt))

    def ps(self, name, shape):
        return self.stack.enter_context(self.nc.psum_tensor(f"{self.name}_{name}", shape, F32))

    def sem(self, name):
        self.sems.append(self.nc.alloc_semaphore(f"{self.name}_{name}"))
        return self.sems[-1]


class Chain:

    def __init__(self, eng, sem):
        self.eng, self.sem, self.n = eng, sem, 0

    def __call__(self, ins):
        self.n += 1
        ins.then_inc(self.sem, 1)
        self.eng.wait_ge(self.sem, self.n)


def each(eng, start, end, unroll, body):
    laps = (end - start) // unroll
    if laps > 1:
        with eng.Fori(0, laps) as i:
            for k in range(unroll):
                body(i * unroll + (start + k), k, i + start // unroll)
        start += laps * unroll
    for n in range(start, end):
        body(n, n % unroll, n // unroll)


def project(nc, name, weights, chunks, tiles, act, c0, dest, d0, slots=2):
    with Scope(nc, name) as s:
        raw = s.sb("raw", [P, slots, chunks * P])
        half = [[s.sb(f"half{b}{h}", [P, chunks * P], F32R) for h in range(2)] for b in range(2)]
        acc = [s.ps(f"acc{b}", [P, T]) for b in range(2)]
        raw_in = [s.sem(f"raw_in{b}") for b in range(slots)]
        hi_done, lo_done, mm_done, out_done, opened = (
            s.sem("hi_done"), s.sem("lo_done"), s.sem("mm_done"), s.sem("out_done"), s.sem("opened"))

        with nc.Block() as block:
            @block.sync
            def _(sp):
                def load(n, r, lap):
                    sp.wait_ge(lo_done, n + 1)
                    sp.wait_ge(opened, 1)
                    sp.dma_start(raw[:, r, :], weights[bass.ds(n, 1)].rearrange("o p f -> p (o f)")
                                 ).then_inc(raw_in[r], 16)
                each(sp, 0, tiles, slots, load)

            @block.scalar
            def _(a):
                a.sem_inc(out_done, 2)

                def round_weights(n, r, lap, free=None):
                    a.wait_ge(raw_in[r], lap * 16 + 16)
                    nc.scalar.activation(half[r % 2][0][:], raw[:, r, :], ACT.Copy).then_inc(hi_done, 1)

                def evacuate(n, r):
                    a.wait_ge(mm_done, n + 1)
                    nc.scalar.activation(dest[:, bass.ds(n + d0, 1), :].rearrange("p o t -> p (o t)"),
                                         acc[r % 2][:], ACT.Copy).then_inc(out_done, 1)

                def body(n, r, lap):
                    evacuate(n, r)
                    round_weights(n + 2, (r + 2) % slots, lap + (r + 2) // slots)

                for n in range(2):
                    round_weights(n, n % slots, n // slots)
                each(a, 0, tiles - 2, slots, body)
                for n in range(tiles - 2, tiles):
                    evacuate(n, n % slots)

            @block.vector
            def _(dve):
                dve.sem_inc(lo_done, slots)
                dve.sem_inc(opened, 1)

                def rest(n, r, lap):
                    dve.wait_ge(hi_done, n + 1)
                    nc.vector.tensor_tensor(half[r % 2][1][:], raw[:, r, :], half[r % 2][0][:].bitcast(F32),
                                            ALU.subtract).then_inc(lo_done, 1)
                each(dve, 0, tiles, slots, rest)

            @block.tensor
            def _(pe):
                def product(n, r, lap):
                    b = r % 2
                    pe.wait_ge(lo_done, n + (slots + 1))
                    pe.wait_ge(out_done, n + 1)
                    for c in range(chunks):
                        for k, (w, x) in enumerate(PASSES):
                            last = nc.tensor.matmul(
                                acc[b][:], half[b][w][:, c * P:(c + 1) * P], act[x][:, c0 + c, :],
                                start=(c == 0 and k == 0), stop=(c == chunks - 1 and k == 2))
                    last.then_inc(mm_done, 1)
                each(pe, 0, tiles, slots, product)


def rms_norms(nc, name, groups, consts, split=None):
    ones, eps = consts["ones"], consts["eps"]
    terms = [(g, t, m) for g, (_, ts, _) in enumerate(groups) for t, m in ts]
    last_term = {g: k for k, (g, _, _) in enumerate(terms)}
    first_term = {}
    for k, (g, _, _) in enumerate(terms):
        first_term.setdefault(g, k)
    with Scope(nc, name) as s:
        R = 4
        sq = s.sb("sq", [P, R, T])
        root = s.sb("root", [P, 2, T])
        tmp = s.sb("tmp", [P, 2, T]) if split else None
        total = [s.ps(f"total{b}", [P, T]) for b in range(2)]
        squared, summed, rooted, normed, inner = (
            s.sem("squared"), s.sem("summed"), s.sem("rooted"), s.sem("normed"), s.sem("inner"))
        with nc.Block() as block:
            @block.scalar
            def _(act):
                def squares(g):
                    for k in range(first_term[g], last_term[g] + 1):
                        tile, _ = terms[k][1:]
                        if k >= R:
                            act.wait_ge(summed, k - R + 1)
                        p0 = tile.start_partition() if callable(tile.start_partition) else tile.start_partition
                        nc.scalar.activation(sq[p0:p0 + tile.shape[0], k % R, :], tile, ACT.Square
                                             ).then_inc(squared, 1)

                squares(0)
                for g, (width, _, _) in enumerate(groups):
                    if g + 1 < len(groups):
                        squares(g + 1)
                    act.wait_ge(summed, last_term[g] + 1)
                    if g >= 2:
                        act.wait_ge(normed, g - 1)
                    nc.scalar.activation(root[:, g % 2, :], total[g % 2][:], ACT.Sqrt, bias=eps[:, 0:1],
                                         scale=1.0 / width).then_inc(rooted, 1)

            @block.tensor
            def _(pe):
                for k, (g, tile, mask) in enumerate(terms):
                    if k == first_term[g] and g >= 2:
                        pe.wait_ge(rooted, g - 1)
                    pe.wait_ge(squared, k + 1)
                    p0 = tile.start_partition() if callable(tile.start_partition) else tile.start_partition
                    n = tile.shape[0]
                    nc.tensor.matmul(total[g % 2][:], ones[p0:p0 + n, :], sq[p0:p0 + n, k % R, :],
                                     start=(k == first_term[g]), stop=(k == last_term[g])).then_inc(summed, 1)

            @block.vector
            def _(dve):
                chain = Chain(dve, inner)
                for g, (_, _, outs) in enumerate(groups):
                    dve.wait_ge(rooted, g + 1)
                    chain(nc.vector.reciprocal(root[:, g % 2, :], root[:, g % 2, :]))
                    for n, (tile, gain, dest) in enumerate(outs):
                        p0 = tile.start_partition() if callable(tile.start_partition) else tile.start_partition
                        m = tile.shape[0]
                        r = root[p0:p0 + m, g % 2, :]
                        if split is None:
                            ins = nc.vector.scalar_tensor_tensor(dest, tile, gain, r, ALU.mult, ALU.mult)
                        else:
                            chain(nc.vector.scalar_tensor_tensor(tmp[:, n % 2, :], tile, gain, r,
                                                                 ALU.mult, ALU.mult))
                            chain(nc.vector.tensor_copy(split[0][:, dest, :], tmp[:, n % 2, :]))
                            ins = nc.vector.tensor_tensor(split[1][:, dest, :], tmp[:, n % 2, :],
                                                          split[0][:, dest, :].bitcast(F32), ALU.subtract)
                        if n < len(outs) - 1:
                            chain(ins)
                    ins.then_inc(normed, 1)


def attention(nc, name, blocks, consts, scale, maps, vtiles, neglam=None):
    ident = consts["ident"]
    N = len(blocks)
    with Scope(nc, name) as s:
        logits = s.sb("logits", [P, 2, maps, T])
        low = s.sb("low", [P, 2, 2])
        sums = s.sb("sums", [P, 2, 2])
        inv = s.sb("inv", [P, 2, 2])
        prob = s.sb("prob", [P, 2, T])
        probT = s.sb("probT", [P, 2, T])
        ps_s = [[s.ps(f"s{b}{m}", [P, T]) for m in range(maps)] for b in range(2)]
        ps_t = [s.ps(f"t{b}", [P, T]) for b in range(2)]
        ps_o = [s.ps(f"o{b}", [P, T]) for b in range(2)]
        scored, maxed, exped, weighted, turned, turned_out, valued, stored, inner = (
            s.sem(x) for x in ("scored", "maxed", "exped", "weighted", "turned", "turned_out", "valued",
                               "stored", "inner"))
        with nc.Block() as block:
            @block.tensor
            def _(pe):
                for st in range(N + 2):
                    if st < N:
                        n = st
                        qb, pairs, _, _, _ = blocks[n]
                        if n >= 2:
                            pe.wait_ge(maxed, n - 1)
                        for m in range(maps):
                            for k, (q, kk) in enumerate(pairs[m]):
                                last = nc.tensor.matmul(ps_s[n % 2][m][:, 0:(qb + 1) * P], q[:, qb * P:(qb + 1) * P],
                                                        kk[:, 0:(qb + 1) * P], start=(k == 0),
                                                        stop=(k == len(pairs[m]) - 1))
                        last.then_inc(scored, 1)
                    if 1 <= st <= N:
                        n = st - 1
                        pe.wait_ge(weighted, n + 1)
                        if n >= 2:
                            pe.wait_ge(turned_out, n - 1)
                        for kb in range(blocks[n][0] + 1):
                            last = nc.tensor.transpose(ps_t[n % 2][:, kb * P:(kb + 1) * P],
                                                       prob[:, n % 2, kb * P:(kb + 1) * P], ident[:])
                        last.then_inc(turned, 1)
                    if st >= 2:
                        n = st - 2
                        qb, _, _, values, _ = blocks[n]
                        pe.wait_ge(turned_out, n + 1)
                        if n >= 2:
                            pe.wait_ge(stored, n - 1)
                        for v in range(vtiles):
                            for kb in range(qb + 1):
                                last = nc.tensor.matmul(ps_o[n % 2][:, v * P:(v + 1) * P],
                                                        values[v][:, kb * P:(kb + 1) * P],
                                                        probT[:, n % 2, kb * P:(kb + 1) * P],
                                                        start=(kb == 0), stop=(kb == qb))
                        last.then_inc(valued, 1)

            @block.vector
            def _(dve):
                chain = Chain(dve, inner)
                for st in range(N + 1):
                    if st < N:
                        n = st
                        qb, _, bias, _, _ = blocks[n]
                        w = (qb + 1) * P
                        dve.wait_ge(scored, n + 1)
                        if n >= 2:
                            dve.wait_ge(weighted, n - 1)
                        for m in range(maps):
                            ins = nc.vector.scalar_tensor_tensor(logits[:, n % 2, m, 0:w], ps_s[n % 2][m][:, 0:w],
                                                                 scale, bias[:, T - w:T], ALU.mult, ALU.add)
                            chain(ins)
                        for m in range(maps):
                            ins = nc.vector.tensor_reduce(low[:, n % 2, m:m + 1], logits[:, n % 2, m, 0:w], AX_X,
                                                          ALU.max, negate=True)
                            if m < maps - 1:
                                chain(ins)
                        ins.then_inc(maxed, 1)
                    if st >= 1:
                        n = st - 1
                        w = (blocks[n][0] + 1) * P
                        dve.wait_ge(exped, n + 1)
                        if n >= 2:
                            dve.wait_ge(turned, n - 1)
                        chain(nc.vector.reciprocal(inv[:, n % 2, 0:maps], sums[:, n % 2, 0:maps]))
                        if maps == 1:
                            nc.vector.tensor_scalar(prob[:, n % 2, 0:w], logits[:, n % 2, 0, 0:w],
                                                    inv[:, n % 2, 0:1], None, ALU.mult).then_inc(weighted, 1)
                        else:
                            chain(nc.vector.tensor_scalar(prob[:, n % 2, 0:w], logits[:, n % 2, 0, 0:w],
                                                          inv[:, n % 2, 0:1], None, ALU.mult))
                            chain(nc.vector.tensor_scalar(inv[:, n % 2, 1:2], inv[:, n % 2, 1:2], neglam, None,
                                                          ALU.mult))
                            nc.vector.scalar_tensor_tensor(prob[:, n % 2, 0:w], logits[:, n % 2, 1, 0:w],
                                                           inv[:, n % 2, 1:2], prob[:, n % 2, 0:w], ALU.mult,
                                                           ALU.add).then_inc(weighted, 1)

            @block.scalar
            def _(act):
                for st in range(N + 2):
                    if st < N:
                        n = st
                        w = (blocks[n][0] + 1) * P
                        act.wait_ge(maxed, n + 1)
                        for m in range(maps):
                            ins = nc.scalar.activation(logits[:, n % 2, m, 0:w], logits[:, n % 2, m, 0:w], ACT.Exp,
                                                       bias=low[:, n % 2, m:m + 1],
                                                       accum_out=sums[:, n % 2, m:m + 1])
                        ins.then_inc(exped, 1)
                    if 1 <= st <= N:
                        n = st - 1
                        w = (blocks[n][0] + 1) * P
                        act.wait_ge(turned, n + 1)
                        if n >= 2:
                            act.wait_ge(valued, n - 1)
                        nc.scalar.activation(probT[:, n % 2, 0:w], ps_t[n % 2][:, 0:w], ACT.Copy
                                             ).then_inc(turned_out, 1)
                    if st >= 2:
                        n = st - 2
                        act.wait_ge(valued, n + 1)
                        nc.scalar.activation(blocks[n][4], ps_o[n % 2][:, 0:vtiles * P].rearrange(
                            "p (v q) -> p v q", v=vtiles), ACT.Copy).then_inc(stored, 1)


def turn_values(nc, name, tiles, consts):
    with Scope(nc, name) as s:
        ps = [s.ps(f"t{b}", [P, T]) for b in range(2)]
        turned, stored = s.sem("turned"), s.sem("stored")
        with nc.Block() as block:
            @block.tensor
            def _(pe):
                for n, tile in enumerate(tiles):
                    if n >= 2:
                        pe.wait_ge(stored, n - 1)
                    for tb in range(TB):
                        last = nc.tensor.transpose(ps[n % 2][:, tb * P:(tb + 1) * P], tile[:, tb * P:(tb + 1) * P],
                                                   consts["ident"][:])
                    last.then_inc(turned, 1)

            @block.scalar
            def _(act):
                for n, tile in enumerate(tiles):
                    act.wait_ge(turned, n + 1)
                    nc.scalar.activation(tile, ps[n % 2][:], ACT.Copy).then_inc(stored, 1)


def split_chunks(nc, name, source, act, count):
    with Scope(nc, name) as s:
        hi = s.sem("hi")
        with nc.Block() as block:
            @block.scalar
            def _(a):
                for c in range(count):
                    nc.scalar.activation(act[0][:, c, :], source[:, c, :], ACT.Copy).then_inc(hi, 1)

            @block.vector
            def _(dve):
                for c in range(count):
                    dve.wait_ge(hi, c + 1)
                    nc.vector.tensor_tensor(act[1][:, c, :], source[:, c, :], act[0][:, c, :].bitcast(F32),
                                            ALU.subtract)


def setup(nc, dram, consts, bias, neglam, xT):
    with Scope(nc, "setup") as s:
        relb = s.sb("relb", [33, DA_HEADS])
        relw = s.sb("relw", [33, DA_HEADS, P])
        onehot = s.sb("onehot", [33, BIAS_LEN])
        row = s.sb("row", [P, DA_HEADS, BIAS_LEN])
        prod = s.sb("prod", [P, 2])
        lam = s.sb("lam", [P, 2])
        ps = [s.ps(f"b{h}", [P, T]) for h in range(DA_HEADS)]
        ps_end = s.ps("end", [P, DA_HEADS, P])
        ps_l = s.ps("lam_ps", [P, 2])
        loaded, filled, rel_in, wide, rowed, row_out, skewed, inner, lam_mm, lam_exp, prodd, bias_mm = (
            s.sem(x) for x in ("loaded", "filled", "rel_in", "wide", "rowed", "row_out", "skewed", "inner", "lam_mm",
                               "lam_exp", "prodd", "bias_mm"))
        with nc.Block() as block:
            @block.sync
            def _(sp):
                sp.dma_start(relb[0:32, :], dram["rel_bias"][:, :]).then_inc(rel_in, 16)
                sp.dma_start(onehot[:], dram["onehot"][:, :]).then_inc(rel_in, 16)
                sp.dma_start(consts["gains"][:], dram["gains"][:, :]).then_inc(loaded, 16)
                for c in range(DC):
                    sp.dma_start(xT[:, c, :], dram["xT"][c]).then_inc(loaded, 16)
                for name in ("ident", "perm", "cos", "sin", "mask", "iota"):
                    sp.dma_start(consts[name][:], dram[name][:, :]).then_inc(loaded, 16)
                sp.wait_ge(rowed, DA_HEADS + 1)
                sp.dma_start(dram["skew"].rearrange("h (q n) -> q h n", n=BIAS_LEN), row[:]).then_inc(row_out, 16)
                sp.wait_ge(row_out, 16)
                for h in range(DA_HEADS):
                    src = dram["skew"][h, P - 1:P - 1 + P * (BIAS_LEN - 1)]
                    sp.dma_start(bias[:, h, :], src.rearrange("(q n) -> q n", n=BIAS_LEN - 1)[:, 0:T]
                                 ).then_inc(skewed, 16)
                sp.wait_ge(skewed, 16 * DA_HEADS)
                sp.wait_ge(loaded, 16 * (1 + DC + 6))

            @block.gpsimd
            def _(pool):
                nc.gpsimd.memset(consts["ones"][:], 1.0).then_inc(filled, 1)
                nc.gpsimd.memset(consts["eps"][:], EPS).then_inc(filled, 1)
                pool.wait_ge(filled, 2)
                nc.gpsimd.memset(relb[32:33, :], NEG).then_inc(filled, 1)

            @block.vector
            def _(dve):
                chain = Chain(dve, inner)
                dve.wait_ge(filled, 3)
                dve.wait_ge(rel_in, 32)
                for h in range(DA_HEADS):
                    nc.vector.tensor_copy(relw[:, h, :], relb[:, h:h + 1].to_broadcast([33, P])).then_inc(wide, 1)
                dve.wait_ge(loaded, 16 * (1 + DC + 6))
                g = consts["gains"]
                for k in range(2):
                    nc.vector.tensor_tensor(prod[:, k:k + 1], g[:, G_LAM + 2 * k:G_LAM + 2 * k + 1],
                                            g[:, G_LAM + 2 * k + 1:G_LAM + 2 * k + 2], ALU.mult).then_inc(prodd, 1)
                chain(nc.vector.tensor_scalar(g[:, G_DAOUT:G_DAOUT + 2], g[:, G_DAOUT:G_DAOUT + 2], 1.0 - LAM_INIT,
                                              None, ALU.mult))
                dve.wait_ge(lam_exp, 1)
                chain(nc.vector.tensor_tensor(neglam[:], lam[:, 1:2], lam[:, 0:1], ALU.subtract))
                chain(nc.vector.tensor_scalar(neglam[:], neglam[:], -LAM_INIT, None, ALU.add))

            @block.tensor
            def _(pe):
                pe.wait_ge(wide, DA_HEADS)
                for h in range(DA_HEADS):
                    nc.tensor.matmul(ps[h][:], relw[:, h, :], onehot[:, 0:T], start=True, stop=True
                                     ).then_inc(bias_mm, 1)
                for h in range(DA_HEADS):
                    last = nc.tensor.matmul(ps_end[:, h, :], relw[:, h, :], onehot[:, T:BIAS_LEN], start=True,
                                            stop=True)
                last.then_inc(bias_mm, 1)
                pe.wait_ge(prodd, 2)
                nc.tensor.matmul(ps_l[:], consts["ones"][:], prod[:], start=True, stop=True).then_inc(lam_mm, 1)

            @block.scalar
            def _(act):
                for h in range(DA_HEADS):
                    act.wait_ge(bias_mm, h + 1)
                    nc.scalar.activation(row[:, h, 0:T], ps[h][:], ACT.Copy).then_inc(rowed, 1)
                act.wait_ge(bias_mm, DA_HEADS + 1)
                nc.scalar.activation(row[:, :, T:BIAS_LEN], ps_end[:], ACT.Copy).then_inc(rowed, 1)
                act.wait_ge(lam_mm, 1)
                nc.scalar.activation(lam[:], ps_l[:], ACT.Exp).then_inc(lam_exp, 1)


def rotate(nc, name, tiles, consts):
    with Scope(nc, name) as s:
        turned = s.sb("turned", [P, 2, T])
        ps = [s.ps(f"p{b}", [P, T]) for b in range(2)]
        swapped, used, inner = s.sem("swapped"), s.sem("used"), s.sem("inner")
        with nc.Block() as block:
            @block.tensor
            def _(pe):
                for n, tile in enumerate(tiles):
                    if n >= 2:
                        pe.wait_ge(used, n - 1)
                    nc.tensor.matmul(ps[n % 2][:], consts["perm"][:], tile, start=True, stop=True
                                     ).then_inc(swapped, 1)

            @block.vector
            def _(dve):
                chain = Chain(dve, inner)
                for n, tile in enumerate(tiles):
                    dve.wait_ge(swapped, n + 1)
                    nc.vector.tensor_tensor(turned[:, n % 2, :], ps[n % 2][:], consts["sin"][:], ALU.mult
                                            ).then_inc(used, 1)
                    chain(nc.vector.tensor_tensor(tile, tile, consts["cos"][:], ALU.mult))
                    dve.wait_ge(used, n + 1)
                    chain(nc.vector.tensor_tensor(tile, tile, turned[:, n % 2, :], ALU.add))


def gate_sigmoids(nc, proj):
    with Scope(nc, "sig") as s:
        with nc.Block() as block:
            @block.scalar
            def _(act):
                for n in range(GATES, IN_TILES, 4):
                    nc.scalar.activation(proj[:, n:n + 4, :], proj[:, n:n + 4, :], ACT.Sigmoid)


def merge(nc, name, ya, gate, out, add):
    with Scope(nc, name) as s:
        done = s.sem("done")
        with nc.Block() as block:
            @block.vector
            def _(dve):
                for c in range(DC):
                    nc.vector.tensor_tensor(ya[:, c, :] if add else out[:, c, :], ya[:, c, :], gate[:, c, :], ALU.mult
                                            ).then_inc(done, 1)
                if add:
                    for c in range(DC):
                        dve.wait_ge(done, c + 1)
                        nc.vector.tensor_tensor(out[:, c, :], out[:, c, :], ya[:, c, :], ALU.add)


def add_chunks(nc, name, out, more):
    with nc.Block() as block:
        @block.vector
        def _(dve):
            for c in range(DC):
                nc.vector.tensor_tensor(out[:, c, :], out[:, c, :], more[:, c, :], ALU.add)


CHUNK = 32
JG = 4


def first_layer(nc, query, dram, consts, act, spilled, gates):
    H, K = PEER_HEADS, TOPK
    QUAD = 4
    ROUTE_J, PAIR_J = 12, 8
    STEPS = P // (2 * CHUNK)
    BLOCK_J = ROUTE_J + STEPS * PAIR_J
    EXP_J = 8
    QUADS_J = 2 * CHUNK // QUAD // PAIR_J
    assert TB * BLOCK_J <= KEYS and ROUTE_J % 4 == 0
    with Scope(nc, "fl") as s:
        u_raw = s.sb("u_raw", [P, 4, D])
        u = [[s.sb(f"u{b}{h}", [P, D], F32R) for h in range(2)] for b in range(2)]
        gel = s.sb("gel", [P, 2, T])
        keys = s.sb("keys", [P, 2 * H, KEYS])
        score = s.sb("score", [P, 2 * H, KEYS])
        top = s.sb("top", [P, 2 * H, K])
        top_i = s.sb("top_i", [P, 2 * H, K], U32)
        top_f = s.sb("top_f", [P, 2 * H, K])
        cand = s.sb("cand", [P, H, K, K])
        best = s.sb("best", [P, H, K])
        pos = s.sb("pos", [P, H, K], U32)
        half_i = s.sb("half_i", [P, 2, H, K], U32)
        half_f = s.sb("half_f", [P, 2, H, K])
        hit = s.sb("hit", [P, H, K, K])
        pick = s.sb("pick", [P, 3, H, K])
        gsum = s.sb("gsum", [P, H])
        pickT = s.sb("pickT", [P, 3, P])
        row_i = s.sb("row_i", [P, 2, QUAD, KEYS])
        row_j = s.sb("row_j", [P, 2, QUAD, KEYS])
        grid = s.sb("grid", [P, 2, KEYS, CHUNK])
        ps_a = [s.ps(f"a{b}", [P, T]) for b in range(2)]
        ps_r = [s.ps(f"r{q}", [P, 4, KEYS]) for q in range(4)]
        ps_g = [s.ps(f"g{b}", [P, QUAD, KEYS]) for b in range(2)]
        u_in = [s.sem(f"u_in{r}") for r in range(4)]
        spill_out = [s.sem(f"spill_out{b}") for b in range(2)]
        grid_out = [s.sem(f"grid_out{b}") for b in range(2)]
        u_hi, u_lo, a_done, gelued, opened = (s.sem(x) for x in ("u_hi", "u_lo", "a_done", "gelued", "opened"))
        keys_in, scored, score_out, inner, shifted, exped, picked, turned, pick_out = (
            s.sem(x) for x in ("keys_in", "scored", "score_out", "inner", "shifted", "exped", "picked", "turned",
                               "pick_out"))
        rows_i, rows_j, quad_done, quad_out = (s.sem(x) for x in ("rows_i", "rows_j", "quad_done", "quad_out"))
        iota = consts["iota"]
        QB = P // QUAD

        def schedule(eng, one_j, one_quad, before, exps, after, chunk_end):
            for tb in range(TB):
                n0 = tb * BLOCK_J
                before(tb)
                for n in range(n0, n0 + ROUTE_J):
                    if n == n0 + EXP_J:
                        exps(tb)
                    one_j(n, n % 4, n // 4)
                after(tb)
                with eng.Fori(0, STEPS) as i:
                    for k in range(PAIR_J):
                        one_j(i * PAIR_J + (n0 + ROUTE_J + k), k % 4, i * (PAIR_J // 4) + (n0 + ROUTE_J + k) // 4)
                        for m in range(QUADS_J):
                            q = k * QUADS_J + m
                            one_quad(tb, i * (2 * CHUNK // QUAD) + q, q)
                        if k % (PAIR_J // 2) == PAIR_J // 2 - 1:
                            chunk_end(tb, i * 2 + (tb * P // CHUNK + k // (PAIR_J // 2)), k // (PAIR_J // 2))
            each(eng, TB * BLOCK_J, KEYS - 4, 4, one_j)
            for n in range(KEYS - 4, KEYS):
                one_j(n, n % 4, n // 4)

        def nothing(*_):
            pass

        with nc.Block() as block:
            @block.sync
            def _(sp):
                sp.dma_start(keys[:], dram["keys"].rearrange("p (g n) -> p g n", n=KEYS)).then_inc(keys_in, 16)

                def load(n, r):
                    sp.wait_ge(u_lo, n + 1)
                    sp.wait_ge(opened, 1)
                    sp.dma_start(u_raw[:, r, :], dram["u"][bass.ds(n, 1)].rearrange("o p f -> p (o f)")
                                 ).then_inc(u_in[r], 16)

                def store(n, r):
                    sp.wait_ge(gelued, n + 3)
                    sp.wait_ge(opened, 1)
                    sp.dma_start(spilled[bass.ds(n, 1)].rearrange("o p f -> p (o f)"), gel[:, r % 2, :]
                                 ).then_inc(spill_out[r % 2], 16)

                def one_j(n, r, lap):
                    store(n, r)
                    if isinstance(n, int) and n + 4 >= KEYS:
                        return
                    load(n + 4, r)

                def store_chunk(tb, chunk, slot):
                    sp.wait_ge(quad_out, chunk * (CHUNK // QUAD) + (CHUNK // QUAD + 2))
                    sp.wait_ge(opened, 1)
                    sp.dma_start(gates.rearrange("g i c f -> c i g f")[bass.ds(chunk, 1)].rearrange(
                        "o i g f -> i (o g) f"),
                        grid[:, slot].rearrange("p (g j) t -> p g (j t)", j=JG)).then_inc(grid_out[slot], 16)

                for n in range(4):
                    load(n, n)
                for tb in range(TB):
                    n0 = tb * BLOCK_J
                    for n in range(n0, n0 + ROUTE_J):
                        one_j(n, n % 4, n // 4)
                    with sp.Fori(0, STEPS) as i:
                        for k in range(PAIR_J):
                            one_j(i * PAIR_J + (n0 + ROUTE_J + k), k % 4, None)
                            if k % (PAIR_J // 2) == PAIR_J // 2 - 1:
                                store_chunk(tb, i * 2 + (tb * P // CHUNK + k // (PAIR_J // 2)), k // (PAIR_J // 2))
                for n in range(TB * BLOCK_J, KEYS):
                    one_j(n, n % 4, None)
                for b in range(2):
                    sp.wait_ge(spill_out[b], 16 * KEYS // 2 + 16)
                    sp.wait_ge(grid_out[b], 16 * (T // CHUNK // 2) + 16)

            @block.gpsimd
            def _(pool):
                for count, free in ((u_lo, 4), (a_done, 2), (gelued, 2), (quad_done, 2), (quad_out, 2)):
                    pool.sem_inc(count, free)
                for b in range(2):
                    pool.sem_inc(spill_out[b], 16)
                    pool.sem_inc(grid_out[b], 16)
                pool.sem_inc(opened, 1)

                def rest(n, r, lap):
                    pool.wait_ge(u_hi, n + 1)
                    nc.gpsimd.tensor_tensor(u[r % 2][1][:], u_raw[:, r, :], u[r % 2][0][:].bitcast(F32), ALU.subtract
                                            ).then_inc(u_lo, 1)
                each(pool, 0, KEYS, 4, rest)

            @block.tensor
            def _(pe):
                def one_j(n, r, lap):
                    b = r % 2
                    pe.wait_ge(u_lo, n + 5)
                    pe.wait_ge(gelued, n + 1)
                    for c in range(DC):
                        for k, (x, y) in enumerate(PASSES):
                            last = nc.tensor.matmul(ps_a[b][:], u[b][x][:, c * P:(c + 1) * P], act[y][:, c, :],
                                                    start=(c == 0 and k == 0), stop=(c == DC - 1 and k == 2))
                    last.then_inc(a_done, 1)

                def one_quad(tb, quad, q):
                    pe.wait_ge(rows_i, quad + (tb * QB + 1))
                    pe.wait_ge(rows_j, quad + (tb * QB + 1))
                    pe.wait_ge(quad_out, quad + (tb * QB + 1))
                    for t in range(QUAD):
                        last = nc.tensor.matmul(ps_g[q % 2][:, t, :], row_i[:, q % 2, t, :], row_j[:, q % 2, t, :],
                                                start=True, stop=True)
                    last.then_inc(quad_done, 1)

                def scores(tb):
                    if tb == 0:
                        pe.wait_ge(keys_in, 16)
                    if tb >= 1:
                        pe.wait_ge(pick_out, tb)
                    for g in range(2 * H):
                        last = nc.tensor.matmul(ps_r[g // 4][:, g % 4, :], query[:, g, tb * P:(tb + 1) * P],
                                                keys[:, g, :], start=True, stop=True)
                    last.then_inc(scored, 1)

                def turn_picks(tb):
                    pe.wait_ge(picked, tb + 1)
                    for k in range(3):
                        last = nc.tensor.transpose(ps_r[0][:, k, :], pick[:, k, :, :].rearrange("p h k -> p (h k)"),
                                                   consts["ident"][:])
                    last.then_inc(turned, 1)

                schedule(pe, one_j, one_quad, scores, nothing, turn_picks, nothing)

            @block.scalar
            def _(a):
                def round_u(n, r, lap):
                    a.wait_ge(u_in[r], lap * 16 + 16)
                    nc.scalar.activation(u[r % 2][0][:], u_raw[:, r, :], ACT.Copy).then_inc(u_hi, 1)

                def one_j(n, r, lap):
                    a.wait_ge(a_done, n + 3)
                    a.wait_ge(spill_out[r % 2], lap * 32 + (16 * (r // 2) + 16))
                    nc.scalar.activation(gel[:, r % 2, :], ps_a[r % 2][:], ACT.Gelu).then_inc(gelued, 1)
                    if isinstance(n, int) and n + 2 >= KEYS:
                        return
                    round_u(n + 2, (r + 2) % 4, lap + (r + 2) // 4)

                def one_quad(tb, quad, q):
                    slot, place = q // (CHUNK // QUAD), q % (CHUNK // QUAD)
                    if place == 0:
                        assert 2 * CHUNK // QUAD == 16
                        a.wait_ge(grid_out[slot], quad + (16 - q + tb * STEPS * 16))
                    a.wait_ge(quad_done, quad + (tb * QB + 3))
                    nc.scalar.activation(grid[:, slot, :, place * QUAD:(place + 1) * QUAD].rearrange("p j t -> p t j"),
                                         ps_g[q % 2][:], ACT.Copy).then_inc(quad_out, 1)

                def evacuate(tb):
                    a.wait_ge(scored, tb + 1)
                    if tb >= 1:
                        a.wait_ge(picked, tb)
                    for q in range(4):
                        last = nc.scalar.activation(score[:, 4 * q:4 * q + 4, :], ps_r[q][:], ACT.Copy)
                    last.then_inc(score_out, 1)

                def exps(tb):
                    a.wait_ge(shifted, tb + 1)
                    nc.scalar.activation(pick[:, 2, :, :], pick[:, 2, :, :], ACT.Exp).then_inc(exped, 1)

                def store_picks(tb):
                    a.wait_ge(turned, tb + 1)
                    if tb >= 1:
                        a.wait_ge(rows_i, tb * QB)
                        a.wait_ge(rows_j, tb * QB)
                    nc.scalar.activation(pickT[:], ps_r[0][:, 0:3, :], ACT.Copy).then_inc(pick_out, 1)

                for n in range(2):
                    round_u(n, n, 0)
                schedule(a, one_j, one_quad, evacuate, exps, store_picks, nothing)

            @block.vector
            def _(dve):
                count = [0]

                def done(ins):
                    count[0] += 1
                    ins.then_inc(inner, 1)

                def sync():
                    dve.wait_ge(inner, count[0])

                def top16(rows, values, indices):
                    for st in range(5):
                        for r, row in enumerate(rows):
                            lo, hi = values[r][:, 0:8], values[r][:, 8:16]
                            if st == 0:
                                done(nc.vector.max(lo, row))
                            elif st == 1:
                                done(nc.vector.max_index(indices[r][:, 0:8], lo, row))
                            elif st == 2:
                                done(nc.vector.match_replace(row, lo, row, -3e38))
                            elif st == 3:
                                done(nc.vector.max(hi, row))
                            else:
                                done(nc.vector.max_index(indices[r][:, 8:16], hi, row))
                        sync()

                def route(tb):
                    dve.wait_ge(score_out, tb + 1)
                    top16([score[:, g, :] for g in range(2 * H)], [top[:, g, :] for g in range(2 * H)],
                          [top_i[:, g, :] for g in range(2 * H)])
                    done(nc.vector.tensor_copy(top_f[:], top_i[:]))
                    pair = top[:].rearrange("p (h c) k -> p h c k", c=2)
                    done(nc.vector.tensor_tensor(cand[:], pair[:, :, 0, :].unsqueeze(3).to_broadcast([P, H, K, K]),
                                                 pair[:, :, 1, :].unsqueeze(2).to_broadcast([P, H, K, K]), ALU.add))
                    sync()
                    top16([cand[:, h, :, :].rearrange("p a b -> p (a b)") for h in range(H)],
                          [best[:, h, :] for h in range(H)], [pos[:, h, :] for h in range(H)])
                    done(nc.vector.tensor_scalar(half_i[:, 0], pos[:], 4, None, ALU.logical_shift_right))
                    done(nc.vector.tensor_scalar(half_i[:, 1], pos[:], 15, None, ALU.bitwise_and))
                    if tb >= 1:
                        dve.wait_ge(turned, tb)
                    nc.vector.tensor_tensor(pick[:, 2], best[:], best[:, :, 0:1].to_broadcast([P, H, K]),
                                            ALU.subtract).then_inc(shifted, 1)
                    sync()
                    done(nc.vector.tensor_copy(half_f[:], half_i[:]))
                    sync()
                    pair_i = top_f[:].rearrange("p (h c) k -> p h c k", c=2)
                    for c in range(2):
                        done(nc.vector.tensor_tensor(
                            hit[:], half_f[:, c].unsqueeze(3).to_broadcast([P, H, K, K]),
                            iota[:, 0:K].unsqueeze(1).unsqueeze(1).to_broadcast([P, H, K, K]), ALU.is_equal))
                        sync()
                        done(nc.vector.tensor_tensor(hit[:], hit[:],
                                                     pair_i[:, :, c, :].unsqueeze(2).to_broadcast([P, H, K, K]),
                                                     ALU.mult))
                        sync()
                        done(nc.vector.tensor_reduce(pick[:, c], hit[:], AX_X, ALU.add))
                        sync()
                    dve.wait_ge(exped, tb + 1)
                    done(nc.vector.tensor_reduce(gsum[:], pick[:, 2], AX_X, ALU.add))
                    sync()
                    done(nc.vector.reciprocal(gsum[:], gsum[:]))
                    sync()
                    nc.vector.tensor_tensor(pick[:, 2], pick[:, 2], gsum[:].unsqueeze(2).to_broadcast([P, H, K]),
                                            ALU.mult).then_inc(picked, 1)

                for tb in range(TB):
                    route(tb)
                    dve.wait_ge(pick_out, tb + 1)
                    with dve.Fori(0, QB // 2) as i:
                        for b in range(2):
                            dve.wait_ge(quad_done, i * 2 + (tb * QB + b + 1))
                            for t in range(QUAD):
                                tok = bass.ds(i * (2 * QUAD) + (b * QUAD + t), 1)
                                x = nc.vector.tensor_scalar(row_i[:, b, t, :], iota[:], pickT[:, 0, tok], None,
                                                            ALU.is_equal)
                                y = nc.vector.tensor_scalar(row_j[:, b, t, :], iota[:], pickT[:, 1, tok],
                                                            pickT[:, 2, tok], ALU.is_equal, ALU.mult)
                            x.then_inc(rows_i, 1)
                            y.then_inc(rows_j, 1)


def second_layer(nc, dram, spilled, gates, total, out):
    U = 2 * JG
    with Scope(nc, "sl") as s:
        v_raw = s.sb("v_raw", [P, 4, D])
        v = [[s.sb(f"v{b}{h}", [P, D], F32R) for h in range(2)] for b in range(2)]
        gel = s.sb("gel", [P, 4, T])
        g_in = s.sb("g_in", [P, 2, T // CHUNK, JG, CHUNK])
        weighted = s.sb("weighted", [P, 2, T])
        w = [[s.sb(f"w{b}{h}", [P, T], F32R) for h in range(2)] for b in range(2)]
        ps = [s.ps(f"o{c}", [P, T]) for c in range(DC)]
        v_in = [s.sem(f"v_in{r}") for r in range(4)]
        gel_in = [s.sem(f"gel_in{r}") for r in range(4)]
        gate_in = [s.sem(f"gate_in{b}") for b in range(2)]
        v_hi, v_lo, w_done, w_hi, w_lo, b_done, opened, added, stored = (
            s.sem(x) for x in ("v_hi", "v_lo", "w_done", "w_hi", "w_lo", "b_done", "opened", "added", "stored"))
        with nc.Block() as block:
            @block.sync
            def _(sp):
                def load(buffer, source, n, free, count, landed):
                    sp.wait_ge(free, count)
                    sp.wait_ge(opened, 1)
                    sp.dma_start(buffer, source[bass.ds(n, 1)].rearrange("o p f -> p (o f)")).then_inc(landed, 16)

                with sp.Fori(0, KEYS // U) as i:
                    for k in range(U):
                        n = sp.snap(i * U + k)
                        if k % JG == 0:
                            grp = sp.snap(i * 2 + k // JG)
                            load(g_in[:, k // JG].rearrange("p c j t -> p (c j t)"),
                                 gates.rearrange("g i c f -> g i (c f)"), grp, w_done, n + 1, gate_in[k // JG])
                        load(gel[:, k % 4, :], spilled, n, w_done, n + (U - 4 + 1), gel_in[k % 4])
                        load(v_raw[:, k % 4, :], dram["v"], n, v_lo, n + 1, v_in[k % 4])
                for c in range(DC):
                    sp.wait_ge(added, c + 1)
                    sp.dma_start(out[c], total[:, c, :]).then_inc(stored, 16)
                sp.wait_ge(stored, 16 * DC)

            @block.scalar
            def _(a):
                a.sem_inc(b_done, 2)

                def one_j(n, k, lap):
                    a.wait_ge(v_in[k % 4], lap * 32 + (16 * (k // 4) + 16))
                    a.wait_ge(b_done, n + 1)
                    nc.scalar.activation(v[k % 2][0][:], v_raw[:, k % 4, :], ACT.Copy).then_inc(v_hi, 1)
                    a.wait_ge(w_done, n + (U + 1))
                    nc.scalar.activation(w[k % 2][0][:], weighted[:, k % 2, :], ACT.Copy).then_inc(w_hi, 1)
                each(a, 0, KEYS, U, one_j)

            @block.vector
            def _(dve):
                dve.sem_inc(w_done, U)
                dve.sem_inc(v_lo, 4)
                dve.sem_inc(opened, 1)
                dve.sem_inc(w_lo, 2)

                def weigh(n, k, lap):
                    dve.wait_ge(gel_in[k % 4], lap * 32 + (16 * (k // 4) + 16))
                    dve.wait_ge(gate_in[k // JG], lap * 16 + 16)
                    dve.wait_ge(w_lo, n + 1)
                    nc.vector.tensor_tensor(
                        weighted[:, k % 2, :].rearrange("p (c t) -> p c t", t=CHUNK),
                        gel[:, k % 4, :].rearrange("p (c t) -> p c t", t=CHUNK), g_in[:, k // JG, :, k % JG, :],
                        ALU.mult).then_inc(w_done, 1)

                def one_j(n, k, lap):
                    dve.wait_ge(v_hi, n + 1)
                    nc.vector.tensor_tensor(v[k % 2][1][:], v_raw[:, k % 4, :], v[k % 2][0][:].bitcast(F32),
                                            ALU.subtract).then_inc(v_lo, 1)
                    dve.wait_ge(w_hi, n + 1)
                    nc.vector.tensor_tensor(w[k % 2][1][:], weighted[:, k % 2, :], w[k % 2][0][:].bitcast(F32),
                                            ALU.subtract).then_inc(w_lo, 1)

                def body(n, k, lap):
                    one_j(n, k, lap)
                    weigh(n + 2, (k + 2) % U, lap + (k + 2) // U)

                weigh(0, 0, 0)
                weigh(1, 1, 0)
                each(dve, 0, KEYS - 2, U, body)
                for n in range(KEYS - 2, KEYS):
                    one_j(n, n % U, n // U)
                for c in range(DC):
                    dve.wait_ge(b_done, KEYS + 2)
                    nc.vector.tensor_tensor(total[:, c, :], total[:, c, :], ps[c][:], ALU.add).then_inc(added, 1)

            @block.tensor
            def _(pe):
                def one_j(n, k, lap):
                    pe.wait_ge(v_lo, n + 5)
                    pe.wait_ge(w_lo, n + 3)
                    for c in range(DC):
                        for p, (x, y) in enumerate(PASSES):
                            last = nc.tensor.matmul(ps[c][:], v[k % 2][x][:, c * P:(c + 1) * P], w[k % 2][y][:],
                                                    start=(isinstance(n, int) and n == 0 and p == 0),
                                                    stop=(isinstance(n, int) and n == KEYS - 1 and p == 2))
                    last.then_inc(b_done, 1)

                for n in range(U):
                    one_j(n, n, 0)
                each(pe, U, KEYS - U, U, one_j)
                for n in range(KEYS - U, KEYS):
                    one_j(n, n % U, n // U)


def program(nc, dram, out):
    USED_SEMAPHORES.clear()
    dram["skew"] = nc.dram_tensor("skew", [DA_HEADS, P * BIAS_LEN], F32).ap()
    gates = nc.dram_tensor("gates", [KEYS // JG, P, T // CHUNK, JG * CHUNK], F32).ap()
    spilled = nc.dram_tensor("spilled", [KEYS, P, T], F32).ap()
    with Scope(nc, "all") as s:
        consts = {"ones": s.sb("ones", [P, P]), "eps": s.sb("eps", [P, 1]), "ident": s.sb("ident", [P, P]),
                  "iota": s.sb("iota", [P, KEYS]), "gains": s.sb("gains", [P, G_COLS])}
        neglam = s.sb("neglam", [P, 1])
        xT = s.sb("xT", [P, DC, T])
        act = [s.sb(f"act{h}", [P, DC, T], F32R) for h in range(2)]
        gain = lambda k: consts["gains"][:, k:k + 1]
        with Scope(nc, "mix") as m:
            proj = m.sb("proj", [P, IN_TILES, T])
            consts.update(perm=m.sb("perm", [P, P]), cos=m.sb("cos", [P, T]), sin=m.sb("sin", [P, T]),
                          mask=m.sb("mask", [P, T]))
            bias = m.sb("bias", [P, DA_HEADS, T])
            setup(nc, dram, consts, bias, neglam, xT)
            rms_norms(nc, "n_x", [(D, [(xT[:, c, :], None) for c in range(DC)],
                                   [(xT[:, c, :], gain(G_ATTN + c), c) for c in range(DC)])], consts, act)
            project(nc, "p_in", dram["w_in"], DC, IN_TILES, act, 0, proj, 0, slots=4)
            gate_sigmoids(nc, proj)
            tile = lambda n: proj[:, n, :]
            rms_norms(nc, "n_qk", [(DA_DIM, [(tile(n), None)], [(tile(n), gain(G_DAQ if n < KA else G_DAK), tile(n))])
                                   for n in range(QA, VA)], consts)
            turn_values(nc, "tv_a", [tile(n) for n in range(VA, CQ)], consts)
            extra = m.sb("extra", [P, 12, T])
            blocks = []
            for h in range(DA_HEADS):
                for qb in range(TB):
                    blocks.append((qb, [[(tile(QA + 2 * h + k), tile(KA + 2 * h + k))] for k in range(2)],
                                   bias[:, h, :], [tile(VA + 2 * h + k) for k in range(2)],
                                   extra[:, 2 * h:2 * h + 2, qb * P:(qb + 1) * P]))
            attention(nc, "da", blocks, consts, DA_DIM ** -0.5, 2, 2, neglam[:, 0:1])
            rms_norms(nc, "n_ya", [(DA_V, [(extra[:, 2 * h + k, :], None) for k in range(2)],
                                    [(extra[:, 2 * h + k, :], gain(G_DAOUT + k), 2 * h + k) for k in range(2)])
                                   for h in range(DA_HEADS)], consts, act)
            project(nc, "p_da", dram["w_da"], DC, DC, act, 0, extra, 0)
            merged = proj[:, 0:DC, :]
            merge(nc, "m_a", extra, proj[:, GATES:GATES + DC, :], merged, False)
            rms_norms(nc, "n_lat",
                      [(Q_RANK, [(tile(CQ + c), None) for c in range(3)],
                        [(tile(CQ + c), gain(G_QLAT + c), c) for c in range(3)]),
                       (KV_RANK, [(tile(CKV + c), None) for c in range(2)],
                        [(tile(CKV + c), gain(G_KVLAT + c), 3 + c) for c in range(2)])], consts, act)
            project(nc, "p_uq", dram["w_uq"], Q_RANK // P, 12, act, 0, extra, 0)
            project(nc, "p_ukv", dram["w_ukv"], KV_RANK // P, 16, act, 3, proj, 8)
            qn = lambda h: extra[:, h, :]
            qr = lambda h: extra[ROPE * (h % 2):ROPE * (h % 2) + ROPE, 8 + h // 2, :]
            kn = lambda h: proj[:, 8 + h, :]
            kr = lambda h: proj[ROPE * (h % 2):ROPE * (h % 2) + ROPE, KR, :]
            kr_out = lambda h: proj[ROPE * (h % 2):ROPE * (h % 2) + ROPE, CQ + h // 2, :]
            g_of = lambda k, h: consts["gains"][ROPE * (h % 2):ROPE * (h % 2) + ROPE, k:k + 1]
            rotate(nc, "rot", [extra[:, 8 + n, :] for n in range(4)] + [tile(KR)], consts)
            rms_norms(nc, "n_mq",
                      [(NOPE + ROPE, [(qn(h), None), (qr(h), None)],
                        [(qn(h), gain(G_MQN), qn(h)), (qr(h), g_of(G_MQR, h), qr(h))]) for h in range(MLA_HEADS)] +
                      [(NOPE + ROPE, [(kn(h), None), (kr(h), None)],
                        [(kn(h), gain(G_MKN), kn(h)), (kr(h), g_of(G_MKR, h), kr_out(h))]) for h in range(MLA_HEADS)],
                      consts)
            turn_values(nc, "tv_b", [proj[:, 16 + h, :] for h in range(MLA_HEADS)], consts)
            blocks = []
            for h in range(MLA_HEADS):
                for qb in range(TB):
                    blocks.append((qb, [[(qn(h), kn(h)), (qr(h), kr_out(h))]], consts["mask"][:],
                                   [proj[:, 16 + h, :]], extra[:, h:h + 1, qb * P:(qb + 1) * P]))
            attention(nc, "mla", blocks, consts, (NOPE + ROPE) ** -0.5, 1, 1)
            split_chunks(nc, "s_yb", extra, act, DC)
            project(nc, "p_mla", dram["w_mla"], DC, DC, act, 0, extra, 0)
            merge(nc, "m_b", extra, proj[:, GATES + DC:GATES + 2 * DC, :], merged, True)
            split_chunks(nc, "s_m", merged, act, DC)
            project(nc, "p_out", dram["w_out"], DC, DC, act, 0, extra, 0)
            add_chunks(nc, "x2", xT, extra)
        recycle_semaphores(nc)
        with Scope(nc, "peer") as m:
            query = m.sb("query", [P, 2 * PEER_HEADS, T])
            rms_norms(nc, "n_x2", [(D, [(xT[:, c, :], None) for c in range(DC)],
                                    [(xT[:, c, :], gain(G_FFN + c), c) for c in range(DC)])], consts, act)
            project(nc, "p_q", dram["w_query"], DC, 2 * PEER_HEADS, act, 0, query, 0, slots=4)
            first_layer(nc, query, dram, consts, act, spilled, gates)
        second_layer(nc, dram, spilled, gates, xT, out)


def shape_constants():
    import numpy as np
    c = {"ident": np.eye(P, dtype=np.float32)}
    c["iota"] = np.tile(np.arange(KEYS, dtype=np.float32), (P, 1))
    f = np.arange(P) % (ROPE // 2)
    inv = np.float32(10000.0) ** (-(2 * f).astype(np.float32) / np.float32(ROPE))
    ang = inv[:, None] * np.arange(T, dtype=np.float32)[None, :]
    first = (np.arange(P) % ROPE) < ROPE // 2
    c["cos"] = np.cos(ang).astype(np.float32)
    c["sin"] = (np.sin(ang) * np.where(first, -1.0, 1.0)[:, None]).astype(np.float32)
    perm = np.zeros((P, P), np.float32)
    for m in range(P):
        perm[m + ROPE // 2 if first[m] else m - ROPE // 2, m] = 1.0
    c["perm"] = perm
    q, n = np.arange(P)[:, None], np.arange(T)[None, :]
    c["mask"] = np.where(T - P + q - n >= 0, 0.0, NEG).astype(np.float32)
    dist = T - 1 - np.arange(BIAS_LEN)
    nf = np.maximum(dist, 16).astype(np.float32)
    large = 16 + (np.log(nf / 16) / np.log(8.0) * 16).astype(np.int32)
    bucket = np.where(dist < 16, np.maximum(dist, 0), np.minimum(large, 31))
    onehot = np.zeros((33, BIAS_LEN), np.float32)
    onehot[np.where(dist >= 0, bucket, 32), np.arange(BIAS_LEN)] = 1.0
    c["onehot"] = onehot
    return c


def kernel(**inputs):
    import numpy as np
    import concourse.bacc as bacc
    from concourse.bass_utils import run_bass_kernel_spmd

    a = {k: np.asarray(v) for k, v in inputs.items()}

    def tiles(w):
        k, n = w.shape
        return np.ascontiguousarray(w.reshape(k // P, P, n // P, P).transpose(2, 1, 0, 3)).reshape(n // P, P, k)

    def cols(v):
        return v.reshape(-1, P).T

    w_in = a["w_in"][0]
    kr0 = (CKV + 2) * P
    uq = a["mla_w_uq"][0].reshape(Q_RANK, MLA_HEADS, NOPE + ROPE)
    ukv = a["mla_w_ukv"][0].reshape(KV_RANK, MLA_HEADS, NOPE + MLA_V)
    qn, kn = a["mla_q_norm"][0], a["mla_k_norm"][0]
    data = {
        "xT": np.ascontiguousarray(a["x"][0].T).reshape(DC, P, T),
        "w_in": tiles(np.concatenate([w_in[:, :kr0 + ROPE], w_in[:, kr0:kr0 + ROPE], w_in[:, kr0 + ROPE:]], axis=1)),
        "w_da": tiles(a["da_proj"][0]),
        "w_uq": tiles(np.concatenate([uq[:, :, :NOPE].reshape(Q_RANK, -1), uq[:, :, NOPE:].reshape(Q_RANK, -1)], axis=1)),
        "w_ukv": tiles(np.concatenate([ukv[:, :, :NOPE].reshape(KV_RANK, -1), ukv[:, :, NOPE:].reshape(KV_RANK, -1)],
                                      axis=1)),
        "w_mla": tiles(a["mla_proj"][0]),
        "w_out": tiles(a["w_out"][0]),
        "w_query": tiles(a["peer_w_query"][0]),
        "rel_bias": a["rel_bias"],
        "keys": np.ascontiguousarray(a["peer_sub_keys"][0].reshape(2 * PEER_HEADS, KEYS, P).transpose(2, 0, 1)
                                     ).reshape(P, 2 * PEER_HEADS * KEYS),
        "u": np.ascontiguousarray(a["peer_u"][0].reshape(KEYS, KEYS, DC, P).transpose(1, 3, 2, 0)).reshape(KEYS, P, D),
        "v": np.ascontiguousarray(a["peer_v"][0].reshape(KEYS, KEYS, D).transpose(1, 0, 2)),
        "gains": np.ascontiguousarray(np.concatenate(
            [cols(a["attn_norm"][0]), cols(a["ffn_norm"][0]), cols(a["da_q_norm"][0]), cols(a["da_k_norm"][0]),
             cols(a["da_out_norm"][0]), cols(a["mla_q_latent_norm"][0]), cols(a["mla_kv_latent_norm"][0]),
             cols(qn[:NOPE]), cols(np.concatenate([qn[NOPE:], qn[NOPE:]])),
             cols(kn[:NOPE]), cols(np.concatenate([kn[NOPE:], kn[NOPE:]])),
             cols(a["da_lambda_q1"][0]), cols(a["da_lambda_k1"][0]), cols(a["da_lambda_q2"][0]),
             cols(a["da_lambda_k2"][0])], axis=1)),
    }
    data.update(shape_constants())
    nc = bacc.Bacc("TRN2", target_bir_lowering=False, num_devices=1)
    arrays, dram = {}, {}
    for name, x in data.items():
        arrays[f"in_{name}"] = x
        dram[name] = nc.dram_tensor(f"in_{name}", x.shape, F32, kind="ExternalInput").ap()
    out = nc.dram_tensor("out_T", (DC, P, T), F32, kind="ExternalOutput").ap()
    program(nc, dram, out)
    r = run_bass_kernel_spmd(nc, [arrays], core_ids=[0])
    return np.ascontiguousarray(r.results[0]["out_T"].reshape(D, T).T)[None]
```

```python
from contextlib import ExitStack

import concourse.bass as bass
from concourse import mybir

F32 = mybir.dt.float32
F32R = mybir.dt.float32r
BF16 = mybir.dt.bfloat16
U32 = mybir.dt.uint32
ALU = mybir.AluOpType
ACT = mybir.ActivationFunctionType
AX_X = mybir.AxisListType.X

P = 128
D = 1024
DC = D // P
T = 512
TB = T // P
EPS = 1e-6
NEG = -1e30

DA_HEADS, DA_DIM, DA_V = 4, 128, 256
MLA_HEADS, NOPE, ROPE, MLA_V = 8, 128, 64, 128
Q_RANK, KV_RANK = 384, 256
LAM_INIT = 0.8 - 0.6
KEYS, TOPK, PEER_HEADS = 128, 16, 8
HK = PEER_HEADS * TOPK

QA, KA, VA, CQ, CKV, KR, GATES, IN_TILES = 0, 8, 16, 24, 27, 29, 30, 46
MEANS = {"d": (D, 0, P), "da": (DA_DIM, 0, P), "cq": (Q_RANK, 0, P), "ckv": (KV_RANK, 0, P), "ya": (DA_V, 0, P),
         "mla": (NOPE + ROPE, 0, P), "mla_even": (NOPE + ROPE, 0, ROPE), "mla_odd": (NOPE + ROPE, ROPE, P)}
G_ATTN, G_FFN, G_DAQ, G_DAK, G_DAOUT, G_QLAT, G_KVLAT, G_MQN, G_MQR, G_MKN, G_MKR, G_LAM, G_COLS = (
    0, 8, 16, 17, 18, 20, 23, 25, 26, 27, 28, 29, 33)
BIAS_LEN = 640
PASSES = ((0, 0), (0, 1), (1, 0))


USED_SEMAPHORES = []


def recycle_semaphores(nc):
    nc.all_engine_barrier()
    nc.clear_and_free_semaphores(USED_SEMAPHORES)
    nc.all_engine_barrier()
    USED_SEMAPHORES.clear()


class Scope:

    def __init__(self, nc, name):
        self.nc, self.name, self.stack, self.sems = nc, name, ExitStack(), []

    def __enter__(self):
        return self

    def __exit__(self, *e):
        USED_SEMAPHORES.extend(self.sems)
        return self.stack.__exit__(*e)

    def sb(self, name, shape, dt=F32):
        return self.stack.enter_context(self.nc.sbuf_tensor(f"{self.name}_{name}", shape, dt))

    def ps(self, name, shape):
        return self.stack.enter_context(self.nc.psum_tensor(f"{self.name}_{name}", shape, F32))

    def sem(self, name):
        self.sems.append(self.nc.alloc_semaphore(f"{self.name}_{name}"))
        return self.sems[-1]


class Chain:

    def __init__(self, eng, sem):
        self.eng, self.sem, self.n = eng, sem, 0

    def __call__(self, ins):
        self.n += 1
        ins.then_inc(self.sem, 1)
        self.eng.wait_ge(self.sem, self.n)


def each(eng, start, end, unroll, body):
    laps = (end - start) // unroll
    if laps > 1:
        with eng.Fori(0, laps) as i:
            for k in range(unroll):
                body(i * unroll + (start + k), (start + k) % unroll, i + (start + k) // unroll)
        start += laps * unroll
    for n in range(start, end):
        body(n, n % unroll, n // unroll)


def first_partition(ap):
    return ap.start_partition()


def wait_all(eng, waits):
    for sem, value in waits:
        eng.wait_ge(sem, value)


class Part:

    def tensor(self, pe, k):
        pass

    def vector(self, dve, k):
        pass

    def scalar(self, act, k):
        pass

    def gpsimd(self, pool, k):
        pass


class Range:

    def __init__(self, slots, outs, chunks, c0, dest, d0, ready=None, by_token=False):
        self.slots, self.outs, self.chunks, self.c0, self.dest, self.d0, self.ready, self.by_token = (
            slots, outs, chunks, c0, dest, d0, ready, by_token)


class Stream:

    def __init__(self, s, nc, weights, act, ranges, slots):
        self.nc, self.weights, self.act, self.slots, self.loaded = nc, weights, act, slots, 0
        self.raw = s.sb("raw", [P, slots, D])
        self.half = [[s.sb(f"half{b}{h}", [P, D], F32R) for h in range(2)] for b in range(2)]
        self.acc = [s.ps(f"acc{b}", [P, T]) for b in range(2)]
        self.raw_in = [s.sem(f"raw_in{b}") for b in range(slots)]
        self.hi_done, self.lo_done, self.mm_done, self.out_done, self.opened = (
            s.sem(x) for x in ("hi_done", "lo_done", "mm_done", "out_done", "opened"))
        n = m = 0
        for r in ranges:
            r.n0, r.m0 = n, m
            n, m = n + r.slots, m + r.slots * r.outs
        self.count, self.ranges = n, ranges

    def range_of(self, n):
        return next(r for r in self.ranges if r.n0 <= n < r.n0 + r.slots)

    def landed(self, r, i):
        return self.out_done, r.m0 + i + 3

    def used(self, r):
        return self.mm_done, r.m0 + r.slots * r.outs

    def width(self, n):
        r = self.range_of(n)
        return r.chunks * (T if r.by_token else r.outs * P)

    def sync(self, sp, last):
        end = min(last.n0 + last.slots + 2 + self.slots, self.count)
        def load(n, r, lap):
            width = self.width(n) if isinstance(n, int) else D
            sp.wait_ge(self.lo_done, n + 1)
            sp.wait_ge(self.opened, 1)
            sp.dma_start(self.raw[:, r, 0:width],
                         self.weights[bass.ds(n, 1)].rearrange("o p f -> p (o f)")[:, 0:width]
                         ).then_inc(self.raw_in[r], 16)
        for r in self.ranges:
            n0, n1 = max(r.n0, self.loaded), min(r.n0 + r.slots, end)
            if self.width(r.n0) == D:
                each(sp, n0, n1, self.slots, load)
            else:
                for n in range(n0, n1):
                    load(n, n % self.slots, n // self.slots)
        self.loaded = end

    def round_weights(self, a, n, r, lap, width):
        a.wait_ge(self.raw_in[r], lap * 16 + 16)
        self.nc.scalar.activation(self.half[r % 2][0][:, 0:width], self.raw[:, r, 0:width], ACT.Copy
                                  ).then_inc(self.hi_done, 1)

    def scalar(self, a, rng, start, end, outs):
        def body(n, r, lap):
            for j in outs:
                i = (n - rng.n0) * rng.outs + j
                par = (rng.m0 + (r - rng.n0) * rng.outs + j) % 2
                a.wait_ge(self.mm_done, i + (rng.m0 + 1))
                if rng.by_token:
                    tile, block = rng.d0 + TB * (i // TB), i % TB
                    dest = rng.dest[:, tile:tile + TB, block * P:(block + 1) * P]
                    source = self.acc[par][:].rearrange("p (h d) -> p h d", d=P)
                else:
                    dest = rng.dest[:, bass.ds(i + rng.d0, 1), :].rearrange("p o t -> p (o t)")
                    source = self.acc[par][:]
                self.nc.scalar.activation(dest, source, ACT.Copy).then_inc(self.out_done, 1)
            if outs[-1] == rng.outs - 1 and (not isinstance(n, int) or n + 2 < self.count):
                self.round_weights(a, n + 2, (r + 2) % self.slots, lap + (r + 2) // self.slots,
                                   self.width(n + 2) if isinstance(n, int) else D)
        self.run(a, start, end, body)

    def rest(self, dve, n, r, width):
        dve.wait_ge(self.hi_done, n + 1)
        self.nc.vector.tensor_tensor(self.half[r % 2][1][:, 0:width], self.raw[:, r, 0:width],
                                     self.half[r % 2][0][:, 0:width].bitcast(F32), ALU.subtract
                                     ).then_inc(self.lo_done, 1)

    def vector(self, dve, rng, start, end, outs):
        def body(n, r, lap):
            if outs[-1] == rng.outs - 1 and (not isinstance(n, int) or n + 2 < self.count):
                self.rest(dve, n + 2, (r + 2) % self.slots, self.width(n + 2) if isinstance(n, int) else D)
        self.run(dve, start, end, body)

    def tensor(self, pe, rng, start, end, outs, chunks):
        def body(n, r, lap, first=False):
            if 0 in chunks:
                pe.wait_ge(self.lo_done, n + (self.slots + 1))
            for j in outs:
                par = (rng.m0 + (r - rng.n0) * rng.outs + j) % 2
                if 0 in chunks:
                    pe.wait_ge(self.out_done, (n - rng.n0) * rng.outs + (rng.m0 + j + 1))
                for c in chunks:
                    if first and j == 0 and rng.ready:
                        pe.wait_ge(*rng.ready(c))
                    for k, (w, x) in enumerate(PASSES):
                        if rng.by_token:
                            left = self.act[x][:, rng.c0 + c, j * P:(j + 1) * P]
                            right = self.half[r % 2][w][:, c * T:(c + 1) * T]
                        else:
                            at = (j * rng.chunks + c) * P
                            left, right = self.half[r % 2][w][:, at:at + P], self.act[x][:, rng.c0 + c, :]
                        last = self.nc.tensor.matmul(
                            self.acc[par][:], left, right,
                            start=(c == 0 and k == 0), stop=(c == rng.chunks - 1 and k == 2))
                if rng.chunks - 1 in chunks:
                    last.then_inc(self.mm_done, 1)
        if start == rng.n0:
            body(start, start % self.slots, start // self.slots, first=True)
            start += 1
        self.run(pe, start, end, body)

    def run(self, eng, start, end, body):
        whole = end - 2 if end - start > 2 * self.slots else end
        if end - start > 2 * self.slots:
            each(eng, start, whole, self.slots, body)
            start = whole
        for n in range(start, end):
            body(n, n % self.slots, n // self.slots)


class Opening(Part):

    def __init__(self, stream):
        self.stream = stream

    def steps(self):
        return [(self, n) for n in range(2)]

    def gpsimd(self, pool, n):
        if n == 0:
            pool.sem_inc(self.stream.lo_done, self.stream.slots)
            pool.sem_inc(self.stream.out_done, 2)
            pool.sem_inc(self.stream.opened, 1)

    def scalar(self, act, n):
        self.stream.round_weights(act, n, n, 0, self.stream.width(n))

    def vector(self, dve, n):
        self.stream.rest(dve, n, n, self.stream.width(n))


class Tiles(Part):

    def __init__(self, stream, rng):
        self.stream, self.rng = stream, rng

    def steps(self, start=0, end=None):
        return [(self, k) for k in range(start, self.rng.slots if end is None else end)]

    def out_steps(self, start=0, end=None):
        return [(self, (k, "output", j)) for _, k in self.steps(start, end) for j in range(self.rng.outs)]

    def part_steps(self):
        return [(self, (k, "part", q)) for _, k in self.steps() for q in range(4)]

    def at(self, k):
        outs = list(range(self.rng.outs))
        if isinstance(k, int):
            start, end = k, k + 1
        elif "part" in k:
            start, end = k[0], k[0] + 1
        elif "output" in k:
            start, end, outs = k[0], k[0] + 1, [k[2]]
        else:
            start, end = k
        return self.rng, self.rng.n0 + start, self.rng.n0 + end, outs

    def tensor(self, pe, k):
        chunks = range(self.rng.chunks)
        if not isinstance(k, int) and "part" in k:
            quarter = self.rng.chunks // 4
            chunks = range(k[2] * quarter, (k[2] + 1) * quarter)
        self.stream.tensor(pe, *self.at(k), chunks)

    def ends_tile(self, k):
        return isinstance(k, int) or "part" not in k or k[2] == 3

    def vector(self, dve, k):
        if self.ends_tile(k):
            self.stream.vector(dve, *self.at(k))

    def scalar(self, act, k):
        if self.ends_tile(k):
            self.stream.scalar(act, *self.at(k))


def phase(nc, order, stream, last, sync=None):
    with nc.Block() as block:
        @block.sync
        def _(sp):
            if sync:
                sync(sp)
            stream.sync(sp, last)

        @block.gpsimd
        def _(pool):
            for part, k in order:
                part.gpsimd(pool, k)

        @block.tensor
        def _(pe):
            for part, k in order:
                part.tensor(pe, k)

        @block.vector
        def _(dve):
            for part, k in order:
                part.vector(dve, k)

        @block.scalar
        def _(act):
            for part, k in order:
                part.scalar(act, k)


def weave(*lists):
    keyed = [((i + 0.5) / len(x), n, i, step) for n, x in enumerate(lists) for i, step in enumerate(x)]
    return [step for _, _, _, step in sorted(keyed, key=lambda t: t[:3])]


class Roots(Part):

    def __init__(self, s, nc, name, squares, groups, consts, bank, room=None, sq=None, added=False):
        self.nc, self.squares, self.groups, self.consts, self.bank, self.added = (
            nc, squares, groups, consts, bank, added)
        self.lag, self.ring = (0, 3) if added else (3, 4)
        kinds = []
        for x in squares:
            if x[2] not in kinds:
                kinds.append(x[2])
        self.kinds = kinds
        room = s.sb(f"{name}_select", [P, groups * len(kinds)]) if room is None else room
        self.selectors = room[:, 0:groups * len(kinds)].rearrange("p (k g) -> p k g", g=groups)
        self.sq = sq if sq is not None else s.sb(f"{name}_sq", [P, 4, T])
        self.inv = s.sb(f"{name}_inv", [P, TB, groups])
        self.selected, self.squared, self.summed, self.copied, self.turned, self.rooted, self.inverted, self.total = (
            s.sem(f"{name}_{x}") for x in ("selected", "squared", "summed", "copied", "turned", "rooted", "inverted",
                                           "total"))
        self.fills = 1 + sum(len(kind) for kind in kinds)

    def select_step(self):
        return [(self, "select")]

    def sum_steps(self, start=0, end=None):
        return [(self, k) for k in range(start, len(self.squares) + self.lag if end is None else end)]

    def root_step(self):
        return [(self, "root")]

    def done(self):
        return self.inverted, 1

    def scalar(self, act, k):
        nc = self.nc
        if k == "root":
            act.wait_ge(self.summed, 1 if self.added else len(self.squares))
            nc.scalar.activation(self.sq[0:self.groups, 0, :], self.bank[0:self.groups, :], ACT.Copy
                                 ).then_inc(self.copied, 1)
            act.wait_ge(self.turned, 1)
            nc.scalar.activation(self.inv[:].rearrange("p b g -> p (b g)"), self.bank[:, 0:TB * self.groups],
                                 ACT.Sqrt, bias=self.consts["eps"][:, 0:1]).then_inc(self.rooted, 1)
        elif k != "select" and k < len(self.squares) and self.added:
            tile, waits, _ = self.squares[k]
            wait_all(act, waits)
            if k >= self.ring:
                act.wait_ge(self.total, k - self.ring + 1)
            nc.scalar.activation(self.sq[:, k % self.ring, :], tile, ACT.Square).then_inc(self.squared, 1)

    def gpsimd(self, pool, k):
        if k in ("root", "select") or k >= len(self.squares) or self.added:
            return
        tile, waits, _ = self.squares[k]
        wait_all(pool, waits)
        if k >= self.ring:
            pool.wait_ge(self.summed, k - self.ring + 1)
        self.nc.gpsimd.tensor_tensor(self.sq[:, k % self.ring, :], tile, tile, ALU.mult).then_inc(self.squared, 1)

    def tensor(self, pe, k):
        if k == "root":
            if self.added:
                pe.wait_ge(self.selected, self.fills)
                pe.wait_ge(self.total, len(self.squares))
                self.sum(0, 3, True, True)
            pe.wait_ge(self.copied, 1)
            for b in range(TB):
                last = self.nc.tensor.matmul(self.bank[:, b * self.groups:(b + 1) * self.groups],
                                             self.sq[0:self.groups, 0, b * P:(b + 1) * P],
                                             self.consts["ident"][0:self.groups, 0:self.groups], start=True, stop=True)
            last.then_inc(self.turned, 1)
        elif k != "select" and k >= self.lag and not self.added:
            k -= self.lag
            if k == 0:
                pe.wait_ge(self.selected, self.fills)
            pe.wait_ge(self.squared, k + 1)
            self.sum(k, k % self.ring, k == 0, k == len(self.squares) - 1)

    def sum(self, k, slot, start, stop):
        kind = self.kinds.index(self.squares[k][2])
        self.nc.tensor.matmul(self.bank[0:self.groups, :], self.selectors[:, kind, :], self.sq[:, slot, :],
                              start=start, stop=stop).then_inc(self.summed, 1)

    def vector(self, dve, k):
        nc = self.nc
        if k == "select":
            nc.vector.memset(self.selectors, 0.0).then_inc(self.selected, 1)
            dve.wait_ge(self.selected, 1)
            for n, kind in enumerate(self.kinds):
                for mean, start, end in kind:
                    width, p0, p1 = MEANS[mean]
                    nc.vector.memset(self.selectors[p0:p1, n, start:end], 1.0 / width).then_inc(self.selected, 1)
        elif k == "root":
            dve.wait_ge(self.rooted, 1)
            nc.vector.reciprocal(self.inv[:], self.inv[:]).then_inc(self.inverted, 1)
        elif self.added and k >= 1:
            total = self.sq[:, 3, :]
            dve.wait_ge(self.squared, k + 1)
            if k >= 2:
                dve.wait_ge(self.total, k)
            nc.vector.tensor_tensor(total, self.sq[:, 0, :] if k == 1 else total, self.sq[:, k % self.ring, :],
                                    ALU.add).then_inc(self.total, 2 if k == 1 else 1)


class Apply(Part):

    def __init__(self, s, nc, name, groups, roots, consts, banks, split=None, free=(), tmp=None):
        self.nc, self.groups, self.roots, self.consts, self.banks, self.split, self.free = (
            nc, groups, roots, consts, banks, split, free)
        self.tmp = (tmp if tmp is not None else s.sb(f"{name}_tmp", [P, 4, T])) if split else None
        self.ring = self.tmp.shape[1] if split else 0
        self.spread, self.scaled = s.sem(f"{name}_spread"), s.sem(f"{name}_scaled")
        if split:
            self.hi, self.lo = s.sem(f"{name}_hi"), [s.sem(f"{name}_lo{k}") for k in range(2)]
        self.first, n = [0], 0
        for _, outs in groups:
            n += len(outs)
            self.first.append(n)

    def steps(self, start=0, end=None):
        return [(self, k) for k in range(start, len(self.groups) if end is None else end)]

    def done(self, k=None):
        return self.scaled, self.first[-1 if k is None else k + 1]

    def chunk(self, c):
        return self.lo[c % 2], c // 2 + 1

    def tensor(self, pe, k):
        if k == 0:
            wait_all(pe, [self.roots.done()])
        if k >= len(self.banks):
            pe.wait_ge(self.scaled, self.first[k - len(self.banks) + 1])
        bank = self.banks[k % len(self.banks)]
        for b in range(TB):
            factor = self.roots.inv[:, b, self.groups[k][0]:self.groups[k][0] + 1]
            last = self.nc.tensor.transpose(bank[:, b * P:(b + 1) * P], factor.to_broadcast([P, P]),
                                            self.consts["ident"][:])
        last.then_inc(self.spread, 1)

    def vector(self, dve, k):
        nc = self.nc
        bank = self.banks[k % len(self.banks)]
        dve.wait_ge(self.spread, k + 1)
        for m, (tile, gain, dest) in enumerate(self.groups[k][1], start=self.first[k]):
            p0 = first_partition(tile)
            if self.split:
                if m >= self.ring:
                    dve.wait_ge(*self.chunk(m - self.ring))
                dest = self.tmp[:, m % self.ring, :]
            nc.vector.scalar_tensor_tensor(dest, tile, gain, bank[p0:p0 + tile.shape[0], :], ALU.mult, ALU.mult
                                           ).then_inc(self.scaled, 1)
            if self.split and m % 2 == 0 and m > self.first[k]:
                self.odd_rest(dve, k, m - 1)
        if self.split and m % 2 == 1:
            self.odd_rest(dve, k, m)

    def odd_rest(self, dve, k, m):
        chunk = self.groups[k][1][m - self.first[k]][2]
        dve.wait_ge(self.hi, m + 1)
        self.nc.vector.tensor_tensor(self.split[1][:, chunk, :], self.tmp[:, m % self.ring, :],
                                     self.split[0][:, chunk, :].bitcast(F32), ALU.subtract).then_inc(self.lo[1], 1)

    def scalar(self, act, k):
        if not self.split:
            return
        if k == 0:
            wait_all(act, self.free)
        for m, (_, _, chunk) in enumerate(self.groups[k][1], start=self.first[k]):
            act.wait_ge(self.scaled, m + 1)
            self.nc.scalar.activation(self.split[0][:, chunk, :], self.tmp[:, m % self.ring, :], ACT.Copy
                                      ).then_inc(self.hi, 1)

    def gpsimd(self, pool, k):
        if not self.split:
            return
        for m, (_, _, chunk) in enumerate(self.groups[k][1], start=self.first[k]):
            if m % 2 == 0:
                pool.wait_ge(self.hi, m + 1)
                self.nc.gpsimd.tensor_tensor(self.split[1][:, chunk, :], self.tmp[:, m % self.ring, :],
                                             self.split[0][:, chunk, :].bitcast(F32), ALU.subtract
                                             ).then_inc(self.lo[0], 1)


class Attention(Part):

    def __init__(self, s, nc, blocks, consts, maps, vtiles, ps_s, ps_t, ps_o, logits, prob, neglam=None,
                 factors_ready=(), values_ready=()):
        self.nc, self.blocks, self.consts, self.maps, self.vtiles = nc, blocks, consts, maps, vtiles
        self.ps_s, self.ps_t, self.ps_o, self.neglam, self.factors_ready, self.values_ready = (
            ps_s, ps_t, ps_o, neglam, factors_ready, values_ready)
        self.logits, self.prob = logits.rearrange("p (b m) t -> p b m t", m=maps), prob
        self.low = s.sb("low", [P, 2, 2])
        self.sums = s.sb("sums", [P, 2, 2])
        self.inv = s.sb("inv", [P, 2, 2])
        self.probT = s.sb("probT", [P, 2, T])
        self.scored, self.maxed, self.exped, self.weighted, self.turned, self.turned_out, self.valued, self.stored, \
            self.inner = (s.sem(x) for x in ("scored", "maxed", "exped", "weighted", "turned", "turned_out",
                                             "valued", "stored", "inner"))
        self.chain = None

    def steps(self):
        return [(self, k) for k in range(len(self.blocks) + 3)]

    def tensor(self, pe, st):
        nc, N = self.nc, len(self.blocks)
        if st < N:
            n = st
            qb, pairs, _, _, _, _, ready = self.blocks[n]
            wait_all(pe, ready)
            if n >= 2:
                pe.wait_ge(self.maxed, n - 1)
            for m in range(self.maps):
                for k, (q, kk) in enumerate(pairs[m]):
                    last = nc.tensor.matmul(self.ps_s[n % 2][m][:, 0:(qb + 1) * P], q[:, qb * P:(qb + 1) * P],
                                            kk[:, 0:(qb + 1) * P], start=(k == 0), stop=(k == len(pairs[m]) - 1))
            last.then_inc(self.scored, 1)
        if 2 <= st < N + 2:
            n = st - 2
            pe.wait_ge(self.weighted, n + 1)
            if n >= 1:
                pe.wait_ge(self.turned_out, n)
            for kb in range(self.blocks[n][0] + 1):
                last = nc.tensor.transpose(self.ps_t[:, kb * P:(kb + 1) * P],
                                           self.prob[:, n % 2, kb * P:(kb + 1) * P], self.consts["ident"][:])
            last.then_inc(self.turned, 1)
        if st >= 3:
            n = st - 3
            qb, values = self.blocks[n][0], self.blocks[n][4]
            if n == 0:
                wait_all(pe, self.values_ready)
            pe.wait_ge(self.turned_out, n + 1)
            if n >= 1:
                pe.wait_ge(self.stored, n)
            for v in range(self.vtiles):
                for kb in range(qb + 1):
                    last = nc.tensor.matmul(self.ps_o[:, v * P:(v + 1) * P], values[v][:, kb * P:(kb + 1) * P],
                                            self.probT[:, n % 2, kb * P:(kb + 1) * P],
                                            start=(kb == 0), stop=(kb == qb))
            last.then_inc(self.valued, 1)

    def vector(self, dve, st):
        nc, N = self.nc, len(self.blocks)
        if self.chain is None:
            self.chain = Chain(dve, self.inner)
            wait_all(dve, self.factors_ready)
        chain = self.chain
        if st < N:
            n = st
            qb, factors, bias = self.blocks[n][0], self.blocks[n][2], self.blocks[n][3]
            w = (qb + 1) * P
            dve.wait_ge(self.scored, n + 1)
            if n >= 2:
                dve.wait_ge(self.weighted, n - 1)
            for m in range(self.maps):
                chain(nc.vector.scalar_tensor_tensor(self.logits[:, n % 2, m, 0:w], self.ps_s[n % 2][m][:, 0:w],
                                                     factors[m], bias[:, T - w:T], ALU.mult, ALU.add))
            for m in range(self.maps):
                ins = nc.vector.tensor_reduce(self.low[:, n % 2, m:m + 1], self.logits[:, n % 2, m, 0:w], AX_X,
                                              ALU.max, negate=True)
                if m < self.maps - 1:
                    chain(ins)
            ins.then_inc(self.maxed, 1)
        if 1 <= st <= N:
            n = st - 1
            w = (self.blocks[n][0] + 1) * P
            inv, prob, logits = self.inv, self.prob, self.logits
            dve.wait_ge(self.exped, n + 1)
            if n >= 2:
                dve.wait_ge(self.turned, n - 1)
            chain(nc.vector.reciprocal(inv[:, n % 2, 0:self.maps], self.sums[:, n % 2, 0:self.maps]))
            ins = nc.vector.tensor_scalar(prob[:, n % 2, 0:w], logits[:, n % 2, 0, 0:w], inv[:, n % 2, 0:1], None,
                                          ALU.mult)
            if self.maps == 2:
                chain(ins)
                chain(nc.vector.tensor_scalar(inv[:, n % 2, 1:2], inv[:, n % 2, 1:2], self.neglam, None, ALU.mult))
                ins = nc.vector.scalar_tensor_tensor(prob[:, n % 2, 0:w], logits[:, n % 2, 1, 0:w],
                                                     inv[:, n % 2, 1:2], prob[:, n % 2, 0:w], ALU.mult, ALU.add)
            ins.then_inc(self.weighted, 1)

    def scalar(self, act, st):
        nc, N = self.nc, len(self.blocks)
        if st < N:
            n = st
            w = (self.blocks[n][0] + 1) * P
            act.wait_ge(self.maxed, n + 1)
            for m in range(self.maps):
                ins = nc.scalar.activation(self.logits[:, n % 2, m, 0:w], self.logits[:, n % 2, m, 0:w], ACT.Exp,
                                           bias=self.low[:, n % 2, m:m + 1], accum_out=self.sums[:, n % 2, m:m + 1])
            ins.then_inc(self.exped, 1)
        if 2 <= st < N + 2:
            n = st - 2
            w = (self.blocks[n][0] + 1) * P
            act.wait_ge(self.turned, n + 1)
            if n >= 2:
                act.wait_ge(self.valued, n - 1)
            nc.scalar.activation(self.probT[:, n % 2, 0:w], self.ps_t[:, 0:w], ACT.Copy).then_inc(self.turned_out, 1)
        if st >= 3:
            n = st - 3
            act.wait_ge(self.valued, n + 1)
            nc.scalar.activation(self.blocks[n][5], self.ps_o[:, 0:self.vtiles * P].rearrange(
                "p (v q) -> p v q", v=self.vtiles), ACT.Copy).then_inc(self.stored, 1)


class Turn(Part):

    def __init__(self, s, nc, name, tiles, consts, banks):
        self.nc, self.tiles, self.consts, self.banks = nc, tiles, consts, banks
        self.turned, self.stored = s.sem(f"{name}_turned"), s.sem(f"{name}_stored")

    def steps(self, start=0, end=None):
        return [(self, k) for k in range(start, len(self.tiles) if end is None else end)]

    def done(self):
        return self.stored, len(self.tiles)

    def tensor(self, pe, n):
        tile, ready = self.tiles[n]
        wait_all(pe, ready)
        if n >= 2:
            pe.wait_ge(self.stored, n - 1)
        for tb in range(TB):
            last = self.nc.tensor.transpose(self.banks[n % 2][:, tb * P:(tb + 1) * P], tile[:, tb * P:(tb + 1) * P],
                                            self.consts["ident"][:])
        last.then_inc(self.turned, 1)

    def scalar(self, act, n):
        act.wait_ge(self.turned, n + 1)
        self.nc.scalar.activation(self.tiles[n][0], self.banks[n % 2][:], ACT.Copy).then_inc(self.stored, 1)


class Rotate(Part):

    def __init__(self, s, nc, tiles, consts, bank, turned):
        self.nc, self.tiles, self.consts, self.bank, self.turned = nc, tiles, consts, bank, turned
        self.swapped, self.used, self.inner, self.rotated = (
            s.sem(f"rot_{x}") for x in ("swapped", "used", "inner", "rotated"))
        self.chain = None

    def steps(self):
        return [(self, k) for k in range(len(self.tiles))]

    def done(self, n):
        return self.rotated, n + 1

    def tensor(self, pe, n):
        tile, ready = self.tiles[n]
        wait_all(pe, ready)
        if n >= 1:
            pe.wait_ge(self.used, n)
        self.nc.tensor.matmul(self.bank[:], self.consts["perm"][:], tile, start=True, stop=True
                              ).then_inc(self.swapped, 1)

    def vector(self, dve, n):
        nc, tile = self.nc, self.tiles[n][0]
        if self.chain is None:
            self.chain = Chain(dve, self.inner)
        dve.wait_ge(self.swapped, n + 1)
        if n >= 1:
            dve.wait_ge(self.rotated, n)
        nc.vector.tensor_tensor(self.turned, self.bank[:], self.consts["sin"][:], ALU.mult).then_inc(self.used, 1)
        self.chain(nc.vector.tensor_tensor(tile, tile, self.consts["cos"][:], ALU.mult))
        dve.wait_ge(self.used, n + 1)
        nc.vector.tensor_tensor(tile, tile, self.turned, ALU.add).then_inc(self.rotated, 1)


class Split(Part):

    def __init__(self, s, nc, name, tiles, act, free=()):
        self.nc, self.tiles, self.act, self.free = nc, tiles, act, free
        self.hi, self.lo = s.sem(f"{name}_hi"), [s.sem(f"{name}_lo{k}") for k in range(2)]

    def steps(self):
        return [(self, k) for k in range(len(self.tiles))]

    def chunk(self, c):
        return self.lo[c % 2], c // 2 + 1

    def scalar(self, act, c):
        tile, ready = self.tiles[c]
        if c == 0:
            wait_all(act, self.free)
        wait_all(act, ready)
        self.nc.scalar.activation(self.act[0][:, c, :], tile, ACT.Copy).then_inc(self.hi, 1)

    def gpsimd(self, pool, c):
        if c % 2 == 0:
            pool.wait_ge(self.hi, c + 1)
            self.nc.gpsimd.tensor_tensor(self.act[1][:, c, :], self.tiles[c][0], self.act[0][:, c, :].bitcast(F32),
                                         ALU.subtract).then_inc(self.lo[0], 1)

    def vector(self, dve, c):
        if c % 2 == 1:
            dve.wait_ge(self.hi, c + 1)
            self.nc.vector.tensor_tensor(self.act[1][:, c, :], self.tiles[c][0], self.act[0][:, c, :].bitcast(F32),
                                         ALU.subtract).then_inc(self.lo[1], 1)


class Sigmoids(Part):

    def __init__(self, s, nc, gates):
        self.nc, self.gates = nc, gates.rearrange("p (g c) t -> p g c t", g=2)
        self.gated = s.sem("gated")

    def done(self, c):
        return self.gated, c + 1

    def scalar(self, act, c):
        g = self.gates[:, :, c, :]
        self.nc.scalar.activation(g, g, ACT.Sigmoid).then_inc(self.gated, 1)


class Merge(Part):

    def __init__(self, s, nc, ya, yb, gates, gated, yb_landed):
        self.nc, self.ya, self.yb, self.gates, self.gated, self.landed = nc, ya, yb, gates, gated, yb_landed
        self.inner, self.merged = s.sem("mg_inner"), s.sem("mg_merged")

    def done(self, c):
        return self.merged, c + 1

    def vector(self, dve, c):
        nc, ya, yb = self.nc, self.ya[:, c, :], self.yb[:, c, :]
        wait_all(dve, [self.gated(c)])
        nc.vector.tensor_tensor(ya, ya, self.gates[:, c, :], ALU.mult).then_inc(self.inner, 1)
        wait_all(dve, [self.landed(c)])
        nc.vector.tensor_tensor(yb, yb, self.gates[:, DC + c, :], ALU.mult).then_inc(self.inner, 1)
        dve.wait_ge(self.inner, 2 * c + 2)
        nc.vector.tensor_tensor(ya, ya, yb, ALU.add).then_inc(self.merged, 1)


class Residual(Part):

    def __init__(self, s, nc, x_dram, x2, projected, landed, x2_dram):
        self.nc, self.x_dram, self.x2, self.projected, self.landed, self.x2_dram = (
            nc, x_dram, x2, projected, landed, x2_dram)
        self.x_in, self.added, self.stored = s.sem("x_in"), s.sem("added"), s.sem("stored")

    def sync(self, sp):
        for c in range(DC):
            sp.dma_start(self.x2[:, c, :], self.x_dram[c]).then_inc(self.x_in, 16)

    def done(self, c):
        return self.added, c + 1

    def vector(self, dve, c):
        if c == "stored":
            return
        dve.wait_ge(self.x_in, 16 * DC)
        wait_all(dve, [self.landed(c)])
        self.nc.vector.tensor_tensor(self.x2[:, c, :], self.x2[:, c, :], self.projected[:, c, :], ALU.add
                                     ).then_inc(self.added, 1)

    def scalar(self, act, c):
        if c == "stored":
            act.wait_ge(self.stored, 16 * DC)
        else:
            act.wait_ge(self.added, c + 1)
            act.dma_start(self.x2_dram[c], self.x2[:, c, :]).then_inc(self.stored, 16)


class Tables(Part):

    def __init__(self, s, nc, dram, consts, bias, neglam, gains_in, row, banks):
        self.nc, self.dram, self.consts, self.bias, self.neglam, self.gains_in, self.row, self.banks = (
            nc, dram, consts, bias, neglam, gains_in, row, banks)
        self.relb = s.sb("relb", [33, DA_HEADS])
        self.relw = s.sb("relw", [33, DA_HEADS, P])
        self.onehot = s.sb("onehot", [33, BIAS_LEN])
        self.prod = s.sb("prod", [P, 2])
        self.lam = s.sb("lam", [P, 2])
        (self.filled, self.rel_in, self.wide, self.rowed, self.row_out, self.skewed, self.inner, self.lam_mm,
         self.lam_exp, self.prodd, self.bias_mm) = (
            s.sem(f"tb_{x}") for x in ("filled", "rel_in", "wide", "rowed", "row_out", "skewed", "inner", "lam_mm",
                                       "lam_exp", "prodd", "bias_mm"))

    def done(self):
        return self.skewed, 16 * DA_HEADS

    def gpsimd(self, pool, k):
        nc = self.nc
        if k == "load":
            nc.gpsimd.memset(self.relb[32:33, :], NEG).then_inc(self.filled, 1)
            pool.wait_ge(self.filled, 1)
            pool.dma_start(self.relb[0:32, :], self.dram["rel_bias"][:, :]).then_inc(self.rel_in, 16)
            pool.dma_start(self.onehot[:], self.dram["onehot"][:, :]).then_inc(self.rel_in, 16)
        elif k == 1:
            pool.wait_ge(self.rowed, DA_HEADS + 1)
            pool.dma_start(self.dram["skew"].rearrange("h (q n) -> q h n", n=BIAS_LEN), self.row[:]
                           ).then_inc(self.row_out, 16)
        elif k == 2:
            pool.wait_ge(self.row_out, 16)
            for h in range(DA_HEADS):
                src = self.dram["skew"][h, P - 1:P - 1 + P * (BIAS_LEN - 1)]
                pool.dma_start(self.bias[:, h, :], src.rearrange("(q n) -> q n", n=BIAS_LEN - 1)[:, 0:T]
                               ).then_inc(self.skewed, 16)

    def vector(self, dve, k):
        if k != 0:
            return
        nc, g = self.nc, self.consts["gains"]
        chain = Chain(dve, self.inner)
        dve.wait_ge(self.filled, 1)
        dve.wait_ge(self.rel_in, 32)
        for h in range(DA_HEADS):
            nc.vector.tensor_copy(self.relw[:, h, :], self.relb[:, h:h + 1].to_broadcast([33, P])
                                  ).then_inc(self.wide, 1)
        wait_all(dve, [self.gains_in])
        for k in range(2):
            nc.vector.tensor_tensor(self.prod[:, k:k + 1], g[:, G_LAM + 2 * k:G_LAM + 2 * k + 1],
                                    g[:, G_LAM + 2 * k + 1:G_LAM + 2 * k + 2], ALU.mult).then_inc(self.prodd, 1)
        chain(nc.vector.tensor_scalar(g[:, G_DAOUT:G_DAOUT + 2], g[:, G_DAOUT:G_DAOUT + 2], 1.0 - LAM_INIT,
                                      None, ALU.mult))
        for kg, qg, scale in ((G_DAK, G_DAQ, DA_DIM ** -0.5), (G_MKN, G_MQN, (NOPE + ROPE) ** -0.5),
                              (G_MKR, G_MQR, (NOPE + ROPE) ** -0.5)):
            chain(nc.vector.tensor_scalar(g[:, kg:kg + 1], g[:, kg:kg + 1], g[:, qg:qg + 1], scale, ALU.mult,
                                          ALU.mult))
        dve.wait_ge(self.lam_exp, 1)
        chain(nc.vector.tensor_tensor(self.neglam[:], self.lam[:, 1:2], self.lam[:, 0:1], ALU.subtract))
        chain(nc.vector.tensor_scalar(self.neglam[:], self.neglam[:], -LAM_INIT, None, ALU.add))

    def tensor(self, pe, k):
        if k != 0:
            return
        nc = self.nc
        pe.wait_ge(self.wide, DA_HEADS)
        for h in range(DA_HEADS):
            nc.tensor.matmul(self.banks[h][:], self.relw[:, h, :], self.onehot[:, 0:T], start=True, stop=True
                             ).then_inc(self.bias_mm, 1)
        pe.wait_ge(self.rowed, 1)
        for h in range(DA_HEADS):
            last = nc.tensor.matmul(self.banks[0][:, h * P:(h + 1) * P], self.relw[:, h, :],
                                    self.onehot[:, T:BIAS_LEN], start=True, stop=True)
        last.then_inc(self.bias_mm, 1)
        pe.wait_ge(self.prodd, 2)
        pe.wait_ge(self.rowed, 2)
        nc.tensor.matmul(self.banks[1][:, 0:2], self.consts["ones"][:], self.prod[:], start=True, stop=True
                         ).then_inc(self.lam_mm, 1)

    def scalar(self, act, k):
        if k != 0:
            return
        nc = self.nc
        for h in range(DA_HEADS):
            act.wait_ge(self.bias_mm, h + 1)
            nc.scalar.activation(self.row[:, h, 0:T], self.banks[h][:], ACT.Copy).then_inc(self.rowed, 1)
        act.wait_ge(self.bias_mm, DA_HEADS + 1)
        nc.scalar.activation(self.row[:, :, T:BIAS_LEN], self.banks[0][:].rearrange("p (h n) -> p h n", n=P),
                             ACT.Copy).then_inc(self.rowed, 1)
        act.wait_ge(self.lam_mm, 1)
        nc.scalar.activation(self.lam[:], self.banks[1][:, 0:2], ACT.Exp).then_inc(self.lam_exp, 1)


CHUNK = 32
JG = 4


class ExpertBuffers:

    def __init__(self, s):
        self.raw = s.sb("raw", [P, 4, D])
        self.half = [[s.sb(f"half{b}{h}", [P, D], F32R) for h in range(2)] for b in range(2)]
        self.gel = s.sb("gel", [P, 4, T])
        self.g_in = s.sb("g_in", [P, 2, T // CHUNK, JG, CHUNK])
        self.v_in = [s.sem(f"v_in{r}") for r in range(4)]
        self.gel_in = [s.sem(f"gel_in{r}") for r in range(4)]
        self.gate_in = [s.sem(f"gate_in{b}") for b in range(2)]


def first_layer(nc, query, dram, consts, act, spilled, gates, shared):
    H, K = PEER_HEADS, TOPK
    QUAD = 4
    ROUTE_J, PAIR_J = 12, 8
    STEPS = P // (2 * CHUNK)
    BLOCK_J = ROUTE_J + STEPS * PAIR_J
    EXP_J, TURN_J = 8, 10
    QUADS_J = 2 * CHUNK // QUAD // PAIR_J
    assert TB * BLOCK_J <= KEYS and ROUTE_J % 4 == 0
    with Scope(nc, "fl") as s:
        u_raw, u, gel = shared.raw, shared.half, shared.gel[:, 2:4, :]
        keys = s.sb("keys", [P, 2 * H, KEYS])
        score = s.sb("score", [P, 2 * H, KEYS])
        top = s.sb("top", [P, 2 * H, K])
        top_i = s.sb("top_i", [P, 2 * H, K], U32)
        top_f = s.sb("top_f", [P, 2 * H, K])
        cand = s.sb("cand", [P, H, K, K])
        best = s.sb("best", [P, H, K])
        pos = s.sb("pos", [P, H, K], U32)
        half_i = s.sb("half_i", [P, 2, H, K], U32)
        half_f = s.sb("half_f", [P, 2, H, K])
        hit = cand
        pick = s.sb("pick", [P, 3, H, K])
        gsum = s.sb("gsum", [P, H])
        pickT = s.sb("pickT", [P, 3, P])
        PARTS = 3
        part = [s.sb(f"part{k}", [P, P], BF16) for k in range(PARTS)]
        left = s.sb("left", [P, P])
        hot_j = s.sb("hot_j", [P, 2, QUAD, KEYS], BF16)
        row_i = s.sb("row_i", [P, 2, QUAD, KEYS], BF16)
        row_j = s.sb("row_j", [P, 2, PARTS, QUAD, KEYS], BF16)
        grid = s.sb("grid", [P, 2, KEYS, CHUNK])
        ps_a = [s.ps(f"a{b}", [P, T]) for b in range(2)]
        ps_r = [s.ps(f"r{q}", [P, 4, KEYS]) for q in range(4)]
        ps_g = [s.ps(f"g{b}", [P, QUAD, KEYS]) for b in range(2)]
        u_in = [s.sem(f"u_in{r}") for r in range(4)]
        spill_out = [s.sem(f"spill_out{b}") for b in range(2)]
        grid_out = [s.sem(f"grid_out{b}") for b in range(2)]
        u_hi, u_lo, a_done, gelued, opened = (s.sem(x) for x in ("u_hi", "u_lo", "a_done", "gelued", "opened"))
        keys_in = [s.sem(f"keys_in{q}") for q in range(4)]
        scored, score_out, inner, shifted, exped, picked, turned, pick_out = (
            s.sem(x) for x in ("scored", "score_out", "inner", "shifted", "exped", "picked", "turned",
                               "pick_out"))
        hot, rows_i, rows_j, quad_done, quad_out = (
            s.sem(x) for x in ("hot", "rows_i", "rows_j", "quad_done", "quad_out"))
        iota = consts["iota"]
        QB = P // QUAD

        def schedule(eng, one_j, one_quad, before, exps, turn, chunk_end):
            for tb in range(TB):
                n0 = tb * BLOCK_J
                before(tb)
                for n in range(n0, n0 + ROUTE_J):
                    if n == n0 + EXP_J:
                        exps(tb)
                    if n == n0 + TURN_J:
                        turn(tb)
                    one_j(n, n % 4, n // 4)
                with eng.Fori(0, STEPS) as i:
                    for k in range(PAIR_J):
                        one_j(i * PAIR_J + (n0 + ROUTE_J + k), k % 4, i * (PAIR_J // 4) + (n0 + ROUTE_J + k) // 4)
                        for m in range(QUADS_J):
                            q = k * QUADS_J + m
                            one_quad(tb, i * (2 * CHUNK // QUAD) + q, q)
                        if k % (PAIR_J // 2) == PAIR_J // 2 - 1:
                            chunk_end(tb, i * 2 + (tb * P // CHUNK + k // (PAIR_J // 2)), k // (PAIR_J // 2))
            each(eng, TB * BLOCK_J, KEYS - 4, 4, one_j)
            for n in range(KEYS - 4, KEYS):
                one_j(n, n % 4, n // 4)

        def nothing(*_):
            pass

        with nc.Block() as block:
            @block.sync
            def _(sp):
                for q in range(4):
                    sp.dma_start(keys[:, 4 * q:4 * q + 4, :], dram["keys"].rearrange("p (g n) -> p g n", n=KEYS)[
                        :, 4 * q:4 * q + 4, :]).then_inc(keys_in[q], 16)

                def load(n, r):
                    sp.wait_ge(u_lo, n + 1)
                    sp.wait_ge(opened, 1)
                    sp.dma_start(u_raw[:, r, :], dram["u"][bass.ds(n, 1)].rearrange("o p f -> p (o f)")
                                 ).then_inc(u_in[r], 16)

                def store(n, r):
                    sp.wait_ge(gelued, n + 3)
                    sp.wait_ge(opened, 1)
                    sp.dma_start(spilled[bass.ds(n, 1)].rearrange("o p f -> p (o f)"), gel[:, r % 2, :]
                                 ).then_inc(spill_out[r % 2], 16)

                def one_j(n, r, lap):
                    store(n, r)
                    if isinstance(n, int) and n + 4 >= KEYS:
                        return
                    load(n + 4, r)

                def store_chunk(tb, chunk, slot):
                    sp.wait_ge(quad_out, chunk * (CHUNK // QUAD) + (CHUNK // QUAD + 2))
                    sp.wait_ge(opened, 1)
                    sp.dma_start(gates.rearrange("g i c f -> c i g f")[bass.ds(chunk, 1)].rearrange(
                        "o i g f -> i (o g) f"),
                        grid[:, slot].rearrange("p (g j) t -> p g (j t)", j=JG)).then_inc(grid_out[slot], 16)

                for n in range(4):
                    load(n, n)
                for tb in range(TB):
                    n0 = tb * BLOCK_J
                    for n in range(n0, n0 + ROUTE_J):
                        one_j(n, n % 4, n // 4)
                    with sp.Fori(0, STEPS) as i:
                        for k in range(PAIR_J):
                            one_j(i * PAIR_J + (n0 + ROUTE_J + k), k % 4, None)
                            if k % (PAIR_J // 2) == PAIR_J // 2 - 1:
                                store_chunk(tb, i * 2 + (tb * P // CHUNK + k // (PAIR_J // 2)), k // (PAIR_J // 2))
                for n in range(TB * BLOCK_J, KEYS):
                    one_j(n, n % 4, None)
                    if n == KEYS - 6:
                        for b in range(2):
                            sp.wait_ge(grid_out[b], 16 * (T // CHUNK // 2) + 16)
                            sp.dma_start(shared.g_in[:, b].rearrange("p c j t -> p (c j t)"),
                                         gates.rearrange("g i c f -> g i (c f)")[b]).then_inc(shared.gate_in[b], 16)
                        for b in range(2):
                            sp.wait_ge(spill_out[b], 32)
                            sp.dma_start(shared.gel[:, b, :], spilled[b]).then_inc(shared.gel_in[b], 16)
                    if n >= KEYS - 4:
                        sp.wait_ge(u_lo, n + 5)
                        sp.dma_start(u_raw[:, n % 4, :], dram["v"][n + 4 - KEYS]).then_inc(shared.v_in[n % 4], 16)
                for b in range(2):
                    sp.wait_ge(spill_out[b], 16 * KEYS // 2 + 16)
                    sp.wait_ge(grid_out[b], 16 * (T // CHUNK // 2) + 16)

            @block.gpsimd
            def _(pool):
                for count, free in ((u_lo, 4), (a_done, 2), (gelued, 2), (quad_done, 2), (quad_out, 2)):
                    pool.sem_inc(count, free)
                for b in range(2):
                    pool.sem_inc(spill_out[b], 16)
                    pool.sem_inc(grid_out[b], 16)
                pool.sem_inc(opened, 1)

                def rest(n, r, lap):
                    pool.wait_ge(u_hi, n + 1)
                    nc.gpsimd.tensor_tensor(u[r % 2][1][:], u_raw[:, r, :], u[r % 2][0][:].bitcast(F32), ALU.subtract
                                            ).then_inc(u_lo, 1)
                each(pool, 0, KEYS, 4, rest)

            @block.tensor
            def _(pe):
                def one_j(n, r, lap):
                    b = r % 2
                    pe.wait_ge(u_lo, n + 5)
                    pe.wait_ge(gelued, n + 1)
                    for c in range(DC):
                        for k, (x, y) in enumerate(PASSES):
                            last = nc.tensor.matmul(ps_a[b][:], u[b][x][:, c * P:(c + 1) * P], act[y][:, c, :],
                                                    start=(c == 0 and k == 0), stop=(c == DC - 1 and k == 2))
                    last.then_inc(a_done, 1)

                def one_quad(tb, quad, q):
                    pe.wait_ge(rows_i, quad + (tb * QB + 1))
                    pe.wait_ge(rows_j, quad + (tb * QB + 1))
                    pe.wait_ge(quad_out, quad + (tb * QB + 1))
                    for t in range(QUAD):
                        for k in range(PARTS):
                            last = nc.tensor.matmul(ps_g[q % 2][:, t, :], row_i[:, q % 2, t, :],
                                                    row_j[:, q % 2, k, t, :], start=(k == 0), stop=(k == PARTS - 1))
                    last.then_inc(quad_done, 1)

                def scores(tb):
                    if tb >= 1:
                        pe.wait_ge(pick_out, tb)
                    for g in range(2 * H):
                        if tb == 0 and g % 4 == 0:
                            pe.wait_ge(keys_in[g // 4], 16)
                        last = nc.tensor.matmul(ps_r[g // 4][:, g % 4, :], query[:, g, tb * P:(tb + 1) * P],
                                                keys[:, g, :], start=True, stop=True)
                    last.then_inc(scored, 1)

                def turn_picks(tb):
                    pe.wait_ge(picked, tb + 1)
                    for k in range(3):
                        last = nc.tensor.transpose(ps_r[0][:, k, :], pick[:, k, :, :].rearrange("p h k -> p (h k)"),
                                                   consts["ident"][:])
                    last.then_inc(turned, 1)

                schedule(pe, one_j, one_quad, scores, nothing, turn_picks, nothing)

            @block.scalar
            def _(a):
                def round_u(n, r, lap):
                    a.wait_ge(u_in[r], lap * 16 + 16)
                    nc.scalar.activation(u[r % 2][0][:], u_raw[:, r, :], ACT.Copy).then_inc(u_hi, 1)

                def one_j(n, r, lap):
                    a.wait_ge(a_done, n + 3)
                    a.wait_ge(spill_out[r % 2], lap * 32 + (16 * (r // 2) + 16))
                    nc.scalar.activation(gel[:, r % 2, :], ps_a[r % 2][:], ACT.Gelu).then_inc(gelued, 1)
                    if isinstance(n, int) and n + 2 >= KEYS:
                        return
                    round_u(n + 2, (r + 2) % 4, lap + (r + 2) // 4)

                def one_quad(tb, quad, q):
                    slot, place = q // (CHUNK // QUAD), q % (CHUNK // QUAD)
                    if place == 0:
                        assert 2 * CHUNK // QUAD == 16
                        a.wait_ge(grid_out[slot], quad + (16 - q + tb * STEPS * 16))
                    a.wait_ge(quad_done, quad + (tb * QB + 3))
                    nc.scalar.activation(grid[:, slot, :, place * QUAD:(place + 1) * QUAD].rearrange("p j t -> p t j"),
                                         ps_g[q % 2][:], ACT.Copy).then_inc(quad_out, 1)

                def evacuate(tb):
                    a.wait_ge(scored, tb + 1)
                    if tb >= 1:
                        a.wait_ge(picked, tb)
                    for q in range(4):
                        last = nc.scalar.activation(score[:, 4 * q:4 * q + 4, :], ps_r[q][:], ACT.Copy)
                    last.then_inc(score_out, 1)

                def exps(tb):
                    a.wait_ge(shifted, tb + 1)
                    nc.scalar.activation(pick[:, 2, :, :], pick[:, 2, :, :], ACT.Exp).then_inc(exped, 1)

                def store_picks(tb):
                    a.wait_ge(turned, tb + 1)
                    if tb >= 1:
                        a.wait_ge(rows_i, tb * QB)
                        a.wait_ge(rows_j, tb * QB)
                    nc.scalar.activation(pickT[:], ps_r[0][:, 0:3, :], ACT.Copy).then_inc(pick_out, 1)

                for n in range(2):
                    round_u(n, n, 0)
                schedule(a, one_j, one_quad, evacuate, exps, store_picks, nothing)

            @block.vector
            def _(dve):
                count = [0]

                def done(ins):
                    count[0] += 1
                    ins.then_inc(inner, 1)

                def sync():
                    dve.wait_ge(inner, count[0])

                def top16(rows, values, indices):
                    for st in range(5):
                        for r, row in enumerate(rows):
                            lo, hi = values[r][:, 0:8], values[r][:, 8:16]
                            if st == 0:
                                done(nc.vector.max(lo, row))
                            elif st == 1:
                                done(nc.vector.max_index(indices[r][:, 0:8], lo, row))
                            elif st == 2:
                                done(nc.vector.match_replace(row, lo, row, -3e38))
                            elif st == 3:
                                done(nc.vector.max(hi, row))
                            else:
                                done(nc.vector.max_index(indices[r][:, 8:16], hi, row))
                        sync()

                def route(tb):
                    dve.wait_ge(score_out, tb + 1)
                    top16([score[:, g, :] for g in range(2 * H)], [top[:, g, :] for g in range(2 * H)],
                          [top_i[:, g, :] for g in range(2 * H)])
                    done(nc.vector.tensor_copy(top_f[:], top_i[:]))
                    pair = top[:].rearrange("p (h c) k -> p h c k", c=2)
                    done(nc.vector.tensor_tensor(cand[:], pair[:, :, 0, :].unsqueeze(3).to_broadcast([P, H, K, K]),
                                                 pair[:, :, 1, :].unsqueeze(2).to_broadcast([P, H, K, K]), ALU.add))
                    sync()
                    top16([cand[:, h, :, :].rearrange("p a b -> p (a b)") for h in range(H)],
                          [best[:, h, :] for h in range(H)], [pos[:, h, :] for h in range(H)])
                    done(nc.vector.tensor_scalar(half_i[:, 0], pos[:], 4, None, ALU.logical_shift_right))
                    done(nc.vector.tensor_scalar(half_i[:, 1], pos[:], 15, None, ALU.bitwise_and))
                    if tb >= 1:
                        dve.wait_ge(turned, tb)
                    nc.vector.tensor_tensor(pick[:, 2], best[:], best[:, :, 0:1].to_broadcast([P, H, K]),
                                            ALU.subtract).then_inc(shifted, 1)
                    sync()
                    done(nc.vector.tensor_copy(half_f[:], half_i[:]))
                    sync()
                    pair_i = top_f[:].rearrange("p (h c) k -> p h c k", c=2)
                    for c in range(2):
                        done(nc.vector.tensor_tensor(
                            hit[:], half_f[:, c].unsqueeze(3).to_broadcast([P, H, K, K]),
                            iota[:, 0:K].unsqueeze(1).unsqueeze(1).to_broadcast([P, H, K, K]), ALU.is_equal))
                        sync()
                        done(nc.vector.tensor_tensor(hit[:], hit[:],
                                                     pair_i[:, :, c, :].unsqueeze(2).to_broadcast([P, H, K, K]),
                                                     ALU.mult))
                        sync()
                        done(nc.vector.tensor_reduce(pick[:, c], hit[:], AX_X, ALU.add))
                        sync()
                    dve.wait_ge(exped, tb + 1)
                    done(nc.vector.tensor_reduce(gsum[:], pick[:, 2], AX_X, ALU.add))
                    sync()
                    done(nc.vector.reciprocal(gsum[:], gsum[:]))
                    sync()
                    nc.vector.tensor_tensor(pick[:, 2], pick[:, 2], gsum[:].unsqueeze(2).to_broadcast([P, H, K]),
                                            ALU.mult).then_inc(picked, 1)

                for tb in range(TB):
                    route(tb)
                    dve.wait_ge(pick_out, tb + 1)
                    for k in range(PARTS):
                        rest = pickT[:, 2, :] if k == 0 else left[:]
                        done(nc.vector.tensor_copy(part[k][:], rest))
                        sync()
                        if k < PARTS - 1:
                            done(nc.vector.tensor_tensor(left[:], rest, part[k][:], ALU.subtract))
                            sync()
                    with dve.Fori(0, QB // 2) as i:
                        for b in range(2):
                            dve.wait_ge(quad_done, i * 2 + (tb * QB + b + 1))
                            toks = bass.ds(i * (2 * QUAD) + b * QUAD, QUAD)
                            place = iota[:].unsqueeze(1).to_broadcast([P, QUAD, KEYS])
                            over = lambda ap: ap.unsqueeze(2).to_broadcast([P, QUAD, KEYS])
                            nc.vector.tensor_tensor(hot_j[:, b], place, over(pickT[:, 1, toks]), ALU.is_equal
                                                    ).then_inc(hot, 1)
                            nc.vector.tensor_tensor(row_i[:, b], place, over(pickT[:, 0, toks]), ALU.is_equal
                                                    ).then_inc(rows_i, 1)
                            dve.wait_ge(hot, i * 2 + (tb * QB + b + 1))
                            for k in range(PARTS):
                                y = nc.vector.tensor_tensor(row_j[:, b, k], hot_j[:, b], over(part[k][:, toks]),
                                                            ALU.mult)
                            y.then_inc(rows_j, 1)


def second_layer(nc, dram, spilled, gates, x2_dram, out, shared):
    U = 2 * JG
    with Scope(nc, "sl") as s:
        total = s.sb("total", [P, DC, T])
        v_raw, v, gel, g_in = shared.raw, shared.half, shared.gel, shared.g_in
        v_in, gel_in, gate_in = shared.v_in, shared.gel_in, shared.gate_in
        weighted = s.sb("weighted", [P, 2, T])
        w = [[s.sb(f"w{b}{h}", [P, T], F32R) for h in range(2)] for b in range(2)]
        ps = [s.ps(f"o{c}", [P, T]) for c in range(DC)]
        v_hi, v_lo, w_done, w_hi, w_lo, b_done, opened, added, stored, x2_in = (
            s.sem(x) for x in ("v_hi", "v_lo", "w_done", "w_hi", "w_lo", "b_done", "opened", "added", "stored",
                               "x2_in"))
        with nc.Block() as block:
            @block.sync
            def _(sp):
                def load(buffer, source, n, free, count, landed):
                    sp.wait_ge(free, count)
                    sp.wait_ge(opened, 1)
                    sp.dma_start(buffer, source[bass.ds(n, 1)].rearrange("o p f -> p (o f)")).then_inc(landed, 16)

                def one_j(n, k, lap):
                    group = n // JG if isinstance(n, int) else lap * (U // JG) + k // JG
                    if k % JG == 0 and not (isinstance(n, int) and group < 2):
                        load(g_in[:, k // JG].rearrange("p c j t -> p (c j t)"),
                             gates.rearrange("g i c f -> g i (c f)"), group, w_done, n + 1, gate_in[k // JG])
                    if not (isinstance(n, int) and n < 2):
                        load(gel[:, k % 4, :], spilled, n, w_done, n + (U - 4 + 1), gel_in[k % 4])
                    if not (isinstance(n, int) and n < 4):
                        load(v_raw[:, k % 4, :], dram["v"], n, v_lo, n + 1, v_in[k % 4])

                for n in range(U):
                    one_j(n, n, 0)
                each(sp, U, KEYS, U, one_j)
                for c in range(DC):
                    sp.dma_start(total[:, c, :], x2_dram[c]).then_inc(x2_in, 16)
                for c in range(DC):
                    sp.wait_ge(added, c + 1)
                    sp.dma_start(out[c], total[:, c, :]).then_inc(stored, 16)
                sp.wait_ge(stored, 16 * DC)

            @block.scalar
            def _(a):
                a.sem_inc(b_done, 2)

                def one_j(n, k, lap):
                    a.wait_ge(v_in[k % 4], lap * 32 + (16 * (k // 4) + 16))
                    a.wait_ge(b_done, n + 1)
                    nc.scalar.activation(v[k % 2][0][:], v_raw[:, k % 4, :], ACT.Copy).then_inc(v_hi, 1)
                    a.wait_ge(w_done, n + (U + 1))
                    nc.scalar.activation(w[k % 2][0][:], weighted[:, k % 2, :], ACT.Copy).then_inc(w_hi, 1)
                each(a, 0, KEYS, U, one_j)

            @block.vector
            def _(dve):
                dve.sem_inc(w_done, U)
                dve.sem_inc(v_lo, 4)
                dve.sem_inc(opened, 1)
                dve.sem_inc(w_lo, 2)

                def weigh(n, k, lap):
                    dve.wait_ge(gel_in[k % 4], lap * 32 + (16 * (k // 4) + 16))
                    dve.wait_ge(gate_in[k // JG], lap * 16 + 16)
                    dve.wait_ge(w_lo, n + 1)
                    nc.vector.tensor_tensor(
                        weighted[:, k % 2, :].rearrange("p (c t) -> p c t", t=CHUNK),
                        gel[:, k % 4, :].rearrange("p (c t) -> p c t", t=CHUNK), g_in[:, k // JG, :, k % JG, :],
                        ALU.mult).then_inc(w_done, 1)

                def one_j(n, k, lap):
                    dve.wait_ge(v_hi, n + 1)
                    nc.vector.tensor_tensor(v[k % 2][1][:], v_raw[:, k % 4, :], v[k % 2][0][:].bitcast(F32),
                                            ALU.subtract).then_inc(v_lo, 1)
                    dve.wait_ge(w_hi, n + 1)
                    nc.vector.tensor_tensor(w[k % 2][1][:], weighted[:, k % 2, :], w[k % 2][0][:].bitcast(F32),
                                            ALU.subtract).then_inc(w_lo, 1)

                def body(n, k, lap):
                    one_j(n, k, lap)
                    weigh(n + 2, (k + 2) % U, lap + (k + 2) // U)

                weigh(0, 0, 0)
                weigh(1, 1, 0)
                each(dve, 0, KEYS - 2, U, body)
                for n in range(KEYS - 2, KEYS):
                    one_j(n, n % U, n // U)
                dve.wait_ge(x2_in, 16 * DC)
                for c in range(DC):
                    dve.wait_ge(b_done, KEYS + 2)
                    nc.vector.tensor_tensor(total[:, c, :], total[:, c, :], ps[c][:], ALU.add).then_inc(added, 1)

            @block.tensor
            def _(pe):
                def one_j(n, k, lap):
                    pe.wait_ge(v_lo, n + 5)
                    pe.wait_ge(w_lo, n + 3)
                    for c in range(DC):
                        for p, (x, y) in enumerate(PASSES):
                            last = nc.tensor.matmul(ps[c][:], v[k % 2][x][:, c * P:(c + 1) * P], w[k % 2][y][:],
                                                    start=(isinstance(n, int) and n == 0 and p == 0),
                                                    stop=(isinstance(n, int) and n == KEYS - 1 and p == 2))
                    last.then_inc(b_done, 1)

                for n in range(U):
                    one_j(n, n, 0)
                each(pe, U, KEYS - U, U, one_j)
                for n in range(KEYS - U, KEYS):
                    one_j(n, n % U, n // U)


def program(nc, dram, out):
    USED_SEMAPHORES.clear()
    dram["skew"] = nc.dram_tensor("skew", [DA_HEADS, P * BIAS_LEN], F32).ap()
    gates = nc.dram_tensor("gates", [KEYS // JG, P, T // CHUNK, JG * CHUNK], F32).ap()
    spilled = nc.dram_tensor("spilled", [KEYS, P, T], F32).ap()
    x2_dram = nc.dram_tensor("x2", [DC, P, T], F32).ap()
    with Scope(nc, "all") as s:
        consts = {"ones": s.sb("ones", [P, P]), "eps": s.sb("eps", [P, 1]), "ident": s.sb("ident", [P, P]),
                  "iota": s.sb("iota", [P, KEYS]), "gains": s.sb("gains", [P, G_COLS])}
        neglam = s.sb("neglam", [P, 1])
        act = [s.sb(f"act{h}", [P, DC, T], F32R) for h in range(2)]
        wide = s.sb("wide", [P, 2 * PEER_HEADS, T])
        gain = lambda k: consts["gains"][:, k:k + 1]
        with Scope(nc, "mix") as m:
            more = m.sb("more", [P, IN_TILES - 16, T])
            tile = lambda n: wide[:, n, :] if n < 16 else more[:, n - 16, :]
            extra = m.sb("extra", [P, 12, T])
            ranges = weight_ranges(wide, more, extra)
            stream = Stream(m, nc, dram["w"], act, list(ranges.values()), 4)
            differential(nc, dram, consts, neglam, act, gain, wide, more, tile, extra, stream, ranges)
            latent(nc, dram, consts, act, gain, wide, more, tile, extra, stream, ranges)
            merge_and_query(nc, dram, consts, act, gain, wide, more, extra, x2_dram, stream, ranges)
        recycle_semaphores(nc)
        with Scope(nc, "ex") as e:
            shared = ExpertBuffers(e)
            first_layer(nc, wide, dram, consts, act, spilled, gates, shared)
            second_layer(nc, dram, spilled, gates, x2_dram, out, shared)


def weight_ranges(wide, more, extra):
    return {
        "lead": Range(16, 1, DC, 0, wide, 0),
        "rest": Range(KR + 1 - 16, 1, DC, 0, more, 0),
        "gate": Range(IN_TILES - GATES, 1, DC, 0, more, GATES - 16),
        "qr": Range(2, 2, Q_RANK // P, 0, extra, 8),
        "qn": Range(4, 2, Q_RANK // P, 0, extra, 0),
        "kn": Range(2, 4, KV_RANK // P, 3, wide, 8),
        "v": Range(2, TB, KV_RANK // P, 3, more, 0, by_token=True),
        "da": Range(DC, 1, DC, 0, wide, 0),
        "mla": Range(DC, 1, DC, 0, extra, 0),
        "out": Range(DC, 1, DC, 0, extra, 0),
        "query": Range(2 * PEER_HEADS, 1, DC, 0, wide, 0),
    }


def differential(nc, dram, consts, neglam, act, gain, wide, more, tile, extra, stream, ranges):
    with Scope(nc, "df") as s:
        lead, rest, gate = ranges["lead"], ranges["rest"], ranges["gate"]
        ps_s = [[s.ps(f"s{b}{m}", [P, T]) for m in range(2)] for b in range(2)]
        ps_t, ps_o = s.ps("t", [P, T]), s.ps("o", [P, T])
        gains_in, consts_in, filled = (s.sem(x) for x in ("gains_in", "consts_in", "filled"))
        x_in = [s.sem(f"x_in{c}") for c in range(DC // 2)]
        xT = more[:, CQ - 16:CQ - 16 + DC, :]
        row = more[:, GATES - 16 + 4:GATES - 16 + 9, :].rearrange("p a t -> p (a t)").rearrange(
            "p (h n) -> p h n", n=BIAS_LEN)
        bias, sq, tmp = extra[:, 0:4, :], extra[:, 4:8, :], extra[:, 8:12, :]
        x_roots = Roots(s, nc, "nx", [(xT[:, c, :], [(x_in[c // 2], 16)], [("d", 0, 1)])
                                      for c in range(DC)], 1, consts, ps_s[0][0], sq=sq, added=True)
        x_norm = Apply(s, nc, "ax", [(0, [(xT[:, c, :], gain(G_ATTN + c), c) for c in range(DC)])], x_roots,
                       consts, [ps_s[0][1]], split=act, tmp=tmp)
        lead.ready = x_norm.chunk
        tables = Tables(s, nc, dram, consts, bias, neglam, (gains_in, 16), row, [ps_s[1][0], ps_s[1][1], ps_t, ps_o])
        roots = Roots(s, nc, "nqk", [(tile(n), [stream.landed(lead, n)], [("da", n - QA, n - QA + 1)])
                                     for n in range(QA, VA)], VA - QA, consts, ps_s[0][0], sq=sq)
        keys = Apply(s, nc, "ak", [(n, [(tile(n), gain(G_DAK), tile(n))]) for n in range(KA, VA)], roots, consts,
                     [ps_s[0][1], ps_s[1][0]])
        lat_roots = Roots(s, nc, "nl", [(tile(n), [stream.landed(rest, n - 16)],
                                         [("cq", 0, 1) if n < CKV else ("ckv", 1, 2)])
                                        for n in range(CQ, KR)], 2, consts, ps_s[1][1], sq=sq)
        lat = Apply(s, nc, "al", [(0, [(tile(CQ + c), gain(G_QLAT + c), tile(CQ + c)) for c in range(CKV - CQ)]),
                                  (1, [(tile(CKV + c), gain(G_KVLAT + c), tile(CKV + c)) for c in range(KR - CKV)])],
                    lat_roots, consts, [ps_s[0][1], ps_s[1][0]])
        turn = Turn(s, nc, "tv", [(tile(VA + n), [stream.landed(rest, n)]) for n in range(CQ - VA)],
                    consts, [ps_t, ps_o])
        blocks = []
        for h in range(DA_HEADS):
            for qb in range(TB):
                blocks.append((qb, [[(tile(QA + 2 * h + k), tile(KA + 2 * h + k))] for k in range(2)],
                               [roots.inv[:, qb, 2 * h + k:2 * h + k + 1] for k in range(2)],
                               bias[:, h, :], [tile(VA + 2 * h + k) for k in range(2)],
                               wide[:, 2 * h:2 * h + 2, qb * P:(qb + 1) * P], [lat.done()]))
        attend = Attention(s, nc, blocks, consts, 2, 2, ps_s, ps_t, ps_o,
                           s.sb("logits", [P, 4, T]), tmp[:, 2:4, :], neglam[:, 0:1],
                           factors_ready=[roots.done(), tables.done()], values_ready=[turn.done()])
        t_lead, t_rest, t_gate = Tiles(stream, lead), Tiles(stream, rest), Tiles(stream, gate)

        def sync(sp):
            for c in range(0, DC // 2, 2):
                load_x(sp, c)
            sp.dma_start(consts["gains"][:], dram["gains"][:, :]).then_inc(gains_in, 16)
            for name in ("ident", "iota"):
                sp.dma_start(consts[name][:], dram[name][:, :]).then_inc(consts_in, 16)

        def load_x(eng, c):
            eng.dma_start(xT[:, 2 * c:2 * c + 2, :], dram["xT"][2 * c:2 * c + 2].rearrange("c p t -> p c t")
                          ).then_inc(x_in[c], 16)

        class Fill(Part):

            def gpsimd(self, pool, k):
                if k == 0:
                    nc.gpsimd.memset(consts["ones"][:], 1.0).then_inc(filled, 1)
                    nc.gpsimd.memset(consts["eps"][:], EPS).then_inc(filled, 1)
                    pool.wait_ge(filled, 2)

            def tensor(self, pe, k):
                pe.wait_ge(filled, 2)
                if k == 1:
                    pe.wait_ge(consts_in, 32)

            def scalar(self, a, k):
                if k == 0:
                    for c in range(1, DC // 2, 2):
                        load_x(a, c)
                a.wait_ge(filled, 2)

            def vector(self, dve, k):
                if k == 1:
                    dve.wait_ge(gains_in, 16)

        fill = Fill()
        order = [(fill, 0), (tables, "load")] + x_roots.select_step() + x_roots.sum_steps()
        order += Opening(stream).steps() + [(fill, 1)] + x_roots.root_step()
        order += roots.select_step() + lat_roots.select_step() + x_norm.steps()
        order += [(t_lead, (0, 2)), (tables, 0), (t_lead, (2, 4)), (tables, 1), (tables, 2), (t_lead, (4, 16))]
        order += weave(roots.sum_steps(), [(t_rest, k) for k in range(8)]) + roots.root_step()
        order += [(t_rest, 8)] + weave(keys.steps(), turn.steps(0, 6), [(t_rest, k) for k in range(9, rest.slots)])
        order += weave(lat_roots.sum_steps(), turn.steps(6), [(t_gate, 0)]) + lat_roots.root_step()
        parts = t_gate.part_steps()[4:]
        order += parts[:4] + lat.steps() + parts[4:7]
        order += weave(attend.steps(), parts[7:])
        phase(nc, order, stream, gate, sync)


def latent(nc, dram, consts, act, gain, wide, more, tile, extra, stream, ranges):
    with Scope(nc, "la") as s:
        perm, cos, sin, mask = (s.sb(n, [P, w]) for n, w in (("perm", P), ("cos", T), ("sin", T), ("mask", T)))
        consts = dict(consts, perm=perm, cos=cos, sin=sin, mask=mask)
        consts_in = s.sem("consts_in")
        ps_n, ps_b = s.ps("n", [P, T]), s.ps("b", [P, T])
        ps_s = [[s.ps(f"s{b}", [P, T])] for b in range(2)]
        ps_t, ps_o = s.ps("t", [P, T]), s.ps("o", [P, T])
        r_qr, r_qn, r_kn, r_v, r_da = (ranges[x] for x in ("qr", "qn", "kn", "v", "da"))
        sq, tmp = s.sb("sq", [P, 4, T]), s.sb("tmp", [P, 2, T])
        lat = Split(s, nc, "sl", [(tile(CQ + c), []) for c in range(KR - CQ)], act)
        r_qr.ready = lat.chunk
        r_kn.ready = lambda c: lat.chunk(3 + c)
        rot = Rotate(s, nc, [(extra[:, 8 + n, :], [stream.landed(r_qr, n)]) for n in range(4)] + [(tile(KR), [])],
                     consts, ps_o, tmp[:, 0, :])
        half = lambda h: slice(ROPE * (h % 2), ROPE * (h % 2) + ROPE)
        qn = lambda h: extra[:, h, :]
        qr = lambda h: extra[half(h), 8 + h // 2, :]
        kn = lambda h: wide[:, 8 + h, :]
        kr = lambda h: more[half(h), KR - 16, :]
        kr_out = lambda h: more[half(h), CQ - 16 + h // 2, :]
        g_of = lambda k, h: consts["gains"][half(h), k:k + 1]
        Q0, K0 = DA_HEADS, DA_HEADS + MLA_HEADS
        squares = [(tile(n), [], [("ya", n // 2, n // 2 + 1)]) for n in range(2 * DA_HEADS)]
        for p in range(MLA_HEADS // 2):
            g = Q0 + 2 * p
            squares += [(qn(2 * p), [stream.landed(r_qn, 2 * p)], [("mla", g, g + 1)]),
                        (extra[:, 8 + p, :], [rot.done(p)], [("mla_even", g, g + 1), ("mla_odd", g + 1, g + 2)]),
                        (qn(2 * p + 1), [stream.landed(r_qn, 2 * p + 1)], [("mla", g + 1, g + 2)])]
        squares += [(kn(h), [stream.landed(r_kn, h)], [("mla", K0 + h, K0 + h + 1)]) for h in range(MLA_HEADS)]
        squares += [(tile(KR), [rot.done(4)], [("mla_even", K0, K0 + MLA_HEADS)])]
        roots = Roots(s, nc, "r", squares, K0 + MLA_HEADS, consts, ps_n, room=tile(CKV + 1), sq=sq)
        keys = Apply(s, nc, "ak", [(K0 + h, [(kn(h), gain(G_MKN), kn(h)), (kr(h), g_of(G_MKR, h), kr_out(h))])
                                   for h in range(MLA_HEADS)], roots, consts, [ps_b])
        ya = Apply(s, nc, "ay", [(h, [(tile(2 * h + k), gain(G_DAOUT + k), 2 * h + k) for k in range(2)])
                                 for h in range(DA_HEADS)], roots, consts, [ps_n], split=act, tmp=tmp,
                   free=[stream.used(r_v)])
        r_da.ready = ya.chunk
        blocks = []
        for h in range(MLA_HEADS):
            for qb in range(TB):
                blocks.append((qb, [[(qn(h), kn(h)), (qr(h), kr_out(h))]], [roots.inv[:, qb, Q0 + h:Q0 + h + 1]],
                               mask[:], [more[:, h, :]], extra[:, h:h + 1, qb * P:(qb + 1) * P], [keys.done(h)]))
        attend = Attention(s, nc, blocks, consts, 1, 1, ps_s, ps_t, ps_o,
                           sq[:, 0:2, :], sq[:, 2:4, :], factors_ready=[roots.done()],
                           values_ready=[stream.landed(r_v, 2 * TB - 1)])

        def sync(sp):
            for name, t in (("perm", perm), ("cos", cos), ("sin", sin), ("mask", mask)):
                sp.dma_start(t[:], dram[name][:, :]).then_inc(consts_in, 16)

        class Ready(Part):

            def tensor(self, pe, k):
                if k == 0:
                    pe.wait_ge(consts_in, 64)

            def vector(self, dve, k):
                if k == 0:
                    dve.wait_ge(consts_in, 64)
                else:
                    dve.wait_ge(*lat.chunk(KR - CQ - 1))

        t = lambda r: Tiles(stream, r).out_steps()
        n_ya, n_q = 2 * DA_HEADS, 2 * DA_HEADS + 3 * MLA_HEADS // 2
        order = lat.steps() + [(Ready(), 1)] + roots.select_step() + t(r_qr) + [(Ready(), 0)]
        order += weave(t(r_qn), rot.steps(), roots.sum_steps(0, n_ya))
        order += weave(t(r_kn), roots.sum_steps(n_ya, n_q))
        order += weave(t(r_v)[:-3], roots.sum_steps(n_q)) + roots.root_step() + t(r_v)[-3:]
        da, steps = Tiles(stream, r_da).part_steps(), attend.steps()
        order += keys.steps(0, 2) + ya.steps(0, 1)
        for k, step in enumerate(steps):
            order.append(step)
            if k % 2 == 0:
                order += ya.steps(k // 2 + 1, k // 2 + 2) if k // 2 + 1 < DA_HEADS else []
            if k % TB == 1:
                order += keys.steps(k // TB + 2, k // TB + 3) if k // TB + 2 < MLA_HEADS else []
            if k >= 2 and da:
                order.append(da.pop(0))
        order += da
        phase(nc, order, stream, r_da, sync)


def merge_and_query(nc, dram, consts, act, gain, wide, more, extra, x2_dram, stream, ranges):
    with Scope(nc, "mq") as s:
        x2 = more[:, 0:DC, :]
        r_mla, r_out, r_q = ranges["mla"], ranges["out"], ranges["query"]
        yb = Split(s, nc, "syb", [(extra[:, c, :], []) for c in range(DC)], act)
        r_mla.ready = yb.chunk
        gates = more[:, GATES - 16:IN_TILES - 16, :]
        sig = Sigmoids(s, nc, gates)
        merge = Merge(s, nc, wide, extra, gates, sig.done, lambda c: stream.landed(r_mla, c))
        merged = Split(s, nc, "sm", [(wide[:, c, :], [merge.done(c)]) for c in range(DC)], act,
                       free=[stream.used(r_mla)])
        r_out.ready = merged.chunk
        add = Residual(s, nc, dram["xT"], x2, extra, lambda c: stream.landed(r_out, c), x2_dram)
        roots = Roots(s, nc, "nx2", [(x2[:, c, :], [add.done(c)], [("d", 0, 1)]) for c in range(DC)],
                      1, consts, s.ps("n", [P, T]), added=True)
        norm = Apply(s, nc, "ax2", [(0, [(x2[:, c, :], gain(G_FFN + c), c) for c in range(DC)])], roots, consts,
                     [s.ps("b", [P, T])], split=act, free=[stream.used(r_out)])
        r_q.ready = norm.chunk

        order = yb.steps() + roots.select_step()
        for c in range(DC):
            order += [(Tiles(stream, r_mla), c), (sig, c), (merge, c)]
        order += merged.steps()
        for c in range(DC):
            order += [(Tiles(stream, r_out), c), (add, c)] + roots.sum_steps(c, c + 1)
        order += roots.sum_steps(DC) + roots.root_step() + norm.steps()
        order += [(Tiles(stream, r_q), (0, r_q.slots)), (add, "stored")]
        phase(nc, order, stream, r_q, add.sync)


def shape_constants():
    import numpy as np
    c = {"ident": np.eye(P, dtype=np.float32)}
    c["iota"] = np.tile(np.arange(KEYS, dtype=np.float32), (P, 1))
    f = np.arange(P) % (ROPE // 2)
    inv = np.float32(10000.0) ** (-(2 * f).astype(np.float32) / np.float32(ROPE))
    ang = inv[:, None] * np.arange(T, dtype=np.float32)[None, :]
    first = (np.arange(P) % ROPE) < ROPE // 2
    c["cos"] = np.cos(ang).astype(np.float32)
    c["sin"] = (np.sin(ang) * np.where(first, -1.0, 1.0)[:, None]).astype(np.float32)
    perm = np.zeros((P, P), np.float32)
    for m in range(P):
        perm[m + ROPE // 2 if first[m] else m - ROPE // 2, m] = 1.0
    c["perm"] = perm
    q, n = np.arange(P)[:, None], np.arange(T)[None, :]
    c["mask"] = np.where(T - P + q - n >= 0, 0.0, NEG).astype(np.float32)
    dist = T - 1 - np.arange(BIAS_LEN)
    nf = np.maximum(dist, 16).astype(np.float32)
    large = 16 + (np.log(nf / 16) / np.log(8.0) * 16).astype(np.int32)
    bucket = np.where(dist < 16, np.maximum(dist, 0), np.minimum(large, 31))
    onehot = np.zeros((33, BIAS_LEN), np.float32)
    onehot[np.where(dist >= 0, bucket, 32), np.arange(BIAS_LEN)] = 1.0
    c["onehot"] = onehot
    return c


def kernel(**inputs):
    import numpy as np
    import concourse.bacc as bacc
    from concourse.bass_utils import run_bass_kernel_spmd

    a = {k: np.asarray(v) for k, v in inputs.items()}

    def tiles(w):
        k, n = w.shape
        return np.ascontiguousarray(w.reshape(k // P, P, n // P, P).transpose(2, 1, 0, 3)).reshape(n // P, P, k)

    def packed(w, outs):
        t = tiles(w)
        full = np.zeros((t.shape[0] // outs, P, D), np.float32)
        full[:, :, :outs * t.shape[2]] = t.reshape(-1, outs, P, t.shape[2]).transpose(0, 2, 1, 3).reshape(
            t.shape[0] // outs, P, -1)
        return full

    def by_token(w):
        k, n = w.shape
        return np.ascontiguousarray(w.reshape(k // P, P, n // T, T).transpose(2, 1, 0, 3)).reshape(n // T, P, D)

    def cols(v):
        return v.reshape(-1, P).T

    w_in = a["w_in"][0]
    kr0 = (CKV + 2) * P
    uq = a["mla_w_uq"][0].reshape(Q_RANK, MLA_HEADS, NOPE + ROPE)
    ukv = a["mla_w_ukv"][0].reshape(KV_RANK, MLA_HEADS, NOPE + MLA_V)
    qn, kn = a["mla_q_norm"][0], a["mla_k_norm"][0]
    data = {
        "xT": np.ascontiguousarray(a["x"][0].T).reshape(DC, P, T),
        "w": np.concatenate([
            tiles(np.concatenate([w_in[:, :kr0 + ROPE], w_in[:, kr0:kr0 + ROPE], w_in[:, kr0 + ROPE:]], axis=1)),
            packed(uq[:, :, NOPE:].reshape(Q_RANK, -1), 2), packed(uq[:, :, :NOPE].reshape(Q_RANK, -1), 2),
            packed(ukv[:, :, :NOPE].reshape(KV_RANK, -1), 4), by_token(ukv[:, :, NOPE:].reshape(KV_RANK, -1)), 
            tiles(a["da_proj"][0]), tiles(a["mla_proj"][0]), tiles(a["w_out"][0]), tiles(a["peer_w_query"][0])]),
        "rel_bias": a["rel_bias"],
        "keys": np.ascontiguousarray(a["peer_sub_keys"][0].reshape(2 * PEER_HEADS, KEYS, P).transpose(2, 0, 1)
                                     ).reshape(P, 2 * PEER_HEADS * KEYS),
        "u": np.ascontiguousarray(a["peer_u"][0].reshape(KEYS, KEYS, DC, P).transpose(1, 3, 2, 0)).reshape(KEYS, P, D),
        "v": np.ascontiguousarray(a["peer_v"][0].reshape(KEYS, KEYS, D).transpose(1, 0, 2)),
        "gains": np.ascontiguousarray(np.concatenate(
            [cols(a["attn_norm"][0]), cols(a["ffn_norm"][0]), cols(a["da_q_norm"][0]), cols(a["da_k_norm"][0]),
             cols(a["da_out_norm"][0]), cols(a["mla_q_latent_norm"][0]), cols(a["mla_kv_latent_norm"][0]),
             cols(qn[:NOPE]), cols(np.concatenate([qn[NOPE:], qn[NOPE:]])),
             cols(kn[:NOPE]), cols(np.concatenate([kn[NOPE:], kn[NOPE:]])),
             cols(a["da_lambda_q1"][0]), cols(a["da_lambda_k1"][0]), cols(a["da_lambda_q2"][0]),
             cols(a["da_lambda_k2"][0])], axis=1)),
    }
    data.update(shape_constants())
    nc = bacc.Bacc("TRN2", target_bir_lowering=False, num_devices=1)
    arrays, dram = {}, {}
    for name, x in data.items():
        arrays[f"in_{name}"] = x
        dram[name] = nc.dram_tensor(f"in_{name}", x.shape, F32, kind="ExternalInput").ap()
    out = nc.dram_tensor("out_T", (DC, P, T), F32, kind="ExternalOutput").ap()
    program(nc, dram, out)
    r = run_bass_kernel_spmd(nc, [arrays], core_ids=[0])
    return np.ascontiguousarray(r.results[0]["out_T"].reshape(D, T).T)[None]
```
